# Optimizing a Trainium2 kernel written in Bass

```python
import math
import jax, jax.numpy as jnp
from jax import lax
import numpy as np

D_MODEL = 1024
BATCH = 1
SEQ = 128
DEPTH = 1
DEC_BATCH = 1
DEC_SEQ = 512
PAST_LEN = 128

GRID_W = 64
ROPE_BASE = 10000.0
RET_HEADS = 4
RET_DK = 128
RET_DV = 256
RET_CHUNK = 128
DIFF_HEADS = 8
DIFF_DH = 64
Q_BLOCK = 128
FFN_HIDDEN = -(-8 * D_MODEL // (3 * 256)) * 256
RET_QK_W = RET_HEADS * RET_DK
RET_V_W = RET_HEADS * RET_DV
DIFF_QK_W = DIFF_HEADS * 2 * DIFF_DH
DIFF_V_W = DIFF_HEADS * 2 * DIFF_DH
W_IN_COLS = 2 * RET_QK_W + 2 * RET_V_W + 2 * DIFF_QK_W + DIFF_V_W + 2 * D_MODEL
RMS_EPS = 1e-6
GN_EPS = 1e-5

kernel_name = "hybrid_retention_diffattn_dit_step"

def rmsnorm(x, g):
    xf = x.astype(jnp.float32)
    y = xf * lax.rsqrt(jnp.mean(xf * xf, axis=-1, keepdims=True) + RMS_EPS)
    return (y * g).astype(x.dtype)

def head_group_norm(y, g):
    yf = y.astype(jnp.float32)
    mu = jnp.mean(yf, axis=-1, keepdims=True)
    var = jnp.mean(jnp.square(yf - mu), axis=-1, keepdims=True)
    return ((yf - mu) * lax.rsqrt(var + GN_EPS) * g).astype(y.dtype)

def modulation(cvec, w_ada, b_ada):
    return jax.nn.silu(cvec) @ w_ada + b_ada

def axial_rope_tables(L, d):
    rows = L // GRID_W
    pos_r = jnp.repeat(jnp.arange(rows), GRID_W).astype(jnp.float32)
    pos_c = jnp.tile(jnp.arange(GRID_W), rows).astype(jnp.float32)
    n = d // 4
    inv = ROPE_BASE ** (-jnp.arange(n, dtype=jnp.float32) / n)
    ang = jnp.concatenate([pos_r[:, None] * inv, pos_c[:, None] * inv], axis=-1)
    return jnp.cos(ang), jnp.sin(ang)

def apply_rope(x, cos, sin):
    shape = (x.shape[1],) + (1,) * (x.ndim - 3) + (cos.shape[-1],)
    c = cos.reshape(shape)
    s = sin.reshape(shape)
    x1, x2 = jnp.split(x, 2, axis=-1)
    return jnp.concatenate([x1 * c - x2 * s, x1 * s + x2 * c], axis=-1).astype(x.dtype)

def retention_scan(q, k, v, log_gamma, s0, inclusive):
    B, L, H, dk = q.shape
    dv = v.shape[-1]
    C = RET_CHUNK
    N = L // C
    qc = q.reshape(B, N, C, H, dk)
    kc = k.reshape(B, N, C, H, dk)
    vc = v.reshape(B, N, C, H, dv)
    idx = jnp.arange(C, dtype=jnp.float32)
    dist = idx[:, None] - idx[None, :]
    mask = (dist >= 0) if inclusive else (dist > 0)
    decay = jnp.where(mask[None], jnp.exp(log_gamma[:, None, None] * jnp.where(mask, dist, 0.0)[None]), 0.0)
    scores = jnp.einsum('bnihd,bnjhd->bnhij', qc, kc) * decay[None, None]
    intra = jnp.einsum('bnhij,bnjhe->bnihe', scores, vc)
    w_k = jnp.exp(log_gamma[:, None] * (C - 1.0 - idx)[None])
    kv = jnp.einsum('bnjhd,hj,bnjhe->bnhde', kc, w_k, vc).astype(jnp.float32)
    gamma_c = jnp.exp(log_gamma * C)[None, :, None, None]

    def step(s, kv_n):
        return gamma_c * s + kv_n, s

    s_final, s_prev = lax.scan(step, s0.astype(jnp.float32), jnp.moveaxis(kv, 1, 0))
    s_prev = jnp.moveaxis(s_prev, 0, 1)
    w_q = jnp.exp(log_gamma[:, None] * (idx + 1.0)[None])
    cross = jnp.einsum('bnihd,hi,bnhde->bnihe', qc, w_q, s_prev)
    out = (intra + cross).reshape(B, L, H, dv).astype(v.dtype)
    return out, s_final.astype(v.dtype)

def diff_attention(q, k, v, lam):
    B, Lq, H, _, dh = q.shape
    nb = Lq // Q_BLOCK
    qb = jnp.moveaxis(q.reshape(B, nb, Q_BLOCK, H, 2, dh), 1, 0)
    scale = dh ** -0.5

    def block(qblk):
        s = jnp.einsum('bqhmd,bkhmd->bhmqk', qblk, k, preferred_element_type=jnp.float32) * scale
        p = jax.nn.softmax(s, axis=-1)
        a = p[:, :, 0] - lam * p[:, :, 1]
        return jnp.einsum('bhqk,bkhe->bqhe', a.astype(v.dtype), v)

    out = lax.map(block, qb)
    return jnp.moveaxis(out, 0, 1).reshape(B, Lq, H, v.shape[-1])

def split_projection(proj):
    widths = (RET_QK_W, RET_QK_W, RET_V_W, RET_V_W, DIFF_QK_W, DIFF_QK_W, DIFF_V_W)
    points, acc = [], 0
    for w in widths:
        acc += w
        points.append(acc)
    return jnp.split(proj, points, axis=-1)

def trunk_layer(x, mod, norm1_g, norm2_g, w_in, b_gate, ret_decay_fwd, ret_decay_bwd, ret_gn_g,
                w_ret_out, lam, lam_init, diff_subln_g, w_diff_out, w_o, w_ffn_gate, w_ffn_up,
                w_ffn_down, ctx_cache):
    B, L, _ = x.shape
    latent = ctx_cache is not None
    shift1, scale1, gate1, shift2, scale2, gate2 = jnp.split(mod, 6, axis=-1)
    h = rmsnorm(x, norm1_g) * (1.0 + scale1) + shift1
    proj = h @ w_in
    q_r, k_r, v_r, g_r, q_d, k_d, v_d, gates = split_projection(proj)
    gates = jax.nn.sigmoid(gates + b_gate)
    gate_r, gate_d = jnp.split(gates, 2, axis=-1)

    q_r = q_r.reshape(B, L, RET_HEADS, RET_DK)
    k_r = k_r.reshape(B, L, RET_HEADS, RET_DK)
    v_r = v_r.reshape(B, L, RET_HEADS, RET_DV)
    q_d = q_d.reshape(B, L, DIFF_HEADS, 2, DIFF_DH)
    k_d = k_d.reshape(B, L, DIFF_HEADS, 2, DIFF_DH)
    v_d = v_d.reshape(B, L, DIFF_HEADS, 2 * DIFF_DH)

    if latent:
        cos_r, sin_r = axial_rope_tables(L, RET_DK)
        q_r = apply_rope(q_r, cos_r, sin_r)
        k_r = apply_rope(k_r, cos_r, sin_r)
        cos_d, sin_d = axial_rope_tables(L, DIFF_DH)
        q_d = apply_rope(q_d, cos_d, sin_d)
        k_d = apply_rope(k_d, cos_d, sin_d)
        s0_f, s0_b, k_ctx, v_ctx = ctx_cache
    else:
        s0_f = jnp.zeros((B, RET_HEADS, RET_DK, RET_DV), jnp.float32)
        s0_b = s0_f
    k_r = k_r * (RET_DK ** -0.5)

    lg_f = jax.nn.log_sigmoid(ret_decay_fwd.astype(jnp.float32))
    lg_b = jax.nn.log_sigmoid(ret_decay_bwd.astype(jnp.float32))
    out_f, s_f = retention_scan(q_r, k_r, v_r, lg_f, s0_f, True)
    out_b_rev, s_b = retention_scan(jnp.flip(q_r, 1), jnp.flip(k_r, 1), jnp.flip(v_r, 1), lg_b, s0_b, False)
    y_r = head_group_norm(out_f + jnp.flip(out_b_rev, 1), ret_gn_g.reshape(RET_HEADS, RET_DV))
    branch_r = (jax.nn.silu(g_r) * y_r.reshape(B, L, RET_V_W)) @ w_ret_out

    if latent:
        k_all = jnp.concatenate([k_d, k_ctx.astype(k_d.dtype)], axis=1)
        v_all = jnp.concatenate([v_d, v_ctx.astype(v_d.dtype)], axis=1)
    else:
        k_all, v_all = k_d, v_d
    o_d = diff_attention(q_d, k_all, v_all, lam)
    o_d = rmsnorm(o_d, diff_subln_g) * (1.0 - lam_init)
    branch_d = o_d.reshape(B, L, DIFF_V_W) @ w_diff_out

    mix = (gate_r * branch_r + gate_d * branch_d) @ w_o
    x = x + gate1 * mix
    h2 = rmsnorm(x, norm2_g) * (1.0 + scale2) + shift2
    ffn = (jax.nn.silu(h2 @ w_ffn_gate) * (h2 @ w_ffn_up)) @ w_ffn_down
    x = x + gate2 * ffn
    ctx_tensors = None if latent else (s_f, s_b, k_d, v_d)
    return x, ctx_tensors

def setup_inputs(seed: int = 0) -> dict:
    key = jax.random.key(seed)
    ks = jax.random.split(key, 32)
    f32 = jnp.float32
    D, F = D_MODEL, FFN_HIDDEN

    def nrm(k, shape, scale):
        return jax.random.normal(k, shape, f32) * scale

    base = 1.0 - 2.0 ** (-5.0 - jnp.arange(RET_HEADS, dtype=f32))
    decay_logit = jnp.log(base) - jnp.log1p(-base)
    return {
        "x_prompt": nrm(ks[0], (BATCH, SEQ, D), 1.0),
        "x_sample": nrm(ks[1], (DEC_BATCH, DEC_SEQ, D), 1.0),
        "state_ret_fwd": nrm(ks[2], (DEC_BATCH, DEPTH, RET_HEADS, RET_DK, RET_DV), 1.0),
        "state_ret_bwd": nrm(ks[3], (DEC_BATCH, DEPTH, RET_HEADS, RET_DK, RET_DV), 1.0),
        "cache_diff_k": nrm(ks[4], (DEC_BATCH, DEPTH, PAST_LEN, DIFF_HEADS, 2, DIFF_DH), 1.0),
        "cache_diff_v": nrm(ks[5], (DEC_BATCH, DEPTH, PAST_LEN, DIFF_HEADS, 2 * DIFF_DH), 1.0),
        "c": nrm(ks[6], (DEC_BATCH, D), 1.0),
        "c_ctx": nrm(ks[7], (D,), 1.0),
        "norm1_g": 1.0 + nrm(ks[8], (DEPTH, D), 0.02),
        "norm2_g": 1.0 + nrm(ks[9], (DEPTH, D), 0.02),
        "w_ada": nrm(ks[10], (DEPTH, D, 6 * D), 0.5 * D ** -0.5),
        "b_ada": nrm(ks[11], (DEPTH, 6 * D), 0.02),
        "w_in": nrm(ks[12], (DEPTH, D, W_IN_COLS), D ** -0.5),
        "b_gate": nrm(ks[13], (DEPTH, 2 * D), 0.1),
        "ret_decay_fwd": decay_logit[None] + nrm(ks[14], (DEPTH, RET_HEADS), 0.1),
        "ret_decay_bwd": decay_logit[None] + nrm(ks[15], (DEPTH, RET_HEADS), 0.1),
        "ret_gn_g": 1.0 + nrm(ks[16], (DEPTH, RET_V_W), 0.02),
        "w_ret_out": nrm(ks[17], (DEPTH, RET_V_W, D), RET_V_W ** -0.5),
        "diff_lambda_q1": nrm(ks[18], (DEPTH, DIFF_DH), 0.1),
        "diff_lambda_k1": nrm(ks[19], (DEPTH, DIFF_DH), 0.1),
        "diff_lambda_q2": nrm(ks[20], (DEPTH, DIFF_DH), 0.1),
        "diff_lambda_k2": nrm(ks[21], (DEPTH, DIFF_DH), 0.1),
        "diff_subln_g": 1.0 + nrm(ks[22], (DEPTH, 2 * DIFF_DH), 0.02),
        "w_diff_out": nrm(ks[23], (DEPTH, DIFF_V_W, D), DIFF_V_W ** -0.5),
        "w_o": nrm(ks[24], (DEPTH, D, D), D ** -0.5),
        "w_ffn_gate": nrm(ks[25], (DEPTH, D, F), D ** -0.5),
        "w_ffn_up": nrm(ks[26], (DEPTH, D, F), D ** -0.5),
        "w_ffn_down": nrm(ks[27], (DEPTH, F, D), F ** -0.5),
        "final_norm_g": 1.0 + nrm(ks[28], (D,), 0.02),
    }

def reference(x_prompt, x_sample, state_ret_fwd, state_ret_bwd, cache_diff_k, cache_diff_v, c,
              c_ctx, norm1_g, norm2_g, w_ada, b_ada, w_in, b_gate, ret_decay_fwd, ret_decay_bwd,
              ret_gn_g, w_ret_out, diff_lambda_q1, diff_lambda_k1, diff_lambda_q2, diff_lambda_k2,
              diff_subln_g, w_diff_out, w_o, w_ffn_gate, w_ffn_up, w_ffn_down, final_norm_g):
    xp, xs = x_prompt, x_sample
    new_f, new_b, new_k, new_v = [], [], [], []
    for l in range(DEPTH):
        lam_init = 0.8 - 0.6 * math.exp(-0.3 * l)
        lam = (jnp.exp(jnp.sum(diff_lambda_q1[l].astype(jnp.float32) * diff_lambda_k1[l].astype(jnp.float32)))
               - jnp.exp(jnp.sum(diff_lambda_q2[l].astype(jnp.float32) * diff_lambda_k2[l].astype(jnp.float32)))
               + lam_init)
        mod_ctx = modulation(c_ctx, w_ada[l], b_ada[l])[None, None, :]
        mod_lat = modulation(c, w_ada[l], b_ada[l])[:, None, :]
        weights = (norm1_g[l], norm2_g[l], w_in[l], b_gate[l], ret_decay_fwd[l], ret_decay_bwd[l],
                   ret_gn_g[l], w_ret_out[l], lam, lam_init, diff_subln_g[l], w_diff_out[l], w_o[l],
                   w_ffn_gate[l], w_ffn_up[l], w_ffn_down[l])
        xp, ctx_t = trunk_layer(xp, mod_ctx, *weights, None)
        xs, _ = trunk_layer(xs, mod_lat, *weights,
                            (state_ret_fwd[:, l], state_ret_bwd[:, l], cache_diff_k[:, l], cache_diff_v[:, l]))
        new_f.append(ctx_t[0])
        new_b.append(ctx_t[1])
        new_k.append(ctx_t[2])
        new_v.append(ctx_t[3])
    y_prompt = rmsnorm(xp, final_norm_g)
    y_sample = rmsnorm(xs, final_norm_g)
    new_ret_fwd = jnp.stack(new_f, axis=1)
    new_ret_bwd = jnp.stack(new_b, axis=1)
    new_diff_k = jnp.stack(new_k, axis=1)
    new_diff_v = jnp.stack(new_v, axis=1)
    return (y_prompt, y_sample, new_ret_fwd, new_ret_bwd, new_diff_k, new_diff_v)


_drawn_inputs = setup_inputs


def setup_inputs(seed=0):
    import zlib

    import numpy as np

    out = dict(_drawn_inputs(seed))
    spreads = {}
    factors = {'cache_diff_k': 3.228,
     'cache_diff_v': 2.959,
     'norm2_g': 8.0,
     'b_gate': 8.0,
     'ret_gn_g': 8.0,
     'diff_lambda_q1': 3.584,
     'diff_lambda_q2': 8.0,
     'diff_lambda_k2': 8.0,
     'diff_subln_g': 8.0,
     'final_norm_g': 2.738}
    for name, (base, spread) in spreads.items():
        noise = np.random.default_rng([zlib.crc32(name.encode()), seed]).standard_normal(out[name].shape)
        drawn = base * np.exp(spread * noise) if base else spread * noise
        out[name] = __import__('jax').numpy.asarray(drawn.astype(out[name].dtype))
    for name, factor in factors.items():
        out[name] = (out[name] * factor).astype(out[name].dtype)
    return out
```

```python
from contextlib import ExitStack

import numpy as np

import concourse.bass as bass
from concourse import mybir

F32 = mybir.dt.float32
F32R = mybir.dt.float32r
ACT = mybir.ActivationFunctionType
ALU = mybir.AluOpType
AX = mybir.AxisListType

P = 128
D = 1024
KT = D // P
LAT_TILES = 4
TILES = 5
LAT = LAT_TILES * P
TOK = TILES * P
HALF = TOK // 2
UC = 256
BANK = 512
RH = 4
RDV = 256
DH = 8
DHD = 64
FFN = 2816
GRID_W = 64
LAM_INIT = 0.2
RMS_EPS = 1e-6
GN_EPS = 1e-5
KB = 1024

ROW_BADA, ROW_G1, ROW_G2, ROW_BGATE, ROW_C, ROW_CCTX, ROW_GN, ROW_SUBLN = 0, 48, 56, 64, 80, 88, 96, 104
ROWS = 105

PHASES = [("qk_r", 4, "act", "act"), ("v_r", 4, "act", "act"), ("g_r", 4, "act", "act"),
          ("gate_r", 4, "act", "act"), ("gate_d", 4, "act", "act"), ("ret_out", 4, "dve", "dve"),
          ("q_d", 4, "act", "act"), ("k_d", 4, "act", "act"), ("v_d", 4, "act", "act"),
          ("diff_out", 4, "dve", "dve"), ("w_o", 4, "dve", "dve"),
          ("up0", 8, "act", "dve"), ("down0", 4, "dve", "dve"), ("up1", 8, "act", "dve"),
          ("down1", 4, "dve", "dve"), ("up2", 6, "act", "dve"), ("down2", 4, "dve", "dve")]


def lay_out_phases():
    first, count, reader, before, start = {}, {}, {}, {}, {}
    unit, total = 0, {"act": 2, "dve": 2}
    last = [("act", 2), ("dve", 2)]
    for name, n, *readers in PHASES:
        first[name], count[name], reader[name] = unit, n, readers
        before[name] = list(last)
        start[name] = dict(total)
        same = readers[0] == readers[1]
        for s in range(2):
            last[s] = (readers[s], total[readers[s]] + (2 * n - 2 + 2 * s if same else n))
        for e in set(readers):
            total[e] += 2 * n if same else n
        unit += n
    return first, count, reader, before, start


FIRST, COUNT, READER, BEFORE, START = lay_out_phases()
UNITS = sum(n for _, n, *_ in PHASES)
ADA_FIRST = {"gate_d": 0, "ret_out": 4}
SETUP_ACT, SETUP_DVE = 14, 8
SHIFT1, SCALE1, GATE1, SHIFT2, SCALE2, GATE2 = (KT * n for n in range(6))
PBUF = (0, 1, 2, 0, 1)
TBUF = (0, 1, 0, 1, 2)
OUT_ORDER = (4, 1, 2, 0, 3)


def freed_after(name, i, par, j):
    r = READER[name]
    if r[0] == r[1]:
        return i * 4 + (START[name][r[0]] + 2 * par + j + 1)
    return i * 2 + (START[name][r[par]] + j + 1)


def unit_of(name, i, par):
    return i * 2 + (FIRST[name] + par)


def ready(name, i, par, j):
    return i * 4 + (2 * FIRST[name] + 2 * par + j + 1)


def tile_of(h, t):
    return h + t // TILES, t % TILES, h * TILES + t


def build(nc, a, o):
    with ExitStack() as ctx:
        arena_bytes = 205 * KB + 512
        ctx.enter_context(nc.sbuf_tensor("arena", [P, arena_bytes // 4], F32))
        origin = nc.sbuf_base - arena_bytes

        def at(name, kb, shape, dt=F32):
            return nc.alloc_sbuf_tensor_at(name, shape, dt, offset=origin + int(kb * KB))

        def small(name, shape, dt=F32):
            return ctx.enter_context(nc.sbuf_tensor(name, shape, dt))

        def sem(name):
            return ctx.enter_context(nc.semaphore(name))

        H, W, A, B, Y, M, S = 0, 40, 88, 128, 148, 168, 188
        h_hi = at("h_hi", H, [P, KT, TOK], F32R)
        h_lo = at("h_lo", H + 20, [P, KT, TOK], F32R)
        o_nat = at("o_nat", H, [P, TILES, D])
        k_out = at("k_out", H + 16, [P, D])
        probs = at("probs", H + 20, [P, 3, 2, TOK])
        qz = at("qz", H + 35, [P, TILES, 2, P])
        diag = at("diag", H + 20, [P, 2, 4, P])
        ones = at("ones", H + 24, [P, P])
        mix_hi = at("mix_hi", H, [P, KT, TOK], F32R)
        mix_lo = at("mix_lo", H + 20, [P, KT, TOK], F32R)
        h2_hi = at("h2_hi", H, [P, KT, TOK], F32R)
        h2_lo = at("h2_lo", H + 20, [P, KT, TOK], F32R)
        w_raw = [at(f"w_raw{s}", W + 8 * s, [P, KT, UC]) for s in range(2)]
        w_hi = [at(f"w_hi{s}", W + 16 + 8 * s, [P, KT, UC], F32R) for s in range(2)]
        w_lo = [at(f"w_lo{s}", W + 32 + 8 * s, [P, KT, UC], F32R) for s in range(2)]
        x_nat = at("x_nat", A, [P, TILES, D])
        rows = at("rows", A + 20, [P, P])
        k_cache = at("k_cache", A + 21, [P, D])
        junk = at("junk", A + 25, [P, D])
        dist = at("dist", A + 29, [P, 2, P])
        row_pos = at("row_pos", A + 30, [P, 2, P])
        lam_in = at("lam_in", A + 31, [P, 4, DHD])
        lam_mul = at("lam_mul", A + 32, [P, 2, DHD])
        qk_r = at("qk_r", A, [P, 2 * RH, TOK])
        v_r = at("v_r", A + 20, [P, TILES, D])
        yg_hi = at("yg_hi", A, [P, KT, TOK], F32R)
        yg_lo = at("yg_lo", A + 20, [P, KT, TOK], F32R)
        qk_d = at("qk_d", A, [P, 2 * DH, TOK])
        od_hi = at("od_hi", A, [P, KT, TOK], F32R)
        od_lo = at("od_lo", A + 20, [P, KT, TOK], F32R)
        hid_hi = at("hid_hi", A, [P, KT, TOK], F32R)
        hid_lo = at("hid_lo", A + 20, [P, KT, TOK], F32R)
        rope = at("rope", B, [P, 2, LAT])
        swapped = at("swapped", B + 4, [P, 2, LAT])
        rope_tmp = at("rope_tmp", B + 8, [P, 2, LAT])
        g_r = at("g_r", B, [P, TILES, D])
        ada_b = [at(f"ada_b{s}", B + 8 * s, [P, KT, UC]) for s in range(2)]
        v_d = at("v_d", B, [P, TILES, D])
        gate_row = at("gate_row", B, [P, 4, D])
        fin_g = at("fin_g", B + 16, [P, D])
        ada_a = [at(f"ada_a{s}", (Y if s < 2 else M) + 8 * (s % 2), [P, KT, UC]) for s in range(4)]
        y_nat = at("y_nat", Y, [P, TILES, D])
        gate_d = at("gate_d", Y, [P, KT, TOK])
        x1 = at("x1", Y, [P, TILES, D])
        k_fb = at("k_fb", M, [P, 2, TILES, P])
        q_fb = at("q_fb", M + 5, [P, 2, LAT_TILES, P])
        state = at("state", M + 9, [P, 2, LAT_TILES, RDV])
        mixT = at("mixT", M, [P, KT, TOK])
        xn = at("xn", M, [P, TILES, D])
        silu_g = at("silu_g", M, [P, 2, TOK])
        hid_f = at("hid_f", M + 5, [P, 2, TOK])
        gated = at("gated", M + 10, [P, 4, UC])
        junk2 = at("junk2", M + 16, [P, D])
        kc_T = at("kc_T", S, [P, DH, P])
        decay = at("decay", S + 4, [P, RH, P])
        w_q = at("w_q", S + 6, [P, 2, RH, P])
        v_cache = at("v_cache", S + 4, [P, D])
        hf = at("hf", S + 10, [P, 2, TOK])
        k_head = at("k_head", S + 10, [P, TOK])
        s_dec = at("s_dec", S + 12.5, [P, TILES, P])
        kv_ctx = at("kv_ctx", S + 15, [P, 2 * RDV])
        bn6 = at("bn6", S + 17, [P, RH * TILES, 6])
        junk_o = at("junk_o", S + 8, [P, P])
        aT = at("aT", S + 10, [P, 3, TILES, P])
        ident = small("ident", [P, P])
        cols = small("cols", [P, ROWS])
        mod = small("mod", [P, 48, 2])
        silu_c = small("silu_c", [P, KT, 2])
        sc = small("sc", [P, KT, 2])
        stats = small("stats", [P, 40])
        rstd = small("rstd", [P, 40])
        pos_col = small("pos_col", [P, 2])
        w_k = small("w_k", [P, 2, RH])
        lg = small("lg", [P, 2, RH])
        gam_c = small("gam_c", [P, 2, RH])
        lamv = small("lamv", [P, 3])
        sm = small("sm", [P, TILES, 6])
        prime = small("prime", [P, 1])
        mean_var = stats[:, :].rearrange("p (n c) -> p n c", c=2)

        psum = ctx.enter_context(nc.psum_tensor("psum", [P, 8 * BANK], F32))

        def bank(b, n=BANK, at_=0):
            return psum[:, b * BANK + at_:b * BANK + at_ + n]

        def T_tile(b):
            return psum[:, b * BANK:(b + 2) * BANK].rearrange("p (b c) -> p b c", b=2)[:, :, 0:HALF]

        def in_halves(x):
            return x.rearrange("p (b c) -> p b c", b=2)

        def one_tile(x, n):
            return x[:, bass.ds(n, 1), :].rearrange("p a (b c) -> p (a b) c", b=2)

        w_landed = [sem(f"w_landed{s}") for s in range(2)]
        w_hi_done, w_lo_done = sem("w_hi_done"), sem("w_lo_done")
        mm_done = sem("mm_done")
        freed = {"act": sem("freed_act"), "dve": sem("freed_dve")}
        ld_ident, ld_rows, ld_x, ld_kc = sem("ld_ident"), sem("ld_rows"), sem("ld_x"), sem("ld_kc")
        ld_tab, ld_rope, ld_scal = sem("ld_tab"), sem("ld_rope"), sem("ld_scal")
        ada_a_in = [sem(f"ada_a_in{s}") for s in range(4)]
        ada_b_in = [sem(f"ada_b_in{s}") for s in range(2)]
        ada_a_used, ada_b_used = sem("ada_a_used"), sem("ada_b_used")
        rows_T, cols_ready, kc_ps, kc_done = sem("rows_T"), sem("cols_ready"), sem("kc_ps"), sem("kc_done")
        norm = {n: {q: sem(f"{n}_{q}") for q in ("sums", "mean", "root", "scaled")}
                for n in ("norm1", "normy", "normo", "norm2", "normf")}
        setup_a, setup_v = sem("setup_a"), sem("setup_v")
        dve_step = sem("dve_step")
        n2t = {n: {q: sem(f"{n}_{q}") for q in ("ps", "f", "hi", "lo")} for n in ("h", "yg", "od", "h2")}
        rope_in, rope_mul, rope_done = sem("rope_in"), sem("rope_mul"), sem("rope_done")
        g_done = sem("g_done")
        r_k, r_kT, r_kfb, r_s, r_dec = sem("r_k"), sem("r_kT"), sem("r_kfb"), sem("r_s"), sem("r_dec")
        r_q, r_s0, r_kv, r_upd, r_state = sem("r_q"), sem("r_s0"), sem("r_kv"), sem("r_upd"), sem("r_state")
        r_ctx, r_ctx_out, r_out, r_y = sem("r_ctx"), sem("r_ctx_out"), sem("r_out"), sem("r_y")
        r_bn, r_mv, y_norm, y_gated = sem("r_bn"), sem("r_mv"), sem("y_norm"), sem("y_gated")
        gr_done, gd_done, mix_r_done = sem("gr_done"), sem("gd_done"), sem("mix_r_done")
        ld_vc, vd_stored = sem("ld_vc"), sem("vd_stored")
        k_ps, k_stored = sem("k_ps"), sem("k_stored")
        at_z, at_qz, at_s, at_max, at_e = sem("at_z"), sem("at_qz"), sem("at_s"), sem("at_max"), sem("at_e")
        at_nm, at_r, at_a1, at_a, at_T = sem("at_nm"), sem("at_r"), sem("at_a1"), sem("at_a"), sem("at_T")
        at_aT, at_o, at_oe = sem("at_aT"), sem("at_o"), sem("at_oe")
        ones_set, gb_diag, gb_ps, gb_row = sem("ones_set"), sem("gb_diag"), sem("gb_ps"), sem("gb_row")
        mix_sum, mix_h, mix_l = sem("mix_sum"), sem("mix_h"), sem("mix_l")
        ld_x1, ld_fin, x1_done = sem("ld_x1"), sem("ld_fin"), sem("x1_done")
        silu_up, hid_h, hid_l = sem("silu_up"), sem("hid_h"), sem("hid_l")
        y_done, stored = sem("y_done"), sem("stored")

        def act_split(act, unit, s):
            act.wait_ge(w_landed[s], (unit - s) * 8 + 16)
            act.wait_ge(mm_done, unit * 2 - 2)
            act.activation(w_hi[s][:, :, :], w_raw[s][:, :, :], ACT.Copy).then_inc(w_hi_done, 1)

        def dve_split(dve, unit, s):
            dve.wait_ge(w_hi_done, unit + 1)
            dve.tensor_tensor(w_lo[s][:, :, :], w_raw[s][:, :, :], w_hi[s][:, :, :].bitcast(F32),
                              ALU.subtract).then_inc(w_lo_done, 1)

        def pe_wait_unit(pe, name, i, par):
            r, val = BEFORE[name][par]
            pe.wait_ge(freed[r], val)
            pe.wait_ge(freed[READER[name][par]], freed_after(name, i, par, 1) - (2 if READER[name][0] != READER[name][1] else 4))
            pe.wait_ge(w_lo_done, unit_of(name, i, par) + 1)

        def pe_T_unit(pe, name, i, par, hi, lo):
            for j in range(2):
                cs = slice(j * P, (j + 1) * P)
                for k in range(KT):
                    for n, (w, x) in enumerate(((w_lo[par], hi), (w_hi[par], lo), (w_hi[par], hi))):
                        for h in range(2):
                            last = pe.matmul(bank(4 * par + 2 * j + h, HALF), w[:, k, cs],
                                             x[:, k, h * HALF:(h + 1) * HALF],
                                             start=(k == 0 and n == 0), stop=(k == KT - 1 and n == 2))
                last.then_inc(mm_done, 1)

        def pe_N_unit(pe, name, i, par, hi, lo, kt=KT):
            for t in range(TILES):
                ts = slice(t * P, (t + 1) * P)
                for k in range(kt):
                    for n, (w, x) in enumerate(((w_lo[par], hi), (w_hi[par], lo), (w_hi[par], hi))):
                        last = pe.matmul(bank(4 * par + t // 2, UC, (t % 2) * UC), x[:, k, ts], w[:, k, :],
                                         start=(k == 0 and n == 0), stop=(k == kt - 1 and n == 2))
                if t >= LAT_TILES - 1:
                    last.then_inc(mm_done, 1)

        def pe_dense(pe, name, unit, hi, lo, **kw):
            with pe.Fori(0, COUNT[name] // 2) as i:
                for par in range(2):
                    pe_wait_unit(pe, name, i, par)
                    unit(pe, name, i, par, hi, lo, **kw)

        def pe_to_T(pe, which, src):
            q = n2t[which]
            for k in range(KT):
                if k >= 4:
                    pe.wait_ge(q["f"], k - 3)
                b = 2 * (k % 4)
                for t in range(TILES):
                    last = pe.transpose(bank(b + t // 4, P, (t % 4) * P), src[:, t, k * P:(k + 1) * P], ident[:, :])
                last.then_inc(q["ps"], 1)

        def dve_to_T(dve, which, hi, lo, pieces):
            q = n2t[which]

            def lo_part(k):
                dve.wait_ge(q["hi"], k + 1)
                dve.tensor_tensor(lo[:, k, :], hf[:, k % 2, :], hi[:, k, :].bitcast(F32),
                                  ALU.subtract).then_inc(q["lo"], 1)

            for k in range(KT):
                dve.wait_ge(q["ps"], k + 1)
                if k >= 2:
                    dve.wait_ge(q["lo"], k - 1)
                b = 2 * (k % 4) * BANK
                for cs, mul, second, op in pieces(k):
                    last = dve.tensor_scalar(hf[:, k % 2, cs], psum[:, b + cs.start:b + cs.stop],
                                             mul, second, ALU.mult, op)
                last.then_inc(q["f"], 1)
                if k >= 1:
                    lo_part(k - 1)
            lo_part(KT - 1)

        def act_to_T(act, which, hi):
            q = n2t[which]
            for k in range(KT):
                act.wait_ge(q["f"], k + 1)
                act.activation(hi[:, k, :], hf[:, k % 2, :], ACT.Copy).then_inc(q["hi"], 1)

        def modulated(shift):
            return lambda k: [(slice(0, LAT), sc[:, k, 0:1], mod[:, shift + k, 0:1], ALU.add),
                              (slice(LAT, TOK), sc[:, k, 1:2], mod[:, shift + k, 1:2], ALU.add)]

        block = ctx.enter_context(nc.Block())

        @block.sync
        def _(sp):
            w_in = a["w_in"][0].rearrange("(k p) c -> p k c", p=P)
            ada = a["w_ada"][0].rearrange("(k p) c -> p k c", p=P)
            sp.dma_start(x_nat[:, 0:LAT_TILES, :], a["x_sample"][0].rearrange("(t p) c -> p t c", p=P)).then_inc(ld_x, 16)
            sp.dma_start(x_nat[:, LAT_TILES, :], a["x_prompt"][0]).then_inc(ld_x, 16)
            for n in range(4):
                sp.dma_start(ada_a[n][:, :, :], ada[:, :, n * UC:(n + 1) * UC]).then_inc(ada_a_in[n], 16)
            sp.dma_start(w_raw[0][:, :, :], w_in[:, :, 0:UC]).then_inc(w_landed[0], 16)
            for n in range(4, 8):
                sp.wait_ge(ada_a_used, n - 3)
                sp.dma_start(ada_a[n % 4][:, :, :], ada[:, :, n * UC:(n + 1) * UC]).then_inc(ada_a_in[n % 4], 16)
            sp.dma_start(w_raw[1][:, :, :], w_in[:, :, UC:2 * UC]).then_inc(w_landed[1], 16)
            for s in range(2):
                sp.wait_ge(w_lo_done, s + 1)
                sp.dma_start(w_raw[s][:, :, :], w_in[:, :, (2 + s) * UC:(3 + s) * UC]).then_inc(w_landed[s], 16)

            def stream(name, sources, ada_col=None):
                with sp.Fori(0, COUNT[name] // 2) as i:
                    for s, (view, col, stride, kt) in enumerate(sources):
                        c = sp.snap(i * stride + col)
                        sp.wait_ge(w_lo_done, unit_of(name, i, s) - 1)
                        sp.dma_start(w_raw[s][:, 0:kt, :], view[:, 0:kt, bass.ds(c, UC)]).then_inc(w_landed[s], 16)
                        if ada_col is not None:
                            for r in range(2):
                                c = sp.snap(i * (4 * UC) + (ada_col + (2 * s + r) * UC))
                                sp.wait_ge(ada_b_used, i * 4 + 2 * (ADA_FIRST[name] + s))
                                sp.dma_start(ada_b[r][:, :, :], ada[:, :, bass.ds(c, UC)]).then_inc(ada_b_in[r], 16)

            def columns(view, col, kt=KT):
                return [(view, col, 2 * UC, kt), (view, col + UC, 2 * UC, kt)]

            by_tile = {n: a[n][0].rearrange("(k p) c -> p k c", p=P)
                       for n in ("w_ret_out", "w_diff_out", "w_o", "w_ffn_gate", "w_ffn_up", "w_ffn_down")}
            stream("v_r", columns(w_in, 1024))
            stream("g_r", columns(w_in, 2048))
            stream("gate_r", columns(w_in, 6144))
            sp.wait_ge(y_gated, RH)
            stream("gate_d", columns(w_in, 7168), ada_col=2 * D)
            stream("ret_out", columns(by_tile["w_ret_out"], 0), ada_col=4 * D)
            stream("q_d", columns(w_in, 3072))
            stream("k_d", columns(w_in, 4096))
            stream("v_d", columns(w_in, 5120))
            stream("diff_out", columns(by_tile["w_diff_out"], 0))
            stream("w_o", columns(by_tile["w_o"], 0))
            for third in range(3):
                c0, kt = third * D, min(KT, FFN // P - third * KT)
                stream(f"up{third}", [(by_tile["w_ffn_gate"], c0, UC, KT), (by_tile["w_ffn_up"], c0, UC, KT)])
                stream(f"down{third}", columns(by_tile["w_ffn_down"][:, third * KT:third * KT + kt, :], 0, kt))
            for t in range(TILES):
                sp.wait_ge(y_done, t + 1)
                dst = o["y_prompt"][0] if t == LAT_TILES else o["y_sample"][0, t * P:(t + 1) * P, :]
                sp.dma_start(dst, x1[:, t, :]).then_inc(stored, 16)
            sp.wait_ge(stored, TILES * 16)
            sp.wait_ge(vd_stored, 16)
            sp.wait_ge(k_stored, 16)
            sp.wait_ge(r_ctx_out, RH * 32)

        @block.gpsimd
        def _(pool):
            pool.dma_start(ident[:, :], a["const_ident"]).then_inc(ld_ident, 16)
            pool.dma_start(k_cache[:, :], a["cache_diff_k"][0, 0].rearrange("p h m d -> p (h m d)")).then_inc(ld_kc, 16)
            pool.dma_start(rope[:, :, :], a["const_rope_ret"].rearrange("a p t -> p a t")).then_inc(ld_rope, 16)
            for n, w in enumerate(("ret_decay_fwd", "ret_decay_bwd")):
                pool.dma_start(lg[:, n, :], a[w][0].partition_broadcast(P)).then_inc(ld_scal, 16)
            for n, w in enumerate(("q1", "q2", "k1", "k2")):
                pool.dma_start(lam_in[:, n, :], a["diff_lambda_" + w][0].partition_broadcast(P)).then_inc(ld_scal, 16)
            pool.dma_start(dist[:, :, :], a["const_dist"].rearrange("a p t -> p a t")).then_inc(ld_tab, 16)
            pool.dma_start(row_pos[:, :, :], a["const_row_pos"].partition_broadcast(P)).then_inc(ld_tab, 16)
            pool.dma_start(pos_col[:, :], a["const_pos_col"]).then_inc(ld_tab, 16)

            def swap_halves(name, qk, size, first, tile0, i, par):
                pool.wait_ge(freed["act"], freed_after(name, i, par, 1))
                pool.wait_ge(rope_done, i * 2 + (first + par))
                tile = i * 4 + (tile0 + 2 * par)
                for r in range(0, P, size):
                    f = r + size if (r // size) % 2 == 0 else r - size
                    pool.dma_start(swapped[r:r + size, :, :], qk[f:f + size, bass.ds(tile, 2), 0:LAT]).then_inc(rope_in, 16)

            with pool.Fori(0, 2) as i:
                for par in range(2):
                    swap_halves("qk_r", qk_r, P // 2, 0, 0, i, par)

            pool.wait_ge(rope_done, 4)
            pool.wait_ge(setup_a, SETUP_ACT)
            with pool.Fori(0, RH) as h:
                pool.wait_ge(r_out, h * TILES)
                for n, (src, c) in enumerate((("state_ret_fwd", 0), ("state_ret_bwd", LAT_TILES - 1))):
                    pool.dma_start(state[:, n, c, :],
                                   a[src][0, 0, bass.ds(h, 1)].rearrange("h k v -> k (h v)")).then_inc(r_s0, 16)
                q = qk_r[:, bass.ds(h, 1), 0:LAT].rearrange("p a (c i) -> p (a c) i", i=P)
                for n in range(2):
                    w = w_q[:, n, bass.ds(h, 1), :].to_broadcast([P, LAT_TILES, P])
                    pool.tensor_tensor(q_fb[:, n, :, :], q, w, ALU.mult).then_inc(r_q, 1)

            pool.wait_ge(r_out, RH * TILES)
            pool.dma_start(v_cache[:, :], a["cache_diff_v"][0, 0].rearrange("p h e -> p (h e)")).then_inc(ld_vc, 16)
            pool.wait_ge(ada_b_used, 16)
            pool.dma_start(rope[:, :, :], a["const_rope_diff"].rearrange("a p t -> p a t")).then_inc(ld_rope, 16)
            for name, first, tile0 in (("q_d", 4, 0), ("k_d", 8, DH)):
                with pool.Fori(0, 2) as i:
                    for par in range(2):
                        swap_halves(name, qk_d, P // 4, first, tile0, i, par)

            pool.wait_ge(freed["act"], START["diff_out"]["act"])
            pool.dma_start(o["new_diff_v"][0, 0].rearrange("p h e -> p (h e)"), v_d[:, LAT_TILES, :]).then_inc(vd_stored, 16)
            pool.memset(qz[:, :, :, :], 0.0).then_inc(at_z, 1)
            pool.wait_ge(at_z, 1)

            def fill_qz(t, src):
                for m in range(2):
                    r = slice(m * DHD, (m + 1) * DHD)
                    pool.tensor_copy(qz[r, t, m, :], src(r)).then_inc(at_qz, 1)

            for t in range(TILES):
                fill_qz(t, lambda r: qk_d[r, 0, t * P:(t + 1) * P])
            pool.wait_ge(at_oe, 2)
            pool.dma_start(o["new_diff_k"][0, 0].rearrange("p h m d -> p (h m d)"), k_out[:, :]).then_inc(k_stored, 16)
            with pool.Fori(1, DH) as h:
                for t in range(TILES):
                    pool.wait_ge(at_s, h * (2 * TILES) + (2 * t + 2 - 2 * TILES))
                    fill_qz(t, lambda r: qk_d[r, bass.ds(h, 1), t * P:(t + 1) * P])

            pool.wait_ge(mix_sum, KT)
            pool.dma_start(x1[:, 0:LAT_TILES, :], a["x_sample"][0].rearrange("(t p) c -> p t c", p=P)).then_inc(ld_x1, 16)
            pool.dma_start(x1[:, LAT_TILES, :], a["x_prompt"][0]).then_inc(ld_x1, 16)
            pool.dma_start(fin_g[:, :], a["final_norm_g"].partition_broadcast(P)).then_inc(ld_fin, 16)

        @block.tensor
        def _(pe):
            pe.wait_ge(ld_ident, 16)
            pe.wait_ge(ld_rows, 8 * 16)
            pe.transpose(bank(6, ROWS), rows[0:ROWS, :], ident[0:ROWS, 0:ROWS]).then_inc(rows_T, 1)
            pe.wait_ge(ld_kc, 16)
            for h in range(DH):
                last = pe.transpose(bank(4 + h // 4, P, (h % 4) * P), k_cache[:, h * P:(h + 1) * P], ident[:, :])
            last.then_inc(kc_ps, 1)

            pe.wait_ge(freed["act"], 2)
            for n in range(8):
                pe.wait_ge(ada_a_in[n % 4], 16 * (n // 4 + 1))
                for j in range(2):
                    for k in range(KT):
                        last = pe.matmul(bank(7, 2, 2 * (2 * n + j)), ada_a[n % 4][:, k, j * P:(j + 1) * P],
                                         silu_c[:, k, :], start=(k == 0), stop=(k == KT - 1))
                last.then_inc(ada_a_used, 1)

            pe.wait_ge(norm["norm1"]["scaled"], TILES)
            pe.wait_ge(kc_done, 1)
            pe.wait_ge(freed["dve"], 2)
            pe_to_T(pe, "h", x_nat)
            pe.wait_ge(n2t["h"]["lo"], KT)

            pe_dense(pe, "qk_r", pe_T_unit, h_hi, h_lo)
            pe_dense(pe, "v_r", pe_N_unit, h_hi, h_lo)
            pe_dense(pe, "g_r", pe_N_unit, h_hi, h_lo)

            for s in range(2):
                pe.wait_ge(freed["act"], START["gate_r"]["act"])
            with pe.Fori(0, RH) as h:
                def chunk(c):
                    return slice(c * P, (c + 1) * P)

                def v_chunk(c):
                    return v_r[:, c, bass.ds(h * RDV, RDV)]

                pe.wait_ge(r_k, h + 1)
                pe.wait_ge(r_kfb, h * 2)
                for c in range(TILES):
                    last = pe.transpose(bank(c // 4, P, (c % 4) * P), k_head[:, chunk(c)], ident[:, :])
                last.then_inc(r_kT, 1)
                pe.wait_ge(rope_done, 4)
                pe.wait_ge(r_dec, h)
                for c in range(TILES):
                    q = qk_r[:, bass.ds(h, 1), chunk(c)].rearrange("p a i -> p (a i)")
                    last = pe.matmul(bank(2 + c // 4, P, (c % 4) * P), k_head[:, chunk(c)], q, start=True, stop=True)
                last.then_inc(r_s, 1)
                pe.wait_ge(r_kfb, h * 2 + 2)
                for s in range(4):
                    f, b = (s, 3 - s) if s < 3 else (4, 4)
                    if s < 2:
                        pe.wait_ge(r_state, h * 3)
                        pe.wait_ge(r_ctx, h)
                    else:
                        pe.wait_ge(r_state, h * 3 + (s - 1))
                    pe.matmul(bank(4 + s % 2, RDV), k_fb[:, 0, f, :], v_chunk(f), start=True, stop=True)
                    pe.matmul(bank(4 + s % 2, RDV, RDV), k_fb[:, 1, b, :], v_chunk(b), start=True, stop=True).then_inc(r_kv, 1)
                pe.wait_ge(r_dec, h + 1)
                pe.wait_ge(r_q, h * 2 + 2)
                pe.wait_ge(r_s0, h * 32 + 32)
                for p_, c in enumerate(OUT_ORDER):
                    pe.wait_ge(r_y, h * TILES + max(0, p_ - 1))
                    out = bank(6 + p_ % 2, RDV)
                    if c < LAT_TILES:
                        pe.wait_ge(r_state, h * 3 + (2 if c in (1, 2) else 3))
                        pe.matmul(out, q_fb[:, 0, c, :], state[:, 0, c, :], start=True, stop=False)
                        pe.matmul(out, q_fb[:, 1, c, :], state[:, 1, c, :], start=False, stop=False)
                    pe.matmul(out, s_dec[:, c, :], v_chunk(c), start=(c == LAT_TILES), stop=True).then_inc(r_out, 1)
            pe.wait_ge(r_y, RH * TILES)
            pe.wait_ge(r_state, RH * 3)
            pe.wait_ge(r_ctx, RH)

            pe_dense(pe, "gate_r", pe_T_unit, h_hi, h_lo)
            pe.wait_ge(freed["act"], START["gate_d"]["act"])
            pe.wait_ge(y_gated, RH)
            pe_to_T(pe, "yg", y_nat)
            pe.wait_ge(n2t["yg"]["lo"], KT)

            def with_ada(pe, name, i, par, hi, lo):
                for r in range(2):
                    pe.wait_ge(ada_b_in[r], i * 32 + 16 * (ADA_FIRST[name] + par + 1))
                    for j in range(2):
                        for k in range(KT):
                            last = pe.matmul(bank(4 * par + 3, 2, HALF + 2 * (2 * r + j)),
                                             ada_b[r][:, k, j * P:(j + 1) * P], silu_c[:, k, :],
                                             start=(k == 0), stop=(k == KT - 1))
                    last.then_inc(ada_b_used, 1)
                pe_T_unit(pe, name, i, par, hi, lo)

            pe_dense(pe, "gate_d", with_ada, h_hi, h_lo)
            pe_dense(pe, "ret_out", with_ada, yg_hi, yg_lo)
            pe_dense(pe, "q_d", pe_T_unit, h_hi, h_lo)
            pe_dense(pe, "k_d", pe_T_unit, h_hi, h_lo)
            pe_dense(pe, "v_d", pe_N_unit, h_hi, h_lo)

            pe.wait_ge(freed["act"], START["diff_out"]["act"])
            pe.wait_ge(rope_done, 12)
            for h in range(DH):
                last = pe.transpose(bank(6 + h // 4, P, (h % 4) * P), qk_d[:, DH + h, LAT:TOK], ident[:, :])
            last.then_inc(k_ps, 1)
            pe.wait_ge(ld_vc, 16)
            pe.wait_ge(kc_done, 1)

            def scores(h0, t0, m, first=False):
                h, t, n = tile_of(h0, t0)
                pe.wait_ge(at_qz, n * 2 + (m + 1))
                if not first:
                    pe.wait_ge(at_e, n * 2 + (m - 1))
                if t < LAT_TILES:
                    k = qk_d[:, bass.ds(h + DH, 1), 0:LAT].rearrange("p a i -> p (a i)")
                    pe.matmul(bank(2 * m), qz[:, t, m, :], k, start=True, stop=True)
                    k = kc_T[:, bass.ds(h, 1), :].rearrange("p a i -> p (a i)")
                    last = pe.matmul(bank(2 * m + 1, P), qz[:, t, m, :], k, start=True, stop=True)
                else:
                    k = qk_d[:, bass.ds(h + DH, 1), LAT:TOK].rearrange("p a i -> p (a i)")
                    last = pe.matmul(bank(2 * m, P), qz[:, t, m, :], k, start=True, stop=True)
                last.then_inc(at_s, 1)

            def weights_T(h0, t0, first=False):
                h, t, n = tile_of(h0, t0)
                pe.wait_ge(at_a, n + 1)
                if not first:
                    pe.wait_ge(at_aT, n)
                for c in range(TILES if t < LAT_TILES else 1):
                    last = pe.transpose(bank(4 + c // 4, P, (c % 4) * P), probs[:, PBUF[t], 0, c * P:(c + 1) * P], ident[:, :])
                last.then_inc(at_T, 1)

            def outputs(h0, t0):
                h, t, n = tile_of(h0, t0)
                pe.wait_ge(at_aT, n + 1)
                pe.wait_ge(at_oe, n + (2 if t == 0 else 1))
                out = bank(6 + t % 2, P)
                for c in range(TILES if t < LAT_TILES else 1):
                    if t == LAT_TILES:
                        val = v_d[:, LAT_TILES, bass.ds(h * P, P)]
                    else:
                        val = v_d[:, c, bass.ds(h * P, P)] if c < LAT_TILES else v_cache[:, bass.ds(h * P, P)]
                    last = pe.matmul(out, aT[:, TBUF[t], c, :], val, start=(c == 0),
                                     stop=(c == LAT_TILES or t == LAT_TILES))
                last.then_inc(at_o, 1)

            scores(0, 0, 0, first=True)
            scores(0, 0, 1, first=True)
            scores(0, 1, 0)
            scores(0, 1, 1)
            scores(0, 2, 0)
            weights_T(0, 0, first=True)
            scores(0, 2, 1)
            with pe.Fori(0, DH - 1) as h:
                for t in range(2, TILES + 2):
                    scores(h, t + 1, 0)
                    weights_T(h, t - 1)
                    scores(h, t + 1, 1)
                    outputs(h, t - 2)
            for t in range(2, TILES + 2):
                if t + 1 < TILES:
                    scores(DH - 1, t + 1, 0)
                if t - 1 < TILES:
                    weights_T(DH - 1, t - 1)
                if t + 1 < TILES:
                    scores(DH - 1, t + 1, 1)
                outputs(DH - 1, t - 2)

            pe.wait_ge(at_oe, 2 + DH * TILES)
            pe.wait_ge(ones_set, 1)
            for n in range(8):
                pe.wait_ge(gb_diag, n + 1)
                pe.matmul(bank(n), ones[:, :], diag[:, n % 2, :, :].rearrange("p a b -> p (a b)"),
                          start=True, stop=True).then_inc(gb_ps, 1)
            pe.wait_ge(norm["normo"]["scaled"], TILES)
            pe.wait_ge(gb_row, 8)
            pe_to_T(pe, "od", o_nat)
            pe.wait_ge(n2t["od"]["lo"], KT)
            pe_dense(pe, "diff_out", pe_T_unit, od_hi, od_lo)
            pe.wait_ge(mix_l, KT)
            pe_dense(pe, "w_o", pe_N_unit, mix_hi, mix_lo)
            pe.wait_ge(freed["dve"], START["up0"]["dve"])
            pe.wait_ge(norm["norm2"]["scaled"], TILES)
            pe_to_T(pe, "h2", xn)
            pe.wait_ge(n2t["h2"]["lo"], KT)
            tiles = 0
            for third in range(3):
                pe_dense(pe, f"up{third}", pe_T_unit, h2_hi, h2_lo)
                kt = COUNT[f"up{third}"]
                tiles += kt
                pe.wait_ge(hid_l, tiles)
                pe_dense(pe, f"down{third}", pe_N_unit, hid_hi, hid_lo, kt=kt)

        @block.scalar
        def _(act):
            packed = ((ROW_BADA, a["b_ada"][0]), (ROW_G1, a["norm1_g"][0]), (ROW_G2, a["norm2_g"][0]),
                      (ROW_BGATE, a["b_gate"][0]), (ROW_C, a["c"][0]), (ROW_CCTX, a["c_ctx"]),
                      (ROW_GN, a["ret_gn_g"][0]), (ROW_SUBLN, a["diff_subln_g"][0]))
            for row, vec in packed:
                n = vec.shape[0] // P
                act.dma_start(rows[row:row + n, :], vec.rearrange("(r c) -> r c", c=P)).then_inc(ld_rows, 16)
            act.wait_ge(rows_T, 1)
            act.activation(cols[:, :], bank(6, ROWS), ACT.Copy).then_inc(cols_ready, 1)
            for n, row in enumerate((ROW_C, ROW_CCTX)):
                act.activation(silu_c[:, :, n], bank(6, KT, row), ACT.Silu).then_inc(freed["act"], 1)
            act.wait_ge(kc_ps, 1)
            act.activation(kc_T[:, :, :].rearrange("p a b -> p (a b)"), psum[:, 4 * BANK:6 * BANK], ACT.Copy).then_inc(kc_done, 1)

            def sums(which, src, waste):
                for t in range(TILES):
                    if t:
                        act.wait_ge(norm[which]["sums"], t)
                    act.activation(waste[:, :], src[:, t, :], ACT.Square, accum_out=stats[:, t:t + 1]).then_inc(norm[which]["sums"], 1)

            def root(which, n):
                act.wait_ge(norm[which]["mean"], 1)
                act.activation(rstd[:, 0:n], rstd[:, 0:n], ACT.Sqrt).then_inc(norm[which]["root"], 1)

            act.wait_ge(ld_x, 32)
            sums("norm1", x_nat, junk)
            root("norm1", TILES)

            act.wait_ge(setup_v, 1)
            act.activation(w_k[:, :, :], gam_c[:, :, :], ACT.Exp, scale=-1.0).then_inc(setup_a, 1)
            act.wait_ge(setup_v, 2)
            act.activation(stats[:, 8:16], gam_c[:, :, :].rearrange("p a b -> p (a b)"), ACT.Ln).then_inc(setup_a, 1)
            act.wait_ge(setup_v, 4)
            act.activation(lamv[:, 0:2], lamv[:, 0:2], ACT.Exp).then_inc(setup_a, 1)
            act.activation(gam_c[:, :, :], lg[:, :, :], ACT.Exp, scale=float(P)).then_inc(setup_a, 1)
            act.wait_ge(setup_v, 6)
            act.activation(w_k[:, :, :], w_k[:, :, :], ACT.Exp).then_inc(setup_a, 1)
            act.activation(decay[:, :, :], decay[:, :, :], ACT.Exp).then_inc(setup_a, 1)
            for n in range(2):
                for h in range(RH):
                    act.activation(w_q[:, n, h, :], row_pos[:, n, :], ACT.Exp, scale=lg[:, n, h:h + 1]).then_inc(setup_a, 1)
            act.wait_ge(w_landed[0], 16)
            act.activation(w_hi[0][:, :, :], w_raw[0][:, :, :], ACT.Copy).then_inc(w_hi_done, 1)
            act_to_T(act, "h", h_hi)

            def dense(name, evacuate, peel=0):
                def pair(i, last):
                    for par in range(2):
                        if not (last and par == 1):
                            act_split(act, unit_of(name, i, par) + 1, 1 - par)
                        evacuate(i, par)

                with act.Fori(0, COUNT[name] // 2 - peel) as i:
                    pair(i, False)
                if peel:
                    pair(COUNT[name] // 2 - 1, True)

            def set_table(func):
                act.activation(prime[:, :], ident[:, 0:1], func)

            def copy_T(name, dst, tile0, scale):
                def evacuate(i, par):
                    for j in range(2):
                        act.wait_ge(mm_done, ready(name, i, par, j))
                        act.activation(one_tile(dst, i * 4 + (tile0 + 2 * par + j)), T_tile(4 * par + 2 * j), ACT.Copy,
                                       scale=scale).then_inc(freed["act"], 1)
                return evacuate

            def copy_N(name, dst, func):
                def evacuate(i, par):
                    cs = i * (2 * UC) + par * UC
                    act.wait_ge(mm_done, ready(name, i, par, 0))
                    act.activation(dst[:, 0:LAT_TILES, bass.ds(cs, UC)],
                                   psum[:, 4 * par * BANK:(4 * par + 2) * BANK].rearrange("p (t c) -> p t c", c=UC),
                                   func).then_inc(freed["act"], 1)
                    act.wait_ge(mm_done, ready(name, i, par, 1))
                    act.activation(dst[:, LAT_TILES, bass.ds(cs, UC)], bank(4 * par + 2, UC), func).then_inc(freed["act"], 1)
                return evacuate

            dense("qk_r", copy_T("qk_r", qk_r, 0, 1.0))
            dense("v_r", copy_N("v_r", v_r, ACT.Copy))
            act.wait_ge(rope_done, 4)
            set_table(ACT.Silu)
            dense("g_r", copy_N("g_r", g_r, ACT.Silu))

            with act.Fori(0, RH) as h:
                act.wait_ge(rope_done, 4)
                act.wait_ge(r_s, h)
                act.activation(k_head[:, :], qk_r[:, bass.ds(h + RH, 1), :].rearrange("p a i -> p (a i)"), ACT.Copy).then_inc(r_k, 1)
                act.wait_ge(r_kT, h + 1)
                act.wait_ge(r_kv, h * 4)
                act.wait_ge(setup_v, SETUP_DVE)
                for n in range(2):
                    act.activation(k_fb[:, n, :, :].rearrange("p a b -> p (a b)"), psum[:, 0:TOK], ACT.Copy,
                                   scale=w_k[:, n, bass.ds(h, 1)]).then_inc(r_kfb, 1)
                act.wait_ge(r_kv, h * 4 + 4)
                act.wait_ge(r_ctx_out, h * 32)
                act.activation(kv_ctx[:, :], bank(5), ACT.Copy).then_inc(r_ctx, 1)
                act.wait_ge(r_ctx, h + 1)
                for n, dst in enumerate(("new_ret_fwd", "new_ret_bwd")):
                    act.dma_start(o[dst][0, 0, bass.ds(h, 1)].rearrange("h k v -> k (h v)"),
                                  kv_ctx[:, n * RDV:(n + 1) * RDV]).then_inc(r_ctx_out, 16)
                for p_, c in enumerate(OUT_ORDER):
                    act.wait_ge(r_out, h * TILES + (p_ + 1))
                    act.activation(y_nat[:, c, bass.ds(h * RDV, RDV)], bank(6 + p_ % 2, RDV), ACT.Copy).then_inc(r_y, 1)
            root("normy", RH * TILES)
            act.wait_ge(norm["normy"]["scaled"], 1)
            for h in range(RH):
                for t in range(TILES):
                    n, y = h * TILES + t, y_nat[:, t, h * RDV:(h + 1) * RDV]
                    act.activation(y, y, ACT.Identity, scale=rstd[:, n:n + 1], bias=rstd[:, 20 + n:21 + n]).then_inc(y_norm, 1)

            def gate(name, dst, col0, done, ada):
                def evacuate(i, par):
                    for j in range(2):
                        act.wait_ge(mm_done, ready(name, i, par, j))
                        if ada and j == 1:
                            act.activation(mod[:, bass.ds(i * 8 + (GATE1 + 4 * (ADA_FIRST[name] + par)), 4), :],
                                           bank(4 * par + 3, 8, HALF).rearrange("p (m s) -> p m s", s=2), ACT.Copy)
                        tile = i * 4 + (2 * par + j)
                        act.activation(one_tile(dst, tile), T_tile(4 * par + 2 * j), ACT.Sigmoid,
                                       bias=cols[:, bass.ds(tile + (ROW_BGATE + col0), 1)]).then_inc(freed["act"], 1)
                return evacuate

            set_table(ACT.Sigmoid)
            dense("gate_r", gate("gate_r", mixT, 0, None, False))
            act_to_T(act, "yg", yg_hi)
            dense("gate_d", gate("gate_d", gate_d, KT, None, True))
            dense("ret_out", lambda i, par: None)
            dense("q_d", copy_T("q_d", qk_d, 0, DHD ** -0.5))
            dense("k_d", copy_T("k_d", qk_d, DH, 1.0))
            act.wait_ge(rope_done, 12)

            dense("v_d", copy_N("v_d", v_d, ACT.Copy))
            act.wait_ge(r_ctx_out, RH * 32)
            act.wait_ge(k_ps, 1)
            act.activation(k_out[:, :], psum[:, 6 * BANK:8 * BANK], ACT.Copy).then_inc(at_oe, 2)

            def exp(h0, t0, m):
                h, t, n = tile_of(h0, t0)
                size = TOK if t < LAT_TILES else P
                if m == 0 and not (isinstance(h0, int) and h0 == 0 and t0 < 3):
                    pe_read = n - (1 if t < 2 else 2)
                    act.wait_ge(at_T, pe_read)
                act.wait_ge(at_max, n * 2 + (m + 1))
                act.activation(probs[:, PBUF[t], m, 0:size], psum[:, 2 * m * BANK:2 * m * BANK + size], ACT.Exp,
                               bias=sm[:, t, m:m + 1], accum_out=sm[:, t, 2 + m:3 + m]).then_inc(at_e, 1)

            def evacuate_T(h0, t0):
                h, t, n = tile_of(h0, t0)
                size = TOK if t < LAT_TILES else P
                act.wait_ge(at_T, n + 1)
                act.activation(aT[:, TBUF[t], :, :].rearrange("p a b -> p (a b)")[:, 0:size],
                               psum[:, 4 * BANK:4 * BANK + size], ACT.Copy).then_inc(at_aT, 1)

            def evacuate_o(h0, t0):
                h, t, n = tile_of(h0, t0)
                act.wait_ge(at_o, n + 1)
                if t == LAT_TILES:
                    act.wait_ge(k_stored, 16)
                act.wait_ge(at_oe, n + 2)
                act.activation(junk_o[:, :], bank(6 + t % 2, P), ACT.Square, accum_out=stats[:, bass.ds(n, 1)])
                act.activation(o_nat[:, t, bass.ds(h * P, P)], bank(6 + t % 2, P), ACT.Copy).then_inc(at_oe, 1)

            set_table(ACT.Exp)
            exp(0, 0, 0)
            exp(0, 0, 1)
            exp(0, 1, 0)
            exp(0, 1, 1)
            exp(0, 2, 0)
            evacuate_T(0, 0)
            exp(0, 2, 1)
            with act.Fori(0, DH - 1) as h:
                for t in range(2, TILES + 2):
                    exp(h, t + 1, 0)
                    evacuate_T(h, t - 1)
                    exp(h, t + 1, 1)
                    evacuate_o(h, t - 2)
            for t in range(2, TILES + 2):
                if t + 1 < TILES:
                    exp(DH - 1, t + 1, 0)
                if t - 1 < TILES:
                    evacuate_T(DH - 1, t - 1)
                if t + 1 < TILES:
                    exp(DH - 1, t + 1, 1)
                evacuate_o(DH - 1, t - 2)
            root("normo", DH * TILES)
            act.wait_ge(vd_stored, 16)
            for n in range(8):
                act.wait_ge(gb_ps, n + 1)
                act.activation(gate_row[:, n // 2, (n % 2) * BANK:(n % 2 + 1) * BANK], bank(n), ACT.Copy).then_inc(gb_row, 1)
            act_to_T(act, "od", od_hi)

            def mix_hi_part(i, par):
                for j in range(2):
                    act.wait_ge(mix_sum, i * 4 + (2 * par + j + 1))
                    tile = i * 4 + (2 * par + j)
                    act.activation(one_tile(mix_hi, tile), one_tile(mixT, tile), ACT.Copy).then_inc(mix_h, 1)

            dense("diff_out", mix_hi_part)
            dense("w_o", lambda i, par: None)
            act.wait_ge(x1_done, 8)
            sums("norm2", x1, xn[:, 0, :])
            root("norm2", TILES)
            act_to_T(act, "h2", h2_hi)

            def up(third):
                name = f"up{third}"
                base = sum(COUNT[f"up{n}"] for n in range(third))

                def evacuate(i, par):
                    for j in range(2):
                        if par == 0:
                            act.wait_ge(freed["dve"], i * 2 + START[name]["dve"])
                            act.wait_ge(mm_done, ready(name, i, 0, j))
                            act.activation(in_halves(silu_g[:, j, :]), T_tile(2 * j), ACT.Silu).then_inc(freed["act"], 1)
                        else:
                            act.wait_ge(freed["dve"], freed_after(name, i, 1, j))
                            tile = i * 2 + j
                            act.activation(hid_hi[:, bass.ds(tile, 1), :].rearrange("p a b -> p (a b)"),
                                           hid_f[:, j, :], ACT.Copy).then_inc(hid_h, 1)
                return evacuate

            set_table(ACT.Silu)
            for third in range(3):
                dense(f"up{third}", up(third))
                dense(f"down{third}", lambda i, par: None, peel=int(third == 2))
            act.wait_ge(x1_done, 32)
            sums("normf", x1, junk2)
            root("normf", TILES)

        @block.vector
        def _(dve):
            steps = [0]

            def link(ins):
                steps[0] += 1
                ins.then_inc(dve_step, 1)
                dve.wait_ge(dve_step, steps[0])

            flat = lambda x: x[:, :, :].rearrange("p a b -> p (a b)")

            def mean(which, n, scale, eps):
                dve.tensor_scalar(rstd[:, 0:n], stats[:, 0:n], scale, eps, ALU.mult, ALU.add).then_inc(norm[which]["mean"], 1)

            def inverse(which, n):
                dve.wait_ge(norm[which]["root"], 1)
                link(dve.reciprocal(rstd[:, 0:n], rstd[:, 0:n]))

            dve.wait_ge(ld_scal, 6 * 16)
            link(dve.tensor_scalar(gam_c[:, :, :], lg[:, :, :], -1.0, None, ALU.mult))
            dve.tensor_tensor(gam_c[:, :, :], lg[:, :, :], gam_c[:, :, :], ALU.max).then_inc(setup_v, 1)
            link(dve.tensor_tensor(lam_mul[:, :, :], lam_in[:, 0:2, :], lam_in[:, 2:4, :], ALU.mult))
            link(dve.reduce_sum(lamv[:, 0:2], lam_mul[:, :, :], axis=AX.X))
            dve.wait_ge(norm["norm1"]["sums"], TILES)
            mean("norm1", TILES, 1.0 / D, RMS_EPS)
            inverse("norm1", TILES)
            for t in range(TILES):
                dve.tensor_scalar(x_nat[:, t, :], x_nat[:, t, :], rstd[:, t:t + 1], None, ALU.mult).then_inc(norm["norm1"]["scaled"], 1)
            y, u, t0, t1, log1p = flat(w_k), flat(gam_c), stats[:, 16:24], stats[:, 24:32], stats[:, 8:16]
            dve.wait_ge(setup_a, 1)
            dve.tensor_scalar(u, y, 1.0, None, ALU.add).then_inc(setup_v, 1)
            dve.wait_ge(setup_v, 2)
            link(dve.tensor_scalar(t0, u, -1.0, None, ALU.add))
            link(dve.tensor_tensor(t0, y, t0, ALU.subtract))
            link(dve.reciprocal(t1, u))
            link(dve.tensor_tensor(t0, t0, t1, ALU.mult))
            dve.wait_ge(setup_a, 2)
            link(dve.tensor_tensor(log1p, log1p, t0, ALU.add))
            link(dve.tensor_scalar(flat(lg), flat(lg), 0.0, None, ALU.min))
            dve.tensor_tensor(flat(lg), flat(lg), log1p, ALU.subtract).then_inc(setup_v, 2)
            dve.wait_ge(setup_v, 4)
            dve.wait_ge(ld_tab, 3 * 16)
            for n in range(2):
                last = dve.tensor_scalar(w_k[:, n, :], lg[:, n, :], pos_col[:, n:n + 1], None, ALU.mult)
            last.then_inc(setup_v, 1)
            for h in range(RH):
                last = dve.tensor_scalar(decay[:, h, :], dist[:, 0, :], lg[:, 0, h:h + 1], None, ALU.mult)
            link(last)
            for h in range(RH):
                last = dve.scalar_tensor_tensor(decay[:, h, :], dist[:, 1, :], lg[:, 1, h:h + 1], decay[:, h, :], ALU.mult, ALU.add)
            last.then_inc(setup_v, 1)
            dve.wait_ge(setup_a, 3)
            link(dve.tensor_tensor(lamv[:, 2:3], lamv[:, 1:2], lamv[:, 0:1], ALU.subtract))
            link(dve.tensor_scalar(lamv[:, 2:3], lamv[:, 2:3], -LAM_INIT, None, ALU.add))
            dve.wait_ge(setup_a, 6)
            dve.tensor_scalar(w_k[:, :, :], w_k[:, :, :], P ** -0.5, None, ALU.mult).then_inc(setup_v, 1)
            dve.tensor_scalar(decay[:, :, :], decay[:, :, :], P ** -0.5, None, ALU.mult).then_inc(setup_v, 1)

            dve_split(dve, 0, 0)

            dve.wait_ge(cols_ready, 1)
            dve.wait_ge(ada_a_used, 8)
            for n, m in enumerate((SHIFT1, SCALE1)):
                last = dve.tensor_tensor(mod[:, m:m + KT, :], bank(7, 2 * KT, 2 * m).rearrange("p (m s) -> p m s", s=2),
                                         cols[:, ROW_BADA + m:ROW_BADA + m + KT].unsqueeze(2).to_broadcast([P, KT, 2]), ALU.add)
                last.then_inc(freed["dve"], 1)
            dve.wait_ge(freed["dve"], 2)

            def scales(m, gain):
                link(dve.scalar_tensor_tensor(sc[:, :, :], mod[:, m:m + KT, :], 1.0,
                                              cols[:, gain:gain + KT].unsqueeze(2).to_broadcast([P, KT, 2]), ALU.add, ALU.mult))

            scales(SCALE1, ROW_G1)
            dve_to_T(dve, "h", h_hi, h_lo, modulated(SHIFT1))

            def dense(name, evacuate, peel=0):
                def pair(i, last):
                    for par in range(2):
                        if not (last and par == 1):
                            dve_split(dve, unit_of(name, i, par) + 1, 1 - par)
                        evacuate(i, par)

                with dve.Fori(0, COUNT[name] // 2 - peel) as i:
                    pair(i, False)
                if peel:
                    pair(COUNT[name] // 2 - 1, True)

            def rotate(name, qk, first, tile0, swaps, before):
                def evacuate(i, par):
                    x = qk[:, bass.ds(i * 4 + (tile0 + 2 * par), 2), 0:LAT]
                    dve.wait_ge(freed["act"], freed_after(name, i, par, 1))
                    dve.wait_ge(rope_done, i * 2 + (first + par))
                    dve.tensor_tensor(rope_tmp[:, :, :], x, rope[:, 0:1, :].to_broadcast([P, 2, LAT]), ALU.mult).then_inc(rope_mul, 1)
                    dve.wait_ge(rope_in, i * (32 * swaps) + (before + 16 * swaps * (par + 1)))
                    dve.tensor_tensor(swapped[:, :, :], swapped[:, :, :], rope[:, 1:2, :].to_broadcast([P, 2, LAT]), ALU.mult).then_inc(rope_mul, 1)
                    dve.wait_ge(rope_mul, i * 4 + (2 * (first + par) + 2))
                    dve.tensor_tensor(x, rope_tmp[:, :, :], swapped[:, :, :], ALU.add).then_inc(rope_done, 1)
                return evacuate

            nothing = lambda i, par: None
            dve.wait_ge(ld_rope, 16)
            dense("qk_r", rotate("qk_r", qk_r, 0, 0, 2, 0))
            dense("v_r", nothing)
            dense("g_r", nothing)

            with dve.Fori(0, RH) as h:
                dve.wait_ge(r_s, h + 1)
                dve.wait_ge(r_out, h * TILES)
                dve.tensor_tensor(s_dec[:, :, :], psum[:, 2 * BANK:2 * BANK + TOK].rearrange("p (c i) -> p c i", i=P),
                                  decay[:, bass.ds(h, 1), :].to_broadcast([P, TILES, P]), ALU.mult).then_inc(r_dec, 1)
                dve.wait_ge(r_s0, h * 32 + 32)
                for s in range(3):
                    dve.wait_ge(r_kv, h * 4 + (s + 1))
                    dve.wait_ge(r_state, h * 3 + s)
                    for n, (c_to, c_from) in enumerate(((s + 1, s), (2 - s, 3 - s))):
                        last = dve.scalar_tensor_tensor(state[:, n, c_to, :], state[:, n, c_from, :], gam_c[:, n, bass.ds(h, 1)],
                                                        bank(4 + s % 2, RDV, n * RDV), ALU.mult, ALU.add)
                    last.then_inc(r_state, 1)
                for p_, c in enumerate(OUT_ORDER):
                    dve.wait_ge(r_y, h * TILES + (p_ + 1))
                    dve.bn_stats(bn6[:, bass.ds(h * TILES + c, 1), :].rearrange("p a b -> p (a b)"),
                                 y_nat[:, c, bass.ds(h * RDV, RDV)]).then_inc(r_bn, 1)
            dve.wait_ge(r_bn, RH * TILES)
            for n in range(RH * TILES):
                last = dve.bn_aggr(mean_var[:, n, :], bn6[:, n, :])
            last.then_inc(r_mv, 1)
            n = RH * TILES
            dve.wait_ge(r_mv, 1)
            dve.tensor_scalar(rstd[:, 0:n], mean_var[:, :, 1], GN_EPS, None, ALU.add).then_inc(norm["normy"]["mean"], 1)
            inverse("normy", n)
            dve.scalar_tensor_tensor(rstd[:, n:2 * n], mean_var[:, :, 0], -1.0, rstd[:, 0:n], ALU.mult, ALU.mult).then_inc(norm["normy"]["scaled"], 1)
            for h in range(RH):
                hs = slice(h * RDV, (h + 1) * RDV)
                dve.wait_ge(y_norm, (h + 1) * TILES)
                dve.tensor_tensor(y_nat[:, :, hs], y_nat[:, :, hs], g_r[:, :, hs], ALU.mult).then_inc(y_gated, 1)

            dense("gate_r", nothing)
            dve_to_T(dve, "yg", yg_hi, yg_lo, lambda k: [(slice(0, TOK), cols[:, ROW_GN + k:ROW_GN + k + 1], None, ALU.bypass)])
            dense("gate_d", nothing)

            def gated_ret(i, par):
                for j in range(2):
                    dve.wait_ge(mm_done, ready("ret_out", i, par, j))
                    if j == 1:
                        dve.tensor_copy(mod[:, bass.ds(i * 8 + (GATE1 + 4 * (ADA_FIRST["ret_out"] + par)), 4), :],
                                        bank(4 * par + 3, 8, HALF).rearrange("p (m s) -> p m s", s=2))
                    x = one_tile(mixT, i * 4 + (2 * par + j))
                    dve.tensor_tensor(x, T_tile(4 * par + 2 * j), x, ALU.mult).then_inc(freed["dve"], 1)

            dense("ret_out", gated_ret)
            dve.wait_ge(freed["dve"], START["diff_out"]["dve"])
            link(dve.tensor_tensor(mod[:, GATE1:, :], mod[:, GATE1:, :],
                                   cols[:, ROW_BADA + GATE1:ROW_BADA + 48].unsqueeze(2).to_broadcast([P, 32, 2]), ALU.add))
            scales(SCALE2, ROW_G2)
            dve.wait_ge(ld_rope, 32)
            dense("q_d", rotate("q_d", qk_d, 4, 0, 4, 128))
            dense("k_d", rotate("k_d", qk_d, 8, DH, 4, 128 + 256))
            dense("v_d", nothing)

            def maximum(h0, t0, m):
                h, t, n = tile_of(h0, t0)
                size = TOK if t < LAT_TILES else P
                dve.wait_ge(at_s, n * 2 + (m + 1))
                dve.reduce_max(sm[:, t, m:m + 1], psum[:, 2 * m * BANK:2 * m * BANK + size], axis=AX.X,
                               negate=True).then_inc(at_max, 1)

            def weights(h0, t0, part):
                h, t, n = tile_of(h0, t0)
                size = TOK if t < LAT_TILES else P
                p0, p1 = probs[:, PBUF[t], 0, 0:size], probs[:, PBUF[t], 1, 0:size]
                if part == 0:
                    dve.wait_ge(at_e, n * 2 + 2)
                    dve.reciprocal(sm[:, t, 4:6], sm[:, t, 2:4]).then_inc(at_r, 1)
                    dve.wait_ge(at_r, n + 1)
                    dve.tensor_scalar(p1, p1, sm[:, t, 5:6], lamv[:, 2:3], ALU.mult, ALU.mult).then_inc(at_a1, 1)
                else:
                    dve.wait_ge(at_a1, n + 1)
                    dve.scalar_tensor_tensor(p0, p0, sm[:, t, 4:5], p1, ALU.mult, ALU.add).then_inc(at_a, 1)

            maximum(0, 0, 0)
            maximum(0, 0, 1)
            maximum(0, 1, 0)
            weights(0, 0, 0)
            maximum(0, 1, 1)
            weights(0, 0, 1)
            maximum(0, 2, 0)
            weights(0, 1, 0)
            maximum(0, 2, 1)
            weights(0, 1, 1)
            with dve.Fori(0, DH - 1) as h:
                for t in range(2, TILES + 2):
                    maximum(h, t + 1, 0)
                    weights(h, t, 0)
                    maximum(h, t + 1, 1)
                    weights(h, t, 1)
            for t in range(2, TILES):
                if t + 1 < TILES:
                    maximum(DH - 1, t + 1, 0)
                weights(DH - 1, t, 0)
                if t + 1 < TILES:
                    maximum(DH - 1, t + 1, 1)
                weights(DH - 1, t, 1)

            dve.wait_ge(at_T, DH * TILES)
            dve.memset(ones[:, :], 1.0).then_inc(ones_set, 1)
            dve.wait_ge(at_oe, 2 + DH * TILES)
            mean("normo", DH * TILES, 1.0 / P, RMS_EPS)
            for n in range(8):
                m = (GATE1 if n < 4 else GATE2) + 4 * (n % 2)
                if n >= 2:
                    dve.wait_ge(gb_ps, n - 1)
                dve.tensor_tensor(diag[:, n % 2, :, :], ident[:, :].unsqueeze(1).to_broadcast([P, 4, P]),
                                  mod[:, m:m + 4, (n // 2) % 2:(n // 2) % 2 + 1].to_broadcast([P, 4, P]), ALU.mult).then_inc(gb_diag, 1)
            inverse("normo", DH * TILES)
            r = rstd[:, :].rearrange("p (h t) -> p h t", t=TILES)
            for t in range(TILES):
                x = o_nat[:, t, :].rearrange("p (h e) -> p h e", e=P)
                dve.tensor_tensor(x, x, r[:, :, t:t + 1].to_broadcast([P, DH, P]), ALU.mult).then_inc(norm["normo"]["scaled"], 1)
            subln = cols[:, ROW_SUBLN:ROW_SUBLN + 1]
            dve_to_T(dve, "od", od_hi, od_lo, lambda k: [(slice(0, TOK), subln, 1.0 - LAM_INIT, ALU.mult)])

            def mixed(i, par):
                for j in range(2):
                    tile = i * 4 + (2 * par + j)
                    g, x = one_tile(gate_d, tile), one_tile(mixT, tile)
                    dve.wait_ge(mm_done, ready("diff_out", i, par, j))
                    dve.tensor_tensor(g, T_tile(4 * par + 2 * j), g, ALU.mult).then_inc(freed["dve"], 1)
                    dve.wait_ge(freed["dve"], freed_after("diff_out", i, par, j))
                    dve.tensor_tensor(x, x, g, ALU.add).then_inc(mix_sum, 1)
                for j in range(2):
                    tile = i * 4 + (2 * par + j)
                    dve.wait_ge(mix_h, i * 4 + (2 * par + j + 1))
                    dve.tensor_tensor(one_tile(mix_lo, tile), one_tile(mixT, tile), one_tile(mix_hi, tile).bitcast(F32),
                                      ALU.subtract).then_inc(mix_l, 1)

            dense("diff_out", mixed)

            def residual(name, g, done0):
                def evacuate(i, par):
                    cs = bass.ds(i * (2 * UC) + par * UC, UC)
                    for j in range(2):
                        dve.wait_ge(mm_done, ready(name, i, par, j))
                        nt = LAT_TILES if j == 0 else 1
                        src = bank(4 * par + 2 * j, nt * UC).rearrange("p (t c) -> p t c", c=UC) if j else \
                            psum[:, 4 * par * BANK:(4 * par + 2) * BANK].rearrange("p (t c) -> p t c", c=UC)
                        row = gate_row[:, 2 * g + j:2 * g + j + 1, cs].to_broadcast([P, nt, UC])
                        x = x1[:, 0:LAT_TILES, cs] if j == 0 else x1[:, LAT_TILES:TILES, cs]
                        dve.wait_ge(x1_done, i * 4 + (done0 + 2 * par + j))
                        dve.tensor_tensor(gated[:, 0:nt, :], src, row, ALU.mult).then_inc(freed["dve"], 1)
                        dve.wait_ge(freed["dve"], freed_after(name, i, par, j))
                        dve.tensor_tensor(x, x, gated[:, 0:nt, :], ALU.add).then_inc(x1_done, 1)
                return evacuate

            dve.wait_ge(ld_x1, 32)
            dense("w_o", residual("w_o", 0, 0))
            dve.wait_ge(norm["norm2"]["sums"], TILES)
            mean("norm2", TILES, 1.0 / D, RMS_EPS)
            inverse("norm2", TILES)
            for t in range(TILES):
                dve.tensor_scalar(xn[:, t, :], x1[:, t, :], rstd[:, t:t + 1], None, ALU.mult).then_inc(norm["norm2"]["scaled"], 1)
            dve_to_T(dve, "h2", h2_hi, h2_lo, modulated(SHIFT2))

            def hidden(third):
                name = f"up{third}"
                base = sum(COUNT[f"up{n}"] for n in range(third))

                def evacuate(i, par):
                    if par == 0:
                        return
                    for j in range(2):
                        dve.wait_ge(mm_done, ready(name, i, 1, j))
                        dve.wait_ge(freed["act"], freed_after(name, i, 0, j))
                        dve.wait_ge(hid_l, i * 2 + base)
                        dve.tensor_tensor(in_halves(hid_f[:, j, :]), T_tile(4 + 2 * j), in_halves(silu_g[:, j, :]),
                                          ALU.mult).then_inc(freed["dve"], 1)
                    for j in range(2):
                        tile = i * 2 + j
                        dve.wait_ge(hid_h, i * 2 + (base + j + 1))
                        dve.tensor_tensor(hid_lo[:, bass.ds(tile, 1), :].rearrange("p a b -> p (a b)"), hid_f[:, j, :],
                                          hid_hi[:, bass.ds(tile, 1), :].rearrange("p a b -> p (a b)").bitcast(F32),
                                          ALU.subtract).then_inc(hid_l, 1)
                return evacuate

            for third in range(3):
                dense(f"up{third}", hidden(third))
                dense(f"down{third}", residual(f"down{third}", 1, 8 * (third + 1)), peel=int(third == 2))
            dve.wait_ge(norm["normf"]["sums"], TILES)
            mean("normf", TILES, 1.0 / D, RMS_EPS)
            inverse("normf", TILES)
            dve.wait_ge(ld_fin, 16)
            for t in range(TILES):
                dve.scalar_tensor_tensor(x1[:, t, :], x1[:, t, :], rstd[:, t:t + 1], fin_g[:, :], ALU.mult, ALU.mult).then_inc(y_done, 1)


def shape_constants():
    f = np.float32
    pos_r, pos_c = np.repeat(np.arange(LAT // GRID_W), GRID_W), np.tile(np.arange(GRID_W), LAT // GRID_W)

    def rotary(d):
        n = d // 4
        inv = (10000.0 ** (-np.arange(n) / n)).astype(f)
        ang = np.concatenate([pos_r[:, None].astype(f) * inv, pos_c[:, None].astype(f) * inv], axis=-1)
        cos, sin = np.cos(ang.astype(np.float64)).T, np.sin(ang.astype(np.float64)).T
        cos, sin = np.concatenate([cos, cos]), np.concatenate([-sin, sin])
        return np.stack([np.tile(cos, (P // d, 1)), np.tile(sin, (P // d, 1))]).astype(f)

    i = np.arange(P)
    gap = (i[None, :] - i[:, None]).astype(f)
    return {"const_ident": np.eye(P, dtype=f), "const_rope_ret": rotary(P), "const_rope_diff": rotary(DHD),
            "const_dist": np.stack([np.maximum(gap, 0), np.maximum(-gap, 0)]).astype(f),
            "const_row_pos": np.stack([i + 1, P - i]).astype(f),
            "const_pos_col": np.stack([P - 1 - i, i], axis=1).astype(f)}


OUTPUTS = (("y_prompt", (1, P, D)), ("y_sample", (1, LAT, D)), ("new_ret_fwd", (1, 1, RH, P, RDV)),
           ("new_ret_bwd", (1, 1, RH, P, RDV)), ("new_diff_k", (1, 1, P, DH, 2, DHD)),
           ("new_diff_v", (1, 1, P, DH, 2 * DHD)))


def kernel(**inputs):
    import concourse.bacc as bacc
    from concourse.bass_utils import run_bass_kernel_spmd

    nc = bacc.Bacc("TRN2", target_bir_lowering=False, num_devices=1)
    arrays, a, o = {}, {}, {}
    for name, x in {**inputs, **shape_constants()}.items():
        x = np.ascontiguousarray(x)
        arrays["in_" + name] = x
        a[name] = nc.dram_tensor("in_" + name, x.shape, F32, kind="ExternalInput").ap()
    for name, shape in OUTPUTS:
        o[name] = nc.dram_tensor("out_" + name, shape, F32, kind="ExternalOutput").ap()
    build(nc, a, o)
    r = run_bass_kernel_spmd(nc, [arrays], core_ids=[0])
    return tuple(r.results[0]["out_" + name] for name, _ in OUTPUTS)
```

```python
from contextlib import ExitStack

import numpy as np

import concourse.bass as bass
from concourse import mybir

F32 = mybir.dt.float32
F32R = mybir.dt.float32r
ACT = mybir.ActivationFunctionType
ALU = mybir.AluOpType
AX = mybir.AxisListType

P = 128
D = 1024
KT = D // P
LAT_TILES = 4
TILES = 5
LAT = LAT_TILES * P
TOK = TILES * P
HALF = TOK // 2
UC = 256
BANK = 512
RH = 4
RDV = 256
DH = 8
DHD = 64
FFN = 2816
GRID_W = 64
LAM_INIT = 0.2
RMS_EPS = 1e-6
GN_EPS = 1e-5
KB = 1024

ROW_BADA, ROW_G1, ROW_G2, ROW_BGATE, ROW_C, ROW_CCTX, ROW_GN, ROW_SUBLN = 0, 48, 56, 64, 80, 88, 96, 104
ROWS = 105

PHASES = [("qk_r", 4, "act", "act"), ("v_r", 4, "act", "act"), ("g_r", 4, "act", "act"),
          ("gate_r", 4, "act", "act"), ("gate_d", 4, "act", "act"), ("ret_out", 4, "dve", "dve"),
          ("q_d", 4, "act", "act"), ("k_d", 4, "act", "act"), ("v_d", 4, "act", "act"),
          ("diff_out", 4, "dve", "dve"), ("w_o", 4, "dve", "dve"),
          ("up0", 8, "act", "dve"), ("down0", 4, "dve", "dve"), ("up1", 8, "act", "dve"),
          ("down1", 4, "dve", "dve"), ("up2", 6, "act", "dve"), ("down2", 4, "dve", "dve")]


def lay_out_phases():
    first, count, reader, before, start = {}, {}, {}, {}, {}
    unit, total = 0, {"act": 2, "dve": 2}
    last = [("act", 2), ("dve", 2)]
    for name, n, *readers in PHASES:
        first[name], count[name], reader[name] = unit, n, readers
        before[name] = list(last)
        start[name] = dict(total)
        same = readers[0] == readers[1]
        for s in range(2):
            last[s] = (readers[s], total[readers[s]] + (2 * n - 2 + 2 * s if same else n))
        for e in set(readers):
            total[e] += 2 * n if same else n
        unit += n
    return first, count, reader, before, start


FIRST, COUNT, READER, BEFORE, START = lay_out_phases()
UNITS = sum(n for _, n, *_ in PHASES)
ADA_FIRST = {"gate_d": 0, "ret_out": 4, "q_d": 8, "k_d": 12}
SETUP_ACT, SETUP_DVE = 14, 8
SHIFT1, SCALE1, GATE1, SHIFT2, SCALE2, GATE2 = (KT * n for n in range(6))
SHIFTED = ("h", "h2")
PBUF = (0, 1, 2, 0, 1)
TBUF = (0, 1, 0, 1, 2)
OUT_ORDER = (4, 1, 2, 0, 3)


def freed_after(name, i, par, j):
    r = READER[name]
    if r[0] == r[1]:
        return i * 4 + (START[name][r[0]] + 2 * par + j + 1)
    return i * 2 + (START[name][r[par]] + j + 1)


def unit_of(name, i, par):
    return i * 2 + (FIRST[name] + par)


def ready(name, i, par, j):
    return i * 4 + (2 * FIRST[name] + 2 * par + j + 1)


def tile_of(h, t):
    return h + t // TILES, t % TILES, h * TILES + t


def build(nc, a, o):
    with ExitStack() as ctx:
        arena_bytes = 205 * KB + 512
        ctx.enter_context(nc.sbuf_tensor("arena", [P, arena_bytes // 4], F32))
        origin = nc.sbuf_base - arena_bytes

        def at(name, kb, shape, dt=F32):
            return nc.alloc_sbuf_tensor_at(name, shape, dt, offset=origin + int(kb * KB))

        def small(name, shape, dt=F32):
            return ctx.enter_context(nc.sbuf_tensor(name, shape, dt))

        def sem(name):
            return ctx.enter_context(nc.semaphore(name))

        H, W, A, B, Y, M, S = 0, 40, 88, 128, 148, 168, 188
        h_hi = at("h_hi", H, [P, KT, TOK], F32R)
        h_lo = at("h_lo", H + 20, [P, KT, TOK], F32R)
        mod_rows = at("mod_rows", H + 24, [2, 2 * D])
        o_nat = at("o_nat", H, [P, TILES, D])
        k_out = at("k_out", H + 16, [P, D])
        probs = at("probs", H + 20, [P, 3, 2, TOK])
        qz = at("qz", H + 35, [P, TILES, 2, P])
        diag = at("diag", H + 20, [P, 2, 4, P])
        ones = at("ones", H + 24, [P, P])
        mix_hi = at("mix_hi", H, [P, KT, TOK], F32R)
        mix_lo = at("mix_lo", H + 20, [P, KT, TOK], F32R)
        h2_hi = at("h2_hi", H, [P, KT, TOK], F32R)
        h2_lo = at("h2_lo", H + 20, [P, KT, TOK], F32R)
        w_raw = [at(f"w_raw{s}", W + 8 * s, [P, KT, UC]) for s in range(2)]
        w_hi = [at(f"w_hi{s}", W + 16 + 8 * s, [P, KT, UC], F32R) for s in range(2)]
        w_lo = [at(f"w_lo{s}", W + 32 + 8 * s, [P, KT, UC], F32R) for s in range(2)]
        x_nat = at("x_nat", A, [P, TILES, D])
        rows = at("rows", A + 20, [P, P])
        k_cache = at("k_cache", A + 21, [P, D])
        junk = at("junk", A + 25, [P, D])
        dist = at("dist", A + 29, [P, 2, P])
        row_pos = at("row_pos", A + 30, [P, 2, P])
        lam_in = at("lam_in", A + 31, [P, 4, DHD])
        lam_mul = at("lam_mul", A + 32, [P, 2, DHD])
        qk_r = at("qk_r", A, [P, 2 * RH, TOK])
        v_r = at("v_r", A + 20, [P, TILES, D])
        yg_hi = at("yg_hi", A, [P, KT, TOK], F32R)
        yg_lo = at("yg_lo", A + 20, [P, KT, TOK], F32R)
        qk_d = at("qk_d", A, [P, 2 * DH, TOK])
        od_hi = at("od_hi", A, [P, KT, TOK], F32R)
        od_lo = at("od_lo", A + 20, [P, KT, TOK], F32R)
        hid_hi = at("hid_hi", A, [P, KT, TOK], F32R)
        hid_lo = at("hid_lo", A + 20, [P, KT, TOK], F32R)
        rope = at("rope", B, [P, 2, LAT])
        swapped = at("swapped", B + 4, [P, 2, LAT])
        rope_tmp = at("rope_tmp", B + 8, [P, 2, LAT])
        g_r = at("g_r", B, [P, TILES, D])
        ada_b = [at(f"ada_b{s}", B + 12 + 4 * s, [P, KT // 2, UC]) for s in range(2)]
        v_d = at("v_d", B, [P, TILES, D])
        gate_row = at("gate_row", B, [P, 4, D])
        fin_g = at("fin_g", B + 16, [P, D])
        ada_a = [at(f"ada_a{s}", Y + 8 * s if s < 5 else H + 8 * (s - 5), [P, KT, UC]) for s in range(8)]
        y_nat = at("y_nat", Y, [P, TILES, D])
        gate_d = at("gate_d", Y, [P, KT, TOK])
        x1 = at("x1", Y, [P, TILES, D])
        k_fb = at("k_fb", M, [P, 2, TILES, P])
        q_fb = at("q_fb", M + 5, [P, 2, LAT_TILES, P])
        state = at("state", M + 9, [P, 2, LAT_TILES, RDV])
        mixT = at("mixT", M, [P, KT, TOK])
        xn = at("xn", M, [P, TILES, D])
        silu_g = at("silu_g", M, [P, 2, TOK])
        hid_f = at("hid_f", M + 5, [P, 2, TOK])
        gated = at("gated", M + 10, [P, 4, UC])
        junk2 = at("junk2", M + 16, [P, D])
        kc_T = at("kc_T", S, [P, DH, P])
        decay = at("decay", S + 4, [P, RH, P])
        w_q = at("w_q", S + 6, [P, 2, RH, P])
        v_cache = at("v_cache", S + 4, [P, D])
        hf = at("hf", S + 10, [P, 3, TOK])
        ada_acc = at("ada_acc", S + 10, [P, 2, 2, UC])
        k_head = at("k_head", S + 10, [P, TOK])
        s_dec = at("s_dec", S + 12.5, [P, TILES, P])
        kv_ctx = at("kv_ctx", S + 15, [P, 2 * RDV])
        bn6 = at("bn6", S + 17, [P, RH * TILES, 6])
        junk_o = at("junk_o", S + 8, [P, P])
        aT = at("aT", S + 10, [P, 3, TILES, P])
        ident = small("ident", [P, P])
        cols = small("cols", [P, ROWS])
        mod = small("mod", [P, 48, 2])
        silu_c = small("silu_c", [P, KT, 2])
        sc = small("sc", [P, KT, 2])
        stats = small("stats", [P, 40])
        rstd = small("rstd", [P, 40])
        pos_col = small("pos_col", [P, 2])
        w_k = small("w_k", [P, 2, RH])
        lg = small("lg", [P, 2, RH])
        gam_c = small("gam_c", [P, 2, RH])
        lamv = small("lamv", [P, 3])
        sm = small("sm", [P, TILES, 6])
        prime = small("prime", [P, 1])
        sub_gain = small("sub_gain", [P, 1])
        ones_col = small("ones_col", [P, 1])
        mean_var = stats[:, :].rearrange("p (n c) -> p n c", c=2)

        psum = ctx.enter_context(nc.psum_tensor("psum", [P, 8 * BANK], F32))

        def bank(b, n=BANK, at_=0):
            return psum[:, b * BANK + at_:b * BANK + at_ + n]

        def T_tile(b):
            return psum[:, b * BANK:(b + 2) * BANK].rearrange("p (b c) -> p b c", b=2)[:, :, 0:HALF]

        def in_halves(x):
            return x.rearrange("p (b c) -> p b c", b=2)

        def one_tile(x, n):
            return x[:, bass.ds(n, 1), :].rearrange("p a (b c) -> p (a b) c", b=2)

        w_landed = [sem(f"w_landed{s}") for s in range(2)]
        w_hi_done, w_lo_done = sem("w_hi_done"), sem("w_lo_done")
        mm_done = sem("mm_done")
        freed = {"act": sem("freed_act"), "dve": sem("freed_dve")}
        ld_ident, ld_rows, ld_x, ld_kc = sem("ld_ident"), sem("ld_rows"), sem("ld_x"), sem("ld_kc")
        ld_tab, ld_rope, ld_scal = sem("ld_tab"), sem("ld_rope"), sem("ld_scal")
        ada_a_in = [sem(f"ada_a_in{s}") for s in range(8)]
        ada_b_in = [sem(f"ada_b_in{s}") for s in range(2)]
        ada_row_ps, ada_row, ada_cols = sem("ada_row_ps"), sem("ada_row"), sem("ada_cols")
        ada_step = sem("ada_step")
        rows_T, cols_ready, kc_ps, kc_done = sem("rows_T"), sem("cols_ready"), sem("kc_ps"), sem("kc_done")
        norm = {n: {q: sem(f"{n}_{q}") for q in ("sums", "mean", "root", "scaled")}
                for n in ("norm1", "normy", "normo", "norm2", "normf")}
        setup_a, setup_v = sem("setup_a"), sem("setup_v")
        dve_step = sem("dve_step")
        n2t = {n: {q: sem(f"{n}_{q}") for q in ("ps", "f", "f2", "hi", "lo", "scale")} for n in ("h", "yg", "od", "h2")}
        rope_in, rope_mul, rope_done = sem("rope_in"), sem("rope_mul"), sem("rope_done")
        g_done = sem("g_done")
        r_k, r_kT, r_kfb, r_s, r_dec = sem("r_k"), sem("r_kT"), sem("r_kfb"), sem("r_s"), sem("r_dec")
        r_q, r_s0, r_kv, r_upd, r_state = sem("r_q"), sem("r_s0"), sem("r_kv"), sem("r_upd"), sem("r_state")
        r_ctx, r_ctx_out, r_out, r_y = sem("r_ctx"), sem("r_ctx_out"), sem("r_out"), sem("r_y")
        sub_ready = sem("sub_ready")
        r_bn, r_mv, y_norm, y_gated = sem("r_bn"), sem("r_mv"), sem("y_norm"), sem("y_gated")
        gr_done, gd_done, mix_r_done = sem("gr_done"), sem("gd_done"), sem("mix_r_done")
        ld_vc, vd_stored = sem("ld_vc"), sem("vd_stored")
        k_ps, k_stored = sem("k_ps"), sem("k_stored")
        at_z, at_qz, at_s, at_max, at_e = sem("at_z"), sem("at_qz"), sem("at_s"), sem("at_max"), sem("at_e")
        at_nm, at_r, at_a1, at_a, at_T = sem("at_nm"), sem("at_r"), sem("at_a1"), sem("at_a"), sem("at_T")
        at_aT, at_o, at_oe = sem("at_aT"), sem("at_o"), sem("at_oe")
        ones_set, gb_diag, gb_ps, gb_row = sem("ones_set"), sem("gb_diag"), sem("gb_ps"), sem("gb_row")
        mix_sum, mix_h, mix_l = sem("mix_sum"), sem("mix_h"), sem("mix_l")
        ld_x1, ld_fin, x1_done = sem("ld_x1"), sem("ld_fin"), sem("x1_done")
        silu_up, hid_h, hid_l = sem("silu_up"), sem("hid_h"), sem("hid_l")
        y_done, stored = sem("y_done"), sem("stored")

        def act_split(act, unit, s):
            act.wait_ge(w_landed[s], (unit - s) * 8 + 16)
            act.wait_ge(mm_done, unit * 2 - 2)
            act.activation(w_hi[s][:, :, :], w_raw[s][:, :, :], ACT.Copy).then_inc(w_hi_done, 1)

        def dve_split(dve, unit, s):
            dve.wait_ge(w_hi_done, unit + 1)
            dve.tensor_tensor(w_lo[s][:, :, :], w_raw[s][:, :, :], w_hi[s][:, :, :].bitcast(F32),
                              ALU.subtract).then_inc(w_lo_done, 1)

        def pe_wait_unit(pe, name, i, par):
            r, val = BEFORE[name][par]
            pe.wait_ge(freed[r], val)
            pe.wait_ge(freed[READER[name][par]], freed_after(name, i, par, 1) - (2 if READER[name][0] != READER[name][1] else 4))
            pe.wait_ge(w_lo_done, unit_of(name, i, par) + 1)

        def pe_T_unit(pe, name, i, par, hi, lo, split=None):
            for j in range(2):
                cs = slice(j * P, (j + 1) * P)
                for k in range(KT):
                    if split and par == 0 and j == 0:
                        pe.wait_ge(split[0], split[1] + k + 1)
                    for n, (w, x) in enumerate(((w_lo[par], hi), (w_hi[par], lo), (w_hi[par], hi))):
                        for h in range(2):
                            last = pe.matmul(bank(4 * par + 2 * j + h, HALF), w[:, k, cs],
                                             x[:, k, h * HALF:(h + 1) * HALF],
                                             start=(k == 0 and n == 0), stop=(k == KT - 1 and n == 2))
                if name in ADA_FIRST and j == 1:
                    pe.wait_ge(ada_step, i * 32 + (16 * (ADA_FIRST[name] + par) + 32))
                    for m in range(2):
                        for c in range(2):
                            last = pe.matmul(bank(4 * par + 3, 1, HALF + 2 * m + c), ada_acc[:, par, c, m * P:(m + 1) * P],
                                             ones_col[:, :], start=True, stop=True)
                last.then_inc(mm_done, 1)

        def pe_N_unit(pe, name, i, par, hi, lo, kt=KT, split=None):
            for t in range(TILES):
                ts = slice(t * P, (t + 1) * P)
                for k in range(kt):
                    if split and par == 0 and t == 0:
                        pe.wait_ge(split[0], split[1] + k + 1)
                    for n, (w, x) in enumerate(((w_lo[par], hi), (w_hi[par], lo), (w_hi[par], hi))):
                        last = pe.matmul(bank(4 * par + t // 2, UC, (t % 2) * UC), x[:, k, ts], w[:, k, :],
                                         start=(k == 0 and n == 0), stop=(k == kt - 1 and n == 2))
                if t >= LAT_TILES - 1:
                    last.then_inc(mm_done, 1)

        def pe_dense(pe, name, unit, hi, lo, **kw):
            with pe.Fori(0, COUNT[name] // 2) as i:
                for par in range(2):
                    pe_wait_unit(pe, name, i, par)
                    unit(pe, name, i, par, hi, lo, **kw)

        def pe_to_T(pe, which, src):
            q = n2t[which]
            readers = (q["f"], q["f2"]) if which in SHIFTED else (q["lo"],)

            def wait_read(k):
                for r in readers:
                    pe.wait_ge(r, k + 1)

            for k in range(KT):
                if k >= 4:
                    wait_read(k - 4)
                b = 2 * (k % 4)
                for t in range(TILES):
                    last = pe.transpose(bank(b + t // 4, P, (t % 4) * P), src[:, t, k * P:(k + 1) * P], ident[:, :])
                last.then_inc(q["ps"], 1)
            wait_read(5)

        def in_pair(k):
            return psum[:, 2 * (k % 4) * BANK:2 * (k % 4) * BANK + TOK]

        def modulated(which, shift, k, c, cs):
            return hf[:, k % 3, cs], in_pair(k)[:, cs], sc[:, k, c:c + 1], mod[:, shift + k, c:c + 1]

        def act_to_T_shifted(act, which, hi, shift):
            q = n2t[which]

            def modulate(k):
                act.wait_ge(q["ps"], k + 1)
                if k >= 3:
                    act.wait_ge(q["lo"], k - 2)
                out, x, scale, bias = modulated(which, shift, k, 1, slice(LAT, TOK))
                act.activation(out, x, ACT.Identity, scale=scale, bias=bias).then_inc(q["f"], 1)

            act.wait_ge(q["scale"], 1)
            modulate(0)
            for k in range(KT):
                if k + 1 < KT:
                    modulate(k + 1)
                act.wait_ge(q["f"], k + 1)
                act.wait_ge(q["f2"], k + 1)
                act.activation(hi[:, k, :], hf[:, k % 3, :], ACT.Copy).then_inc(q["hi"], 1)

        def dve_to_T_shifted(dve, which, hi, lo, shift):
            q = n2t[which]
            dve.wait_ge(q["scale"], 1)
            for k in range(KT + 2):
                if k < KT:
                    dve.wait_ge(q["ps"], k + 1)
                    if k >= 3:
                        dve.wait_ge(q["lo"], k - 2)
                    out, x, scale, bias = modulated(which, shift, k, 0, slice(0, LAT))
                    dve.tensor_scalar(out, x, scale, bias, ALU.mult, ALU.add).then_inc(q["f2"], 1)
                if k >= 2:
                    dve.wait_ge(q["hi"], k - 1)
                    dve.tensor_tensor(lo[:, k - 2, :], hf[:, (k - 2) % 3, :], hi[:, k - 2, :].bitcast(F32),
                                      ALU.subtract).then_inc(q["lo"], 1)

        def act_to_T(act, which, hi, scale):
            q = n2t[which]
            for k in range(KT):
                act.wait_ge(q["ps"], k + 1)
                act.activation(hi[:, k, :], in_pair(k), ACT.Copy, scale=scale(k)).then_inc(q["hi"], 1)

        def dve_to_T(dve, which, hi, lo, scale):
            q = n2t[which]
            for k in range(KT):
                dve.wait_ge(q["hi"], k + 1)
                dve.scalar_tensor_tensor(lo[:, k, :], in_pair(k), scale(k), hi[:, k, :].bitcast(F32),
                                         ALU.mult, ALU.subtract).then_inc(q["lo"], 1)

        def gn_gain(k):
            return cols[:, ROW_GN + k:ROW_GN + k + 1]

        def subln_gain(k):
            return sub_gain[:, :]

        packed = ((ROW_C, a["c"][0]), (ROW_CCTX, a["c_ctx"]), (ROW_BADA, a["b_ada"][0]), (ROW_G1, a["norm1_g"][0]),
                  (ROW_G2, a["norm2_g"][0]), (ROW_BGATE, a["b_gate"][0]), (ROW_GN, a["ret_gn_g"][0]),
                  (ROW_SUBLN, a["diff_subln_g"][0]))

        def load_rows(engine, vectors):
            for row, vec in vectors:
                n = vec.shape[0] // P
                engine.dma_start(rows[row:row + n, :], vec.rearrange("(r c) -> r c", c=P)).then_inc(ld_rows, 16)

        block = ctx.enter_context(nc.Block())

        @block.sync
        def _(sp):
            w_in = a["w_in"][0].rearrange("(k p) c -> p k c", p=P)
            ada = a["w_ada"][0].rearrange("(k p) c -> p k c", p=P)
            load_rows(sp, packed[:4])
            sp.dma_start(x_nat[:, 0:LAT_TILES, :], a["x_sample"][0].rearrange("(t p) c -> p t c", p=P)).then_inc(ld_x, 16)
            sp.dma_start(x_nat[:, LAT_TILES, :], a["x_prompt"][0]).then_inc(ld_x, 16)
            sp.dma_start(dist[:, :, :], a["const_dist"].rearrange("a p t -> p a t")).then_inc(ld_tab, 16)
            sp.dma_start(row_pos[:, :, :], a["const_row_pos"].partition_broadcast(P)).then_inc(ld_tab, 16)
            sp.dma_start(pos_col[:, :], a["const_pos_col"]).then_inc(ld_tab, 16)
            sp.dma_start(k_cache[:, :], a["cache_diff_k"][0, 0].rearrange("p h m d -> p (h m d)")).then_inc(ld_kc, 16)
            for n in range(8):
                sp.dma_start(ada_a[n][:, :, :], ada[:, :, n * UC:(n + 1) * UC]).then_inc(ada_a_in[n], 16)
                if n == 4:
                    sp.dma_start(w_raw[0][:, :, :], w_in[:, :, 0:UC]).then_inc(w_landed[0], 16)
            sp.dma_start(w_raw[1][:, :, :], w_in[:, :, UC:2 * UC]).then_inc(w_landed[1], 16)
            for s in range(2):
                sp.wait_ge(w_lo_done, s + 1)
                sp.dma_start(w_raw[s][:, :, :], w_in[:, :, (2 + s) * UC:(3 + s) * UC]).then_inc(w_landed[s], 16)

            def stream(name, sources):
                with sp.Fori(0, COUNT[name] // 2) as i:
                    for s, (view, col, stride, kt) in enumerate(sources):
                        c = sp.snap(i * stride + col)
                        sp.wait_ge(w_lo_done, unit_of(name, i, s) - 1)
                        sp.dma_start(w_raw[s][:, 0:kt, :], view[:, 0:kt, bass.ds(c, UC)]).then_inc(w_landed[s], 16)

            def columns(view, col, kt=KT):
                return [(view, col, 2 * UC, kt), (view, col + UC, 2 * UC, kt)]

            by_tile = {n: a[n][0].rearrange("(k p) c -> p k c", p=P)
                       for n in ("w_ret_out", "w_diff_out", "w_o", "w_ffn_gate", "w_ffn_up", "w_ffn_down")}
            stream("v_r", columns(w_in, 1024))
            stream("g_r", columns(w_in, 2048))
            stream("gate_r", columns(w_in, 6144))
            stream("gate_d", columns(w_in, 7168))
            stream("ret_out", columns(by_tile["w_ret_out"], 0))
            stream("q_d", columns(w_in, 3072))
            stream("k_d", columns(w_in, 4096))
            stream("v_d", columns(w_in, 5120))
            stream("diff_out", columns(by_tile["w_diff_out"], 0))
            stream("w_o", columns(by_tile["w_o"], 0))
            for third in range(3):
                c0, kt = third * D, min(KT, FFN // P - third * KT)
                stream(f"up{third}", [(by_tile["w_ffn_gate"], c0, UC, KT), (by_tile["w_ffn_up"], c0, UC, KT)])
                stream(f"down{third}", columns(by_tile["w_ffn_down"][:, third * KT:third * KT + kt, :], 0, kt))
            for t in range(TILES):
                sp.wait_ge(y_done, t + 1)
                dst = o["y_prompt"][0] if t == LAT_TILES else o["y_sample"][0, t * P:(t + 1) * P, :]
                sp.dma_start(dst, x1[:, t, :]).then_inc(stored, 16)
            sp.wait_ge(stored, TILES * 16)
            sp.wait_ge(vd_stored, 16)
            sp.wait_ge(k_stored, 16)
            sp.wait_ge(r_ctx_out, RH * 32)

        @block.gpsimd
        def _(pool):
            pool.dma_start(ident[:, :], a["const_ident"]).then_inc(ld_ident, 16)
            for n, w in enumerate(("ret_decay_fwd", "ret_decay_bwd")):
                pool.dma_start(lg[:, n, :], a[w][0].partition_broadcast(P)).then_inc(ld_scal, 16)
            for n, w in enumerate(("q1", "q2", "k1", "k2")):
                pool.dma_start(lam_in[:, n, :], a["diff_lambda_" + w][0].partition_broadcast(P)).then_inc(ld_scal, 16)
            pool.dma_start(rope[:, :, :], a["const_rope_ret"].rearrange("a p t -> p a t")).then_inc(ld_rope, 16)

            ada = a["w_ada"][0].rearrange("(k p) c -> p k c", p=P)

            def load_ada(name, i, par):
                u = ADA_FIRST[name] + par
                c = pool.snap(i * (2 * UC) + (2 * D + u * UC))
                for r in range(2):
                    pool.wait_ge(ada_step, i * 32 + (16 * u + 8 * r + 8))
                    pool.dma_start(ada_b[r][:, :, :],
                                   ada[:, r * KT // 2:(r + 1) * KT // 2, bass.ds(c, UC)]).then_inc(ada_b_in[r], 16)

            def swap_halves(name, qk, size, first, tile0, i, par):
                pool.wait_ge(freed["act"], freed_after(name, i, par, 1))
                pool.wait_ge(rope_done, i * 2 + (first + par))
                tile = i * 4 + (tile0 + 2 * par)
                for r in range(0, P, size):
                    f = r + size if (r // size) % 2 == 0 else r - size
                    pool.dma_start(swapped[r:r + size, :, :], qk[f:f + size, bass.ds(tile, 2), 0:LAT]).then_inc(rope_in, 16)

            with pool.Fori(0, 2) as i:
                for par in range(2):
                    swap_halves("qk_r", qk_r, P // 2, 0, 0, i, par)

            pool.wait_ge(rope_done, 4)
            pool.wait_ge(setup_a, SETUP_ACT)
            with pool.Fori(0, RH) as h:
                pool.wait_ge(r_out, h * TILES)
                for n, (src, c) in enumerate((("state_ret_fwd", 0), ("state_ret_bwd", LAT_TILES - 1))):
                    pool.dma_start(state[:, n, c, :],
                                   a[src][0, 0, bass.ds(h, 1)].rearrange("h k v -> k (h v)")).then_inc(r_s0, 16)
                q = qk_r[:, bass.ds(h, 1), 0:LAT].rearrange("p a (c i) -> p (a c) i", i=P)
                for n in range(2):
                    w = w_q[:, n, bass.ds(h, 1), :].to_broadcast([P, LAT_TILES, P])
                    pool.tensor_tensor(q_fb[:, n, :, :], q, w, ALU.mult).then_inc(r_q, 1)

            pool.wait_ge(r_out, RH * TILES)
            pool.dma_start(v_cache[:, :], a["cache_diff_v"][0, 0].rearrange("p h e -> p (h e)")).then_inc(ld_vc, 16)
            pool.wait_ge(y_gated, RH)
            pool.dma_start(rope[:, :, :], a["const_rope_diff"].rearrange("a p t -> p a t")).then_inc(ld_rope, 16)
            for name in ("gate_d", "ret_out"):
                with pool.Fori(0, 2) as i:
                    for par in range(2):
                        load_ada(name, i, par)
            for name, first, tile0 in (("q_d", 4, 0), ("k_d", 8, DH)):
                with pool.Fori(0, 2) as i:
                    for par in range(2):
                        load_ada(name, i, par)
                        swap_halves(name, qk_d, P // 4, first, tile0, i, par)

            pool.wait_ge(freed["act"], START["diff_out"]["act"])
            pool.dma_start(o["new_diff_v"][0, 0].rearrange("p h e -> p (h e)"), v_d[:, LAT_TILES, :]).then_inc(vd_stored, 16)
            pool.memset(qz[:, :, :, :], 0.0).then_inc(at_z, 1)
            pool.wait_ge(at_z, 1)

            def fill_qz(t, src):
                for m in range(2):
                    r = slice(m * DHD, (m + 1) * DHD)
                    pool.tensor_copy(qz[r, t, m, :], src(r)).then_inc(at_qz, 1)

            for t in range(TILES):
                fill_qz(t, lambda r: qk_d[r, 0, t * P:(t + 1) * P])
            pool.wait_ge(at_oe, 2)
            pool.dma_start(o["new_diff_k"][0, 0].rearrange("p h m d -> p (h m d)"), k_out[:, :]).then_inc(k_stored, 16)
            with pool.Fori(1, DH) as h:
                for t in range(TILES):
                    pool.wait_ge(at_s, h * (2 * TILES) + (2 * t + 2 - 2 * TILES))
                    fill_qz(t, lambda r: qk_d[r, bass.ds(h, 1), t * P:(t + 1) * P])

            pool.wait_ge(mix_sum, KT)
            pool.dma_start(x1[:, 0:LAT_TILES, :], a["x_sample"][0].rearrange("(t p) c -> p t c", p=P)).then_inc(ld_x1, 16)
            pool.dma_start(x1[:, LAT_TILES, :], a["x_prompt"][0]).then_inc(ld_x1, 16)
            pool.dma_start(fin_g[:, :], a["final_norm_g"].partition_broadcast(P)).then_inc(ld_fin, 16)

        @block.tensor
        def _(pe):
            pe.wait_ge(ld_ident, 16)
            pe.wait_ge(ld_rows, 8 * 16)
            pe.transpose(bank(6, ROWS), rows[0:ROWS, :], ident[0:ROWS, 0:ROWS]).then_inc(rows_T, 1)
            pe.wait_ge(ld_kc, 16)
            for h in range(DH):
                last = pe.transpose(bank(4 + h // 4, P, (h % 4) * P), k_cache[:, h * P:(h + 1) * P], ident[:, :])
            last.then_inc(kc_ps, 1)

            def mod_columns(group, start, stop):
                pe.wait_ge(ada_row, group)
                for m in range(start, stop):
                    last = pe.transpose(bank(7, 2, 2 * m), mod_rows[0:2, m * P:(m + 1) * P], ident[0:2, 0:2])
                last.then_inc(ada_cols, 1)

            pe.wait_ge(freed["act"], 2)
            for n in range(8):
                pe.wait_ge(ada_a_in[n], 16)
                for k in range(KT):
                    last = pe.matmul(psum[0:2, n * UC:(n + 1) * UC], silu_c[:, k, :], ada_a[n][:, k, :],
                                     start=(k == 0), stop=(k == KT - 1))
                last.then_inc(ada_row_ps, 1)
            mod_columns(1, 0, 12)
            mod_columns(2, 12, 16)

            pe.wait_ge(norm["norm1"]["scaled"], TILES)
            pe.wait_ge(kc_done, 1)
            pe.wait_ge(freed["dve"], 2)
            pe_to_T(pe, "h", x_nat)
            pe_dense(pe, "qk_r", pe_T_unit, h_hi, h_lo, split=(n2t["h"]["lo"], 0))
            pe_dense(pe, "v_r", pe_N_unit, h_hi, h_lo)
            pe_dense(pe, "g_r", pe_N_unit, h_hi, h_lo)

            for s in range(2):
                pe.wait_ge(freed["act"], START["gate_r"]["act"])
            with pe.Fori(0, RH) as h:
                def chunk(c):
                    return slice(c * P, (c + 1) * P)

                def v_chunk(c):
                    return v_r[:, c, bass.ds(h * RDV, RDV)]

                pe.wait_ge(r_k, h + 1)
                pe.wait_ge(r_kfb, h * 2)
                for c in range(TILES):
                    last = pe.transpose(bank(c // 4, P, (c % 4) * P), k_head[:, chunk(c)], ident[:, :])
                last.then_inc(r_kT, 1)
                pe.wait_ge(rope_done, 4)
                pe.wait_ge(r_dec, h)
                for c in range(TILES):
                    q = qk_r[:, bass.ds(h, 1), chunk(c)].rearrange("p a i -> p (a i)")
                    last = pe.matmul(bank(2 + c // 4, P, (c % 4) * P), k_head[:, chunk(c)], q, start=True, stop=True)
                last.then_inc(r_s, 1)
                pe.wait_ge(r_kfb, h * 2 + 2)
                for s in range(4):
                    f, b = (s, 3 - s) if s < 3 else (4, 4)
                    if s < 2:
                        pe.wait_ge(r_state, h * 3)
                        pe.wait_ge(r_ctx, h)
                    else:
                        pe.wait_ge(r_state, h * 3 + (s - 1))
                    pe.matmul(bank(4 + s % 2, RDV), k_fb[:, 0, f, :], v_chunk(f), start=True, stop=True)
                    pe.matmul(bank(4 + s % 2, RDV, RDV), k_fb[:, 1, b, :], v_chunk(b), start=True, stop=True).then_inc(r_kv, 1)
                pe.wait_ge(r_dec, h + 1)
                pe.wait_ge(r_q, h * 2 + 2)
                pe.wait_ge(r_s0, h * 32 + 32)
                for p_, c in enumerate(OUT_ORDER):
                    pe.wait_ge(r_y, h * TILES + max(0, p_ - 1))
                    out = bank(6 + p_ % 2, RDV)
                    if c < LAT_TILES:
                        pe.wait_ge(r_state, h * 3 + (2 if c in (1, 2) else 3))
                        pe.matmul(out, q_fb[:, 0, c, :], state[:, 0, c, :], start=True, stop=False)
                        pe.matmul(out, q_fb[:, 1, c, :], state[:, 1, c, :], start=False, stop=False)
                    pe.matmul(out, s_dec[:, c, :], v_chunk(c), start=(c == LAT_TILES), stop=True).then_inc(r_out, 1)
            pe.wait_ge(r_y, RH * TILES)
            pe.wait_ge(r_state, RH * 3)
            pe.wait_ge(r_ctx, RH)

            pe_dense(pe, "gate_r", pe_T_unit, h_hi, h_lo)
            pe.wait_ge(freed["act"], START["gate_d"]["act"])
            pe.wait_ge(y_gated, RH)
            pe_to_T(pe, "yg", y_nat)
            pe_dense(pe, "gate_d", pe_T_unit, h_hi, h_lo)
            pe_dense(pe, "ret_out", pe_T_unit, yg_hi, yg_lo, split=(n2t["yg"]["lo"], 0))
            pe_dense(pe, "q_d", pe_T_unit, h_hi, h_lo)
            pe_dense(pe, "k_d", pe_T_unit, h_hi, h_lo)
            pe_dense(pe, "v_d", pe_N_unit, h_hi, h_lo)

            pe.wait_ge(freed["act"], START["diff_out"]["act"])
            pe.wait_ge(rope_done, 12)
            for h in range(DH):
                last = pe.transpose(bank(6 + h // 4, P, (h % 4) * P), qk_d[:, DH + h, LAT:TOK], ident[:, :])
            last.then_inc(k_ps, 1)
            pe.wait_ge(ld_vc, 16)
            pe.wait_ge(kc_done, 1)

            def scores(h0, t0, m, first=False):
                h, t, n = tile_of(h0, t0)
                pe.wait_ge(at_qz, n * 2 + (m + 1))
                if not first:
                    pe.wait_ge(at_e, n * 2 + (m - 1))
                if t < LAT_TILES:
                    k = qk_d[:, bass.ds(h + DH, 1), 0:LAT].rearrange("p a i -> p (a i)")
                    pe.matmul(bank(2 * m), qz[:, t, m, :], k, start=True, stop=True)
                    k = kc_T[:, bass.ds(h, 1), :].rearrange("p a i -> p (a i)")
                    last = pe.matmul(bank(2 * m + 1, P), qz[:, t, m, :], k, start=True, stop=True)
                else:
                    k = qk_d[:, bass.ds(h + DH, 1), LAT:TOK].rearrange("p a i -> p (a i)")
                    last = pe.matmul(bank(2 * m, P), qz[:, t, m, :], k, start=True, stop=True)
                last.then_inc(at_s, 1)

            def weights_T(h0, t0, first=False):
                h, t, n = tile_of(h0, t0)
                pe.wait_ge(at_a, n + 1)
                if not first:
                    pe.wait_ge(at_aT, n)
                for c in range(TILES if t < LAT_TILES else 1):
                    last = pe.transpose(bank(4 + c // 4, P, (c % 4) * P), probs[:, PBUF[t], 0, c * P:(c + 1) * P], ident[:, :])
                last.then_inc(at_T, 1)

            def outputs(h0, t0):
                h, t, n = tile_of(h0, t0)
                pe.wait_ge(at_aT, n + 1)
                pe.wait_ge(at_oe, n + (2 if t == 0 else 1))
                out = bank(6 + t % 2, P)
                for c in range(TILES if t < LAT_TILES else 1):
                    if t == LAT_TILES:
                        val = v_d[:, LAT_TILES, bass.ds(h * P, P)]
                    else:
                        val = v_d[:, c, bass.ds(h * P, P)] if c < LAT_TILES else v_cache[:, bass.ds(h * P, P)]
                    last = pe.matmul(out, aT[:, TBUF[t], c, :], val, start=(c == 0),
                                     stop=(c == LAT_TILES or t == LAT_TILES))
                last.then_inc(at_o, 1)

            scores(0, 0, 0, first=True)
            scores(0, 0, 1, first=True)
            scores(0, 1, 0)
            scores(0, 1, 1)
            scores(0, 2, 0)
            weights_T(0, 0, first=True)
            scores(0, 2, 1)
            with pe.Fori(0, DH - 1) as h:
                for t in range(2, TILES + 2):
                    scores(h, t + 1, 0)
                    weights_T(h, t - 1)
                    scores(h, t + 1, 1)
                    outputs(h, t - 2)
            for t in range(2, TILES + 2):
                if t + 1 < TILES:
                    scores(DH - 1, t + 1, 0)
                if t - 1 < TILES:
                    weights_T(DH - 1, t - 1)
                if t + 1 < TILES:
                    scores(DH - 1, t + 1, 1)
                outputs(DH - 1, t - 2)

            pe.wait_ge(at_oe, 2 + DH * TILES)
            pe.wait_ge(ones_set, 1)
            for n in range(8):
                pe.wait_ge(gb_diag, n + 1)
                pe.matmul(bank(n), ones[:, :], diag[:, n % 2, :, :].rearrange("p a b -> p (a b)"),
                          start=True, stop=True).then_inc(gb_ps, 1)
            pe.wait_ge(norm["normo"]["scaled"], TILES)
            pe.wait_ge(gb_row, 8)
            pe_to_T(pe, "od", o_nat)
            pe_dense(pe, "diff_out", pe_T_unit, od_hi, od_lo, split=(n2t["od"]["lo"], 0))
            pe_dense(pe, "w_o", pe_N_unit, mix_hi, mix_lo, split=(mix_l, 0))
            pe.wait_ge(freed["dve"], START["up0"]["dve"])
            pe.wait_ge(norm["norm2"]["scaled"], TILES)
            pe_to_T(pe, "h2", xn)
            tiles = 0
            for third in range(3):
                pe_dense(pe, f"up{third}", pe_T_unit, h2_hi, h2_lo, split=(n2t["h2"]["lo"], 0))
                kt = COUNT[f"up{third}"]
                pe_dense(pe, f"down{third}", pe_N_unit, hid_hi, hid_lo, kt=kt, split=(hid_l, tiles))
                tiles += kt

        @block.scalar
        def _(act):
            load_rows(act, packed[4:])
            act.wait_ge(rows_T, 1)
            act.activation(cols[:, :], bank(6, ROWS), ACT.Copy).then_inc(cols_ready, 1)
            for n, row in enumerate((ROW_C, ROW_CCTX)):
                act.activation(silu_c[:, :, n], bank(6, KT, row), ACT.Silu).then_inc(freed["act"], 1)
            def sums(which, src, waste):
                for t in range(TILES):
                    if t:
                        act.wait_ge(norm[which]["sums"], t)
                    act.activation(waste[:, :], src[:, t, :], ACT.Square, accum_out=stats[:, t:t + 1]).then_inc(norm[which]["sums"], 1)

            def root(which, n):
                act.wait_ge(norm[which]["mean"], 1)
                act.activation(rstd[:, 0:n], rstd[:, 0:n], ACT.Sqrt).then_inc(norm[which]["root"], 1)

            act.wait_ge(ld_x, 32)
            sums("norm1", x_nat, junk)
            root("norm1", TILES)

            act.wait_ge(kc_ps, 1)
            act.activation(kc_T[:, :, :].rearrange("p a b -> p (a b)"), psum[:, 4 * BANK:6 * BANK], ACT.Copy).then_inc(kc_done, 1)

            act.wait_ge(setup_v, 1)
            act.activation(w_k[:, :, :], gam_c[:, :, :], ACT.Exp, scale=-1.0).then_inc(setup_a, 1)
            act.wait_ge(setup_v, 2)
            act.activation(stats[:, 8:16], gam_c[:, :, :].rearrange("p a b -> p (a b)"), ACT.Ln).then_inc(setup_a, 1)
            act.wait_ge(setup_v, 4)
            act.activation(lamv[:, 0:2], lamv[:, 0:2], ACT.Exp).then_inc(setup_a, 1)
            act.activation(gam_c[:, :, :], lg[:, :, :], ACT.Exp, scale=float(P)).then_inc(setup_a, 1)
            act.wait_ge(setup_v, 6)
            act.activation(w_k[:, :, :], w_k[:, :, :], ACT.Exp).then_inc(setup_a, 1)
            act.activation(decay[:, :, :], decay[:, :, :], ACT.Exp).then_inc(setup_a, 1)
            for n in range(2):
                for h in range(RH):
                    act.activation(w_q[:, n, h, :], row_pos[:, n, :], ACT.Exp, scale=lg[:, n, h:h + 1]).then_inc(setup_a, 1)
            act.wait_ge(w_landed[0], 16)
            act.activation(w_hi[0][:, :, :], w_raw[0][:, :, :], ACT.Copy).then_inc(w_hi_done, 1)
            for group, (u, v) in enumerate(((0, 6), (6, 8))):
                act.wait_ge(ada_row_ps, v)
                act.activation(mod_rows[:, u * UC:v * UC], psum[0:2, u * UC:v * UC], ACT.Copy).then_inc(ada_row, 1)
            act_to_T_shifted(act, "h", h_hi, SHIFT1)

            def dense(name, evacuate, peel=0):
                def pair(i, last):
                    for par in range(2):
                        if not (last and par == 1):
                            act_split(act, unit_of(name, i, par) + 1, 1 - par)
                        evacuate(i, par)

                with act.Fori(0, COUNT[name] // 2 - peel) as i:
                    pair(i, False)
                if peel:
                    pair(COUNT[name] // 2 - 1, True)

            def set_table(func):
                act.activation(prime[:, :], ident[:, 0:1], func)

            def copy_ada(name, i, par):
                act.activation(mod[:, bass.ds(i * 4 + (GATE1 + 2 * (ADA_FIRST[name] + par)), 2), :],
                               bank(4 * par + 3, 4, HALF).rearrange("p (m s) -> p m s", s=2), ACT.Copy)

            def copy_T(name, dst, tile0, scale):
                def evacuate(i, par):
                    for j in range(2):
                        act.wait_ge(mm_done, ready(name, i, par, j))
                        if name in ADA_FIRST and j == 1:
                            copy_ada(name, i, par)
                        act.activation(one_tile(dst, i * 4 + (tile0 + 2 * par + j)), T_tile(4 * par + 2 * j), ACT.Copy,
                                       scale=scale).then_inc(freed["act"], 1)
                return evacuate

            def copy_N(name, dst, func):
                def evacuate(i, par):
                    cs = i * (2 * UC) + par * UC
                    act.wait_ge(mm_done, ready(name, i, par, 0))
                    act.activation(dst[:, 0:LAT_TILES, bass.ds(cs, UC)],
                                   psum[:, 4 * par * BANK:(4 * par + 2) * BANK].rearrange("p (t c) -> p t c", c=UC),
                                   func).then_inc(freed["act"], 1)
                    act.wait_ge(mm_done, ready(name, i, par, 1))
                    act.activation(dst[:, LAT_TILES, bass.ds(cs, UC)], bank(4 * par + 2, UC), func).then_inc(freed["act"], 1)
                return evacuate

            dense("qk_r", copy_T("qk_r", qk_r, 0, 1.0))
            dense("v_r", copy_N("v_r", v_r, ACT.Copy))
            act.wait_ge(rope_done, 4)
            set_table(ACT.Silu)
            dense("g_r", copy_N("g_r", g_r, ACT.Silu))

            with act.Fori(0, RH) as h:
                act.wait_ge(rope_done, 4)
                act.wait_ge(r_s, h)
                act.activation(k_head[:, :], qk_r[:, bass.ds(h + RH, 1), :].rearrange("p a i -> p (a i)"), ACT.Copy).then_inc(r_k, 1)
                act.wait_ge(r_kT, h + 1)
                act.wait_ge(r_kv, h * 4)
                act.wait_ge(setup_v, SETUP_DVE)
                for n in range(2):
                    act.activation(k_fb[:, n, :, :].rearrange("p a b -> p (a b)"), psum[:, 0:TOK], ACT.Copy,
                                   scale=w_k[:, n, bass.ds(h, 1)]).then_inc(r_kfb, 1)
                act.wait_ge(r_kv, h * 4 + 4)
                act.wait_ge(r_ctx_out, h * 32)
                act.activation(kv_ctx[:, :], bank(5), ACT.Copy).then_inc(r_ctx, 1)
                act.wait_ge(r_ctx, h + 1)
                for n, dst in enumerate(("new_ret_fwd", "new_ret_bwd")):
                    act.dma_start(o[dst][0, 0, bass.ds(h, 1)].rearrange("h k v -> k (h v)"),
                                  kv_ctx[:, n * RDV:(n + 1) * RDV]).then_inc(r_ctx_out, 16)
                for p_, c in enumerate(OUT_ORDER):
                    act.wait_ge(r_out, h * TILES + (p_ + 1))
                    act.activation(y_nat[:, c, bass.ds(h * RDV, RDV)], bank(6 + p_ % 2, RDV), ACT.Copy).then_inc(r_y, 1)
            root("normy", RH * TILES)
            act.wait_ge(norm["normy"]["scaled"], 1)
            for h in range(RH):
                for t in range(TILES):
                    n, y = h * TILES + t, y_nat[:, t, h * RDV:(h + 1) * RDV]
                    act.activation(y, y, ACT.Identity, scale=rstd[:, n:n + 1], bias=rstd[:, 20 + n:21 + n]).then_inc(y_norm, 1)

            def gate(name, dst, col0, done, ada):
                def evacuate(i, par):
                    for j in range(2):
                        act.wait_ge(mm_done, ready(name, i, par, j))
                        if ada and j == 1:
                            copy_ada(name, i, par)
                        tile = i * 4 + (2 * par + j)
                        act.activation(one_tile(dst, tile), T_tile(4 * par + 2 * j), ACT.Sigmoid,
                                       bias=cols[:, bass.ds(tile + (ROW_BGATE + col0), 1)]).then_inc(freed["act"], 1)
                return evacuate

            set_table(ACT.Sigmoid)
            dense("gate_r", gate("gate_r", mixT, 0, None, False))
            act_to_T(act, "yg", yg_hi, gn_gain)
            dense("gate_d", gate("gate_d", gate_d, KT, None, True))
            dense("ret_out", lambda i, par: None)
            dense("q_d", copy_T("q_d", qk_d, 0, DHD ** -0.5))
            dense("k_d", copy_T("k_d", qk_d, DH, 1.0))
            act.wait_ge(rope_done, 12)

            dense("v_d", copy_N("v_d", v_d, ACT.Copy))
            act.wait_ge(r_ctx_out, RH * 32)
            act.wait_ge(k_ps, 1)
            act.activation(k_out[:, :], psum[:, 6 * BANK:8 * BANK], ACT.Copy).then_inc(at_oe, 2)

            def exp(h0, t0, m):
                h, t, n = tile_of(h0, t0)
                size = TOK if t < LAT_TILES else P
                if m == 0 and not (isinstance(h0, int) and h0 == 0 and t0 < 3):
                    pe_read = n - (1 if t < 2 else 2)
                    act.wait_ge(at_T, pe_read)
                act.wait_ge(at_max, n * 2 + (m + 1))
                act.activation(probs[:, PBUF[t], m, 0:size], psum[:, 2 * m * BANK:2 * m * BANK + size], ACT.Exp,
                               bias=sm[:, t, m:m + 1], accum_out=sm[:, t, 2 + m:3 + m]).then_inc(at_e, 1)

            def evacuate_T(h0, t0):
                h, t, n = tile_of(h0, t0)
                size = TOK if t < LAT_TILES else P
                act.wait_ge(at_T, n + 1)
                act.activation(aT[:, TBUF[t], :, :].rearrange("p a b -> p (a b)")[:, 0:size],
                               psum[:, 4 * BANK:4 * BANK + size], ACT.Copy).then_inc(at_aT, 1)

            def evacuate_o(h0, t0):
                h, t, n = tile_of(h0, t0)
                act.wait_ge(at_o, n + 1)
                if t == LAT_TILES:
                    act.wait_ge(k_stored, 16)
                act.wait_ge(at_oe, n + 2)
                act.activation(junk_o[:, :], bank(6 + t % 2, P), ACT.Square, accum_out=stats[:, bass.ds(n, 1)])
                act.activation(o_nat[:, t, bass.ds(h * P, P)], bank(6 + t % 2, P), ACT.Copy).then_inc(at_oe, 1)

            set_table(ACT.Exp)
            exp(0, 0, 0)
            exp(0, 0, 1)
            exp(0, 1, 0)
            exp(0, 1, 1)
            exp(0, 2, 0)
            evacuate_T(0, 0)
            exp(0, 2, 1)
            with act.Fori(0, DH - 1) as h:
                for t in range(2, TILES + 2):
                    exp(h, t + 1, 0)
                    evacuate_T(h, t - 1)
                    exp(h, t + 1, 1)
                    evacuate_o(h, t - 2)
            for t in range(2, TILES + 2):
                if t + 1 < TILES:
                    exp(DH - 1, t + 1, 0)
                if t - 1 < TILES:
                    evacuate_T(DH - 1, t - 1)
                if t + 1 < TILES:
                    exp(DH - 1, t + 1, 1)
                evacuate_o(DH - 1, t - 2)
            root("normo", DH * TILES)
            act.wait_ge(vd_stored, 16)
            for n in range(8):
                act.wait_ge(gb_ps, n + 1)
                act.activation(gate_row[:, n // 2, (n % 2) * BANK:(n % 2 + 1) * BANK], bank(n), ACT.Copy).then_inc(gb_row, 1)
            act.wait_ge(sub_ready, 1)
            act_to_T(act, "od", od_hi, subln_gain)

            def mix_hi_part(i, par):
                for j in range(2):
                    act.wait_ge(mix_sum, i * 4 + (2 * par + j + 1))
                    tile = i * 4 + (2 * par + j)
                    act.activation(one_tile(mix_hi, tile), one_tile(mixT, tile), ACT.Copy).then_inc(mix_h, 1)

            dense("diff_out", mix_hi_part)
            dense("w_o", lambda i, par: None)
            act.wait_ge(x1_done, 8)
            sums("norm2", x1, xn[:, 0, :])
            root("norm2", TILES)
            act_to_T_shifted(act, "h2", h2_hi, SHIFT2)

            def up(third):
                name = f"up{third}"
                base = sum(COUNT[f"up{n}"] for n in range(third))

                def evacuate(i, par):
                    for j in range(2):
                        if par == 0:
                            act.wait_ge(freed["dve"], i * 2 + START[name]["dve"])
                            act.wait_ge(mm_done, ready(name, i, 0, j))
                            act.activation(in_halves(silu_g[:, j, :]), T_tile(2 * j), ACT.Silu).then_inc(freed["act"], 1)
                        else:
                            act.wait_ge(freed["dve"], freed_after(name, i, 1, j))
                            tile = i * 2 + j
                            act.activation(hid_hi[:, bass.ds(tile, 1), :].rearrange("p a b -> p (a b)"),
                                           hid_f[:, j, :], ACT.Copy).then_inc(hid_h, 1)
                return evacuate

            set_table(ACT.Silu)
            for third in range(3):
                dense(f"up{third}", up(third))
                dense(f"down{third}", lambda i, par: None, peel=int(third == 2))
            act.wait_ge(x1_done, 32)
            sums("normf", x1, junk2)
            root("normf", TILES)

        @block.vector
        def _(dve):
            steps = [0]

            def link(ins):
                steps[0] += 1
                ins.then_inc(dve_step, 1)
                dve.wait_ge(dve_step, steps[0])

            flat = lambda x: x[:, :, :].rearrange("p a b -> p (a b)")

            def mean(which, n, scale, eps):
                dve.tensor_scalar(rstd[:, 0:n], stats[:, 0:n], scale, eps, ALU.mult, ALU.add).then_inc(norm[which]["mean"], 1)

            def inverse(which, n):
                dve.wait_ge(norm[which]["root"], 1)
                link(dve.reciprocal(rstd[:, 0:n], rstd[:, 0:n]))

            dve.memset(ones_col[:, :], 1.0).then_inc(ada_step, 16)
            dve.wait_ge(ld_scal, 6 * 16)
            link(dve.tensor_scalar(gam_c[:, :, :], lg[:, :, :], -1.0, None, ALU.mult))
            dve.tensor_tensor(gam_c[:, :, :], lg[:, :, :], gam_c[:, :, :], ALU.max).then_inc(setup_v, 1)
            link(dve.tensor_tensor(lam_mul[:, :, :], lam_in[:, 0:2, :], lam_in[:, 2:4, :], ALU.mult))
            link(dve.reduce_sum(lamv[:, 0:2], lam_mul[:, :, :], axis=AX.X))
            dve.wait_ge(norm["norm1"]["sums"], TILES)
            mean("norm1", TILES, 1.0 / D, RMS_EPS)
            inverse("norm1", TILES)
            for t in range(TILES):
                dve.tensor_scalar(x_nat[:, t, :], x_nat[:, t, :], rstd[:, t:t + 1], None, ALU.mult).then_inc(norm["norm1"]["scaled"], 1)
            y, u, t0, t1, log1p = flat(w_k), flat(gam_c), stats[:, 16:24], stats[:, 24:32], stats[:, 8:16]
            dve.wait_ge(setup_a, 1)
            dve.tensor_scalar(u, y, 1.0, None, ALU.add).then_inc(setup_v, 1)
            dve.wait_ge(setup_v, 2)
            link(dve.tensor_scalar(t0, u, -1.0, None, ALU.add))
            link(dve.tensor_tensor(t0, y, t0, ALU.subtract))
            link(dve.reciprocal(t1, u))
            link(dve.tensor_tensor(t0, t0, t1, ALU.mult))
            dve.wait_ge(setup_a, 2)
            link(dve.tensor_tensor(log1p, log1p, t0, ALU.add))
            link(dve.tensor_scalar(flat(lg), flat(lg), 0.0, None, ALU.min))
            dve.tensor_tensor(flat(lg), flat(lg), log1p, ALU.subtract).then_inc(setup_v, 2)
            dve.wait_ge(setup_v, 4)
            dve.wait_ge(ld_tab, 3 * 16)
            for n in range(2):
                last = dve.tensor_scalar(w_k[:, n, :], lg[:, n, :], pos_col[:, n:n + 1], None, ALU.mult)
            last.then_inc(setup_v, 1)
            for h in range(RH):
                last = dve.tensor_scalar(decay[:, h, :], dist[:, 0, :], lg[:, 0, h:h + 1], None, ALU.mult)
            link(last)
            for h in range(RH):
                last = dve.scalar_tensor_tensor(decay[:, h, :], dist[:, 1, :], lg[:, 1, h:h + 1], decay[:, h, :], ALU.mult, ALU.add)
            last.then_inc(setup_v, 1)
            dve.wait_ge(setup_a, 3)
            link(dve.tensor_tensor(lamv[:, 2:3], lamv[:, 1:2], lamv[:, 0:1], ALU.subtract))
            link(dve.tensor_scalar(lamv[:, 2:3], lamv[:, 2:3], -LAM_INIT, None, ALU.add))
            dve.wait_ge(setup_a, 6)
            dve.tensor_scalar(w_k[:, :, :], w_k[:, :, :], P ** -0.5, None, ALU.mult).then_inc(setup_v, 1)
            dve.tensor_scalar(decay[:, :, :], decay[:, :, :], P ** -0.5, None, ALU.mult).then_inc(setup_v, 1)

            dve_split(dve, 0, 0)

            dve.wait_ge(cols_ready, 1)
            dve.wait_ge(ada_cols, 2)
            for n, m in enumerate((SHIFT1, SCALE1)):
                last = dve.tensor_tensor(mod[:, m:m + KT, :], bank(7, 2 * KT, 2 * m).rearrange("p (m s) -> p m s", s=2),
                                         cols[:, ROW_BADA + m:ROW_BADA + m + KT].unsqueeze(2).to_broadcast([P, KT, 2]), ALU.add)
                last.then_inc(freed["dve"], 1)
            dve.wait_ge(freed["dve"], 2)

            dve.tensor_scalar(sub_gain[:, :], cols[:, ROW_SUBLN:ROW_SUBLN + 1], 1.0 - LAM_INIT, None, ALU.mult).then_inc(sub_ready, 1)

            def scales(which, m, gain):
                dve.wait_ge(dve_step, steps[0])
                (dve.scalar_tensor_tensor(sc[:, :, :], mod[:, m:m + KT, :], 1.0,
                                              cols[:, gain:gain + KT].unsqueeze(2).to_broadcast([P, KT, 2]), ALU.add, ALU.mult)
                 .then_inc(n2t[which]["scale"], 1))

            scales("h", SCALE1, ROW_G1)
            dve_to_T_shifted(dve, "h", h_hi, h_lo, SHIFT1)

            def ada_partial(name, i, par):
                u = ADA_FIRST[name] + par
                for k in range(KT):
                    if k % (KT // 2) == 0:
                        dve.wait_ge(ada_b_in[2 * k // KT], i * 32 + 16 * (u + 1))
                    for c in range(2):
                        acc, w, x = ada_acc[:, par, c, :], ada_b[2 * k // KT][:, k % (KT // 2), :], silu_c[:, k, c:c + 1]
                        if k == 0:
                            last = dve.tensor_scalar(acc, w, x, None, ALU.mult)
                        else:
                            dve.wait_ge(ada_step, i * 32 + (16 + 16 * u + 2 * k + c - 1))
                            last = dve.scalar_tensor_tensor(acc, w, x, acc, ALU.mult, ALU.add)
                        last.then_inc(ada_step, 1)

            def dense(name, evacuate, peel=0):
                def pair(i, last):
                    for par in range(2):
                        if not (last and par == 1):
                            dve_split(dve, unit_of(name, i, par) + 1, 1 - par)
                        if name in ADA_FIRST:
                            ada_partial(name, i, par)
                        evacuate(i, par)

                with dve.Fori(0, COUNT[name] // 2 - peel) as i:
                    pair(i, False)
                if peel:
                    pair(COUNT[name] // 2 - 1, True)

            def rotate(name, qk, first, tile0, swaps, before):
                def evacuate(i, par):
                    x = qk[:, bass.ds(i * 4 + (tile0 + 2 * par), 2), 0:LAT]
                    dve.wait_ge(freed["act"], freed_after(name, i, par, 1))
                    dve.wait_ge(rope_done, i * 2 + (first + par))
                    dve.tensor_tensor(rope_tmp[:, :, :], x, rope[:, 0:1, :].to_broadcast([P, 2, LAT]), ALU.mult).then_inc(rope_mul, 1)
                    dve.wait_ge(rope_in, i * (32 * swaps) + (before + 16 * swaps * (par + 1)))
                    dve.tensor_tensor(swapped[:, :, :], swapped[:, :, :], rope[:, 1:2, :].to_broadcast([P, 2, LAT]), ALU.mult).then_inc(rope_mul, 1)
                    dve.wait_ge(rope_mul, i * 4 + (2 * (first + par) + 2))
                    dve.tensor_tensor(x, rope_tmp[:, :, :], swapped[:, :, :], ALU.add).then_inc(rope_done, 1)
                return evacuate

            nothing = lambda i, par: None
            dve.wait_ge(ld_rope, 16)
            dense("qk_r", rotate("qk_r", qk_r, 0, 0, 2, 0))
            dense("v_r", nothing)
            dense("g_r", nothing)

            with dve.Fori(0, RH) as h:
                dve.wait_ge(r_s, h + 1)
                dve.wait_ge(r_out, h * TILES)
                dve.tensor_tensor(s_dec[:, :, :], psum[:, 2 * BANK:2 * BANK + TOK].rearrange("p (c i) -> p c i", i=P),
                                  decay[:, bass.ds(h, 1), :].to_broadcast([P, TILES, P]), ALU.mult).then_inc(r_dec, 1)
                dve.wait_ge(r_s0, h * 32 + 32)
                for s in range(3):
                    dve.wait_ge(r_kv, h * 4 + (s + 1))
                    dve.wait_ge(r_state, h * 3 + s)
                    for n, (c_to, c_from) in enumerate(((s + 1, s), (2 - s, 3 - s))):
                        last = dve.scalar_tensor_tensor(state[:, n, c_to, :], state[:, n, c_from, :], gam_c[:, n, bass.ds(h, 1)],
                                                        bank(4 + s % 2, RDV, n * RDV), ALU.mult, ALU.add)
                    last.then_inc(r_state, 1)
                for p_, c in enumerate(OUT_ORDER):
                    dve.wait_ge(r_y, h * TILES + (p_ + 1))
                    dve.bn_stats(bn6[:, bass.ds(h * TILES + c, 1), :].rearrange("p a b -> p (a b)"),
                                 y_nat[:, c, bass.ds(h * RDV, RDV)]).then_inc(r_bn, 1)
            dve.wait_ge(r_bn, RH * TILES)
            for n in range(RH * TILES):
                last = dve.bn_aggr(mean_var[:, n, :], bn6[:, n, :])
            last.then_inc(r_mv, 1)
            n = RH * TILES
            dve.wait_ge(r_mv, 1)
            dve.tensor_scalar(rstd[:, 0:n], mean_var[:, :, 1], GN_EPS, None, ALU.add).then_inc(norm["normy"]["mean"], 1)
            inverse("normy", n)
            dve.scalar_tensor_tensor(rstd[:, n:2 * n], mean_var[:, :, 0], -1.0, rstd[:, 0:n], ALU.mult, ALU.mult).then_inc(norm["normy"]["scaled"], 1)
            for h in range(RH):
                hs = slice(h * RDV, (h + 1) * RDV)
                dve.wait_ge(y_norm, (h + 1) * TILES)
                dve.tensor_tensor(y_nat[:, :, hs], y_nat[:, :, hs], g_r[:, :, hs], ALU.mult).then_inc(y_gated, 1)

            dense("gate_r", nothing)
            dve_to_T(dve, "yg", yg_hi, yg_lo, gn_gain)
            dve.wait_ge(r_y, RH * TILES)
            dense("gate_d", nothing)

            def gated_ret(i, par):
                for j in range(2):
                    dve.wait_ge(mm_done, ready("ret_out", i, par, j))
                    if j == 1:
                        dve.tensor_copy(mod[:, bass.ds(i * 4 + (GATE1 + 2 * (ADA_FIRST["ret_out"] + par)), 2), :],
                                        bank(4 * par + 3, 4, HALF).rearrange("p (m s) -> p m s", s=2))
                    x = one_tile(mixT, i * 4 + (2 * par + j))
                    dve.tensor_tensor(x, T_tile(4 * par + 2 * j), x, ALU.mult).then_inc(freed["dve"], 1)

            dense("ret_out", gated_ret)
            dve.wait_ge(ld_rope, 32)
            dense("q_d", rotate("q_d", qk_d, 4, 0, 4, 128))
            dense("k_d", rotate("k_d", qk_d, 8, DH, 4, 128 + 256))
            dve.wait_ge(freed["act"], START["v_d"]["act"])
            dve.wait_ge(freed["dve"], START["diff_out"]["dve"])
            link(dve.tensor_tensor(mod[:, GATE1:, :], mod[:, GATE1:, :],
                                   cols[:, ROW_BADA + GATE1:ROW_BADA + 48].unsqueeze(2).to_broadcast([P, 32, 2]), ALU.add))
            scales("h2", SCALE2, ROW_G2)
            dense("v_d", nothing)

            def maximum(h0, t0, m):
                h, t, n = tile_of(h0, t0)
                size = TOK if t < LAT_TILES else P
                dve.wait_ge(at_s, n * 2 + (m + 1))
                dve.reduce_max(sm[:, t, m:m + 1], psum[:, 2 * m * BANK:2 * m * BANK + size], axis=AX.X,
                               negate=True).then_inc(at_max, 1)

            def weights(h0, t0, part):
                h, t, n = tile_of(h0, t0)
                size = TOK if t < LAT_TILES else P
                p0, p1 = probs[:, PBUF[t], 0, 0:size], probs[:, PBUF[t], 1, 0:size]
                if part == 0:
                    dve.wait_ge(at_e, n * 2 + 2)
                    dve.reciprocal(sm[:, t, 4:6], sm[:, t, 2:4]).then_inc(at_r, 1)
                    dve.wait_ge(at_r, n + 1)
                    dve.tensor_scalar(p1, p1, sm[:, t, 5:6], lamv[:, 2:3], ALU.mult, ALU.mult).then_inc(at_a1, 1)
                else:
                    dve.wait_ge(at_a1, n + 1)
                    dve.scalar_tensor_tensor(p0, p0, sm[:, t, 4:5], p1, ALU.mult, ALU.add).then_inc(at_a, 1)

            maximum(0, 0, 0)
            maximum(0, 0, 1)
            maximum(0, 1, 0)
            weights(0, 0, 0)
            maximum(0, 1, 1)
            weights(0, 0, 1)
            maximum(0, 2, 0)
            weights(0, 1, 0)
            maximum(0, 2, 1)
            weights(0, 1, 1)
            with dve.Fori(0, DH - 1) as h:
                for t in range(2, TILES + 2):
                    maximum(h, t + 1, 0)
                    weights(h, t, 0)
                    maximum(h, t + 1, 1)
                    weights(h, t, 1)
            for t in range(2, TILES):
                if t + 1 < TILES:
                    maximum(DH - 1, t + 1, 0)
                weights(DH - 1, t, 0)
                if t + 1 < TILES:
                    maximum(DH - 1, t + 1, 1)
                weights(DH - 1, t, 1)

            dve.wait_ge(at_T, DH * TILES)
            dve.memset(ones[:, :], 1.0).then_inc(ones_set, 1)
            dve.wait_ge(at_oe, 2 + DH * TILES)
            mean("normo", DH * TILES, 1.0 / P, RMS_EPS)
            for n in range(8):
                m = (GATE1 if n < 4 else GATE2) + 4 * (n % 2)
                if n >= 2:
                    dve.wait_ge(gb_ps, n - 1)
                dve.tensor_tensor(diag[:, n % 2, :, :], ident[:, :].unsqueeze(1).to_broadcast([P, 4, P]),
                                  mod[:, m:m + 4, (n // 2) % 2:(n // 2) % 2 + 1].to_broadcast([P, 4, P]), ALU.mult).then_inc(gb_diag, 1)
            inverse("normo", DH * TILES)
            r = rstd[:, :].rearrange("p (h t) -> p h t", t=TILES)
            for t in range(TILES):
                x = o_nat[:, t, :].rearrange("p (h e) -> p h e", e=P)
                dve.tensor_tensor(x, x, r[:, :, t:t + 1].to_broadcast([P, DH, P]), ALU.mult).then_inc(norm["normo"]["scaled"], 1)
            dve_to_T(dve, "od", od_hi, od_lo, subln_gain)

            def mixed(i, par):
                for j in range(2):
                    tile = i * 4 + (2 * par + j)
                    g, x = one_tile(gate_d, tile), one_tile(mixT, tile)
                    dve.wait_ge(mm_done, ready("diff_out", i, par, j))
                    dve.tensor_tensor(g, T_tile(4 * par + 2 * j), g, ALU.mult).then_inc(freed["dve"], 1)
                    dve.wait_ge(freed["dve"], freed_after("diff_out", i, par, j))
                    dve.tensor_tensor(x, x, g, ALU.add).then_inc(mix_sum, 1)
                for j in range(2):
                    tile = i * 4 + (2 * par + j)
                    dve.wait_ge(mix_h, i * 4 + (2 * par + j + 1))
                    dve.tensor_tensor(one_tile(mix_lo, tile), one_tile(mixT, tile), one_tile(mix_hi, tile).bitcast(F32),
                                      ALU.subtract).then_inc(mix_l, 1)

            dense("diff_out", mixed)

            def residual(name, g, done0):
                def evacuate(i, par):
                    cs = bass.ds(i * (2 * UC) + par * UC, UC)
                    for j in range(2):
                        dve.wait_ge(mm_done, ready(name, i, par, j))
                        nt = LAT_TILES if j == 0 else 1
                        src = bank(4 * par + 2 * j, nt * UC).rearrange("p (t c) -> p t c", c=UC) if j else \
                            psum[:, 4 * par * BANK:(4 * par + 2) * BANK].rearrange("p (t c) -> p t c", c=UC)
                        row = gate_row[:, 2 * g + j:2 * g + j + 1, cs].to_broadcast([P, nt, UC])
                        x = x1[:, 0:LAT_TILES, cs] if j == 0 else x1[:, LAT_TILES:TILES, cs]
                        dve.wait_ge(x1_done, i * 4 + (done0 + 2 * par + j))
                        dve.tensor_tensor(gated[:, 0:nt, :], src, row, ALU.mult).then_inc(freed["dve"], 1)
                        dve.wait_ge(freed["dve"], freed_after(name, i, par, j))
                        dve.tensor_tensor(x, x, gated[:, 0:nt, :], ALU.add).then_inc(x1_done, 1)
                return evacuate

            dve.wait_ge(ld_x1, 32)
            dense("w_o", residual("w_o", 0, 0))
            dve.wait_ge(norm["norm2"]["sums"], TILES)
            mean("norm2", TILES, 1.0 / D, RMS_EPS)
            inverse("norm2", TILES)
            for t in range(TILES):
                dve.tensor_scalar(xn[:, t, :], x1[:, t, :], rstd[:, t:t + 1], None, ALU.mult).then_inc(norm["norm2"]["scaled"], 1)
            dve_to_T_shifted(dve, "h2", h2_hi, h2_lo, SHIFT2)

            def hidden(third):
                name = f"up{third}"
                base = sum(COUNT[f"up{n}"] for n in range(third))

                def evacuate(i, par):
                    if par == 0:
                        return
                    for j in range(2):
                        dve.wait_ge(mm_done, ready(name, i, 1, j))
                        dve.wait_ge(freed["act"], freed_after(name, i, 0, j))
                        dve.wait_ge(hid_l, i * 2 + base)
                        dve.tensor_tensor(in_halves(hid_f[:, j, :]), T_tile(4 + 2 * j), in_halves(silu_g[:, j, :]),
                                          ALU.mult).then_inc(freed["dve"], 1)
                    for j in range(2):
                        tile = i * 2 + j
                        dve.wait_ge(hid_h, i * 2 + (base + j + 1))
                        dve.tensor_tensor(hid_lo[:, bass.ds(tile, 1), :].rearrange("p a b -> p (a b)"), hid_f[:, j, :],
                                          hid_hi[:, bass.ds(tile, 1), :].rearrange("p a b -> p (a b)").bitcast(F32),
                                          ALU.subtract).then_inc(hid_l, 1)
                return evacuate

            for third in range(3):
                dense(f"up{third}", hidden(third))
                dense(f"down{third}", residual(f"down{third}", 1, 8 * (third + 1)), peel=int(third == 2))
            dve.wait_ge(norm["normf"]["sums"], TILES)
            mean("normf", TILES, 1.0 / D, RMS_EPS)
            inverse("normf", TILES)
            dve.wait_ge(ld_fin, 16)
            for t in range(TILES):
                dve.scalar_tensor_tensor(x1[:, t, :], x1[:, t, :], rstd[:, t:t + 1], fin_g[:, :], ALU.mult, ALU.mult).then_inc(y_done, 1)


def shape_constants():
    f = np.float32
    pos_r, pos_c = np.repeat(np.arange(LAT // GRID_W), GRID_W), np.tile(np.arange(GRID_W), LAT // GRID_W)

    def rotary(d):
        n = d // 4
        inv = (10000.0 ** (-np.arange(n) / n)).astype(f)
        ang = np.concatenate([pos_r[:, None].astype(f) * inv, pos_c[:, None].astype(f) * inv], axis=-1)
        cos, sin = np.cos(ang.astype(np.float64)).T, np.sin(ang.astype(np.float64)).T
        cos, sin = np.concatenate([cos, cos]), np.concatenate([-sin, sin])
        return np.stack([np.tile(cos, (P // d, 1)), np.tile(sin, (P // d, 1))]).astype(f)

    i = np.arange(P)
    gap = (i[None, :] - i[:, None]).astype(f)
    return {"const_ident": np.eye(P, dtype=f), "const_rope_ret": rotary(P), "const_rope_diff": rotary(DHD),
            "const_dist": np.stack([np.maximum(gap, 0), np.maximum(-gap, 0)]).astype(f),
            "const_row_pos": np.stack([i + 1, P - i]).astype(f),
            "const_pos_col": np.stack([P - 1 - i, i], axis=1).astype(f)}


OUTPUTS = (("y_prompt", (1, P, D)), ("y_sample", (1, LAT, D)), ("new_ret_fwd", (1, 1, RH, P, RDV)),
           ("new_ret_bwd", (1, 1, RH, P, RDV)), ("new_diff_k", (1, 1, P, DH, 2, DHD)),
           ("new_diff_v", (1, 1, P, DH, 2 * DHD)))


def kernel(**inputs):
    import concourse.bacc as bacc
    from concourse.bass_utils import run_bass_kernel_spmd

    nc = bacc.Bacc("TRN2", target_bir_lowering=False, num_devices=1)
    arrays, a, o = {}, {}, {}
    for name, x in {**inputs, **shape_constants()}.items():
        x = np.ascontiguousarray(x)
        arrays["in_" + name] = x
        a[name] = nc.dram_tensor("in_" + name, x.shape, F32, kind="ExternalInput").ap()
    for name, shape in OUTPUTS:
        o[name] = nc.dram_tensor("out_" + name, shape, F32, kind="ExternalOutput").ap()
    build(nc, a, o)
    r = run_bass_kernel_spmd(nc, [arrays], core_ids=[0])
    return tuple(r.results[0]["out_" + name] for name, _ in OUTPUTS)
```

```python
from contextlib import ExitStack

import numpy as np

import concourse.bass as bass
from concourse import mybir

F32 = mybir.dt.float32
F32R = mybir.dt.float32r
ACT = mybir.ActivationFunctionType
ALU = mybir.AluOpType
AX = mybir.AxisListType

P = 128
D = 1024
KT = D // P
LAT_TILES = 4
TILES = 5
LAT = LAT_TILES * P
TOK = TILES * P
HALF = TOK // 2
UC = 256
BANK = 512
RH = 4
RDV = 256
DH = 8
DHD = 64
FFN = 2816
GRID_W = 64
LAM_INIT = 0.2
RMS_EPS = 1e-6
GN_EPS = 1e-5
KB = 1024

ROW_BADA, ROW_G1, ROW_G2, ROW_BGATE, ROW_C, ROW_CCTX, ROW_GN, ROW_SUBLN = 0, 48, 56, 64, 80, 88, 96, 104
ROWS = 105

PHASES = [("qk_r", 4, "act", "act"), ("v_r", 4, "act", "act"), ("g_r", 4, "act", "act"),
          ("gate_r", 4, "act", "act"), ("gate_d", 4, "act", "act"), ("ret_out", 4, "dve", "dve"),
          ("q_d", 4, "act", "act"), ("k_d", 4, "act", "act"), ("v_d", 4, "act", "act"),
          ("diff_out", 4, "dve", "dve"), ("w_o", 4, "dve", "dve"),
          ("up0", 8, "act", "dve"), ("down0", 4, "dve", "dve"), ("up1", 8, "act", "dve"),
          ("down1", 4, "dve", "dve"), ("up2", 6, "act", "dve"), ("down2", 4, "dve", "dve")]


def lay_out_phases():
    first, count, reader, before, start = {}, {}, {}, {}, {}
    unit, total = 0, {"act": 2, "dve": 2}
    last = [("act", 2), ("dve", 2)]
    for name, n, *readers in PHASES:
        first[name], count[name], reader[name] = unit, n, readers
        before[name] = list(last)
        start[name] = dict(total)
        same = readers[0] == readers[1]
        for s in range(2):
            last[s] = (readers[s], total[readers[s]] + (2 * n - 2 + 2 * s if same else n))
        for e in set(readers):
            total[e] += 2 * n if same else n
        unit += n
    return first, count, reader, before, start


FIRST, COUNT, READER, BEFORE, START = lay_out_phases()
ADA_FIRST = {"gate_r": 0, "gate_d": 4, "ret_out": 8, "v_d": 12}
AHEAD = 1
SETUP_ACT, SETUP_DVE = 14, 8
SHIFT1, SCALE1, GATE1, SHIFT2, SCALE2, GATE2 = (KT * n for n in range(6))
SHIFTED = ("h", "h2")
PBUF = (0, 1, 2, 0, 1)
TBUF = (0, 1, 0, 1, 2)
OUT_ORDER = (4, 1, 2, 0, 3)


def freed_after(name, i, par, j):
    r = READER[name]
    if r[0] == r[1]:
        return i * 4 + (START[name][r[0]] + 2 * par + j + 1)
    return i * 2 + (START[name][r[par]] + j + 1)


def unit_of(name, i, par):
    return i * 2 + (FIRST[name] + par)


def ready(name, i, par, j):
    return i * 4 + (2 * FIRST[name] + 2 * par + j + 1 + AHEAD)


def tile_of(h, t):
    return h + t // TILES, t % TILES, h * TILES + t


def build(nc, a, o):
    with ExitStack() as ctx:
        arena_bytes = 205 * KB + 512
        ctx.enter_context(nc.sbuf_tensor("arena", [P, arena_bytes // 4], F32))
        origin = nc.sbuf_base - arena_bytes

        def at(name, kb, shape, dt=F32):
            return nc.alloc_sbuf_tensor_at(name, shape, dt, offset=origin + int(kb * KB))

        def small(name, shape, dt=F32):
            return ctx.enter_context(nc.sbuf_tensor(name, shape, dt))

        def sem(name):
            return ctx.enter_context(nc.semaphore(name))

        H, W, A, B, Y, M, S = 0, 40, 88, 128, 148, 168, 188
        h_hi = at("h_hi", H, [P, KT, TOK], F32R)
        h_lo = at("h_lo", H + 20, [P, KT, TOK], F32R)
        mod_rows = at("mod_rows", H + 24, [2, 2 * D])
        o_nat = at("o_nat", H, [P, TILES, D])
        k_out = at("k_out", H + 16, [P, D])
        probs = at("probs", H + 20, [P, 3, 2, TOK])
        qz = at("qz", H + 35, [P, TILES, 2, P])
        diag = at("diag", H + 20, [P, 8, 4, P])
        ones = at("ones", H + 36, [P, P])
        mix_hi = at("mix_hi", H, [P, KT, TOK], F32R)
        mix_lo = at("mix_lo", H + 20, [P, KT, TOK], F32R)
        h2_hi = at("h2_hi", H, [P, KT, TOK], F32R)
        h2_lo = at("h2_lo", H + 20, [P, KT, TOK], F32R)
        w_raw = [at(f"w_raw{s}", W + 8 * s, [P, KT, UC]) for s in range(2)]
        w_hi = [at(f"w_hi{s}", W + 16 + 8 * s, [P, KT, UC], F32R) for s in range(2)]
        w_lo = [at(f"w_lo{s}", W + 32 + 8 * s, [P, KT, UC], F32R) for s in range(2)]
        x_nat = at("x_nat", A, [P, TILES, D])
        rows = at("rows", A + 20, [P, P])
        k_cache = at("k_cache", A + 21, [P, D])
        junk = at("junk", A + 25, [P, D])
        dist = at("dist", A + 29, [P, 2, P])
        row_pos = at("row_pos", A + 30, [P, 2, P])
        lam_in = at("lam_in", A + 31, [P, 4, DHD])
        lam_mul = at("lam_mul", A + 32, [P, 2, DHD])
        qk_r = at("qk_r", A, [P, 2 * RH, TOK])
        v_r = at("v_r", A + 20, [P, TILES, D])
        yg_hi = at("yg_hi", A, [P, KT, TOK], F32R)
        yg_lo = at("yg_lo", A + 20, [P, KT, TOK], F32R)
        qk_d = at("qk_d", A, [P, 2 * DH, TOK])
        od_hi = at("od_hi", A, [P, KT, TOK], F32R)
        od_lo = at("od_lo", A + 20, [P, KT, TOK], F32R)
        hid_hi = at("hid_hi", A, [P, KT, TOK], F32R)
        hid_lo = at("hid_lo", A + 20, [P, KT, TOK], F32R)
        rope = at("rope", B, [P, 2, LAT])
        swapped = at("swapped", B + 4, [P, 2, LAT])
        rope_tmp = at("rope_tmp", B + 8, [P, 2, LAT])
        g_r = at("g_r", B, [P, TILES, D])
        v_d = at("v_d", B, [P, TILES, D])
        gate_row = at("gate_row", B, [P, 4, D])
        fin_g = at("fin_g", B + 16, [P, D])
        ada_a = [at(f"ada_a{s}", Y + 8 * s if s < 5 else H + 8 * (s - 5), [P, KT, UC]) for s in range(8)]
        y_nat = at("y_nat", Y, [P, TILES, D])
        gate_d = at("gate_d", Y, [P, KT, TOK])
        x1 = at("x1", Y, [P, TILES, D])
        k_fb = at("k_fb", M, [P, 2, TILES, P])
        q_fb = at("q_fb", M + 5, [P, 2, LAT_TILES, P])
        state = at("state", M + 9, [P, 2, LAT_TILES, RDV])
        s_ends = at("s_ends", M + 17, [P, 2, RDV])
        mixT = at("mixT", M, [P, KT, TOK])
        diag_r = at("diag_r", M, [P, TILES, P])
        silu_g = at("silu_g", M, [P, 2, TOK])
        hid_f = at("hid_f", M + 5, [P, 2, TOK])
        gated = at("gated", M + 10, [P, 4, UC])
        junk2 = at("junk2", M + 16, [P, D])
        kc_T = at("kc_T", S, [P, DH, P])
        decay = at("decay", S + 4, [P, RH, P])
        w_q = at("w_q", S + 6, [P, 2, RH, P])
        v_cache = at("v_cache", S + 4, [P, D])
        hf = at("hf", S + 10, [P, 3, TOK])
        ada_b = [at(f"ada_b{s}", S + 4 + 4 * s, [P, KT // 2, UC]) for s in range(2)]
        ada_acc = at("ada_acc", S + 12, [P, 2, 2, UC])
        k_head = at("k_head", S + 10, [P, TOK])
        s_dec = at("s_dec", S + 12.5, [P, TILES, P])
        kv_ctx = at("kv_ctx", S + 15, [P, 2 * RDV])
        bn6 = at("bn6", S + 17, [P, RH * TILES, 6])
        junk_o = at("junk_o", S + 8, [P, P])
        aT = at("aT", S + 10, [P, 3, TILES, P])
        ident = small("ident", [P, P])
        cols = small("cols", [P, ROWS])
        mod = small("mod", [P, 48, 2])
        silu_c = small("silu_c", [P, KT, 2])
        sc = small("sc", [P, KT, 2])
        stats = small("stats", [P, 40])
        rstd = small("rstd", [P, 40])
        pos_col = small("pos_col", [P, 2])
        w_k = small("w_k", [P, 2, RH])
        lg = small("lg", [P, 2, RH])
        gam_c = small("gam_c", [P, 2, RH])
        lamv = small("lamv", [P, 3])
        sm = small("sm", [P, TILES, 7])
        prime = small("prime", [P, 16])
        sub_gain = small("sub_gain", [P, 1])
        spare = small("spare", [P, 3])
        ones_col = small("ones_col", [P, 1])
        mean_var = stats[:, :].rearrange("p (n c) -> p n c", c=2)

        psum = ctx.enter_context(nc.psum_tensor("psum", [P, 8 * BANK], F32))

        def bank(b, n=BANK, at_=0):
            return psum[:, b * BANK + at_:b * BANK + at_ + n]

        def T_tile(b):
            return psum[:, b * BANK:(b + 2) * BANK].rearrange("p (b c) -> p b c", b=2)[:, :, 0:HALF]

        def in_halves(x):
            return x.rearrange("p (b c) -> p b c", b=2)

        def one_tile(x, n):
            return x[:, bass.ds(n, 1), :].rearrange("p a (b c) -> p (a b) c", b=2)

        w_landed = [sem(f"w_landed{s}") for s in range(2)]
        w_hi_done, w_lo_done = sem("w_hi_done"), sem("w_lo_done")
        mm_done = sem("mm_done")
        freed = {"act": sem("freed_act"), "dve": sem("freed_dve")}
        ld_ident, ld_rows, ld_x, ld_kc = sem("ld_ident"), sem("ld_rows"), sem("ld_x"), sem("ld_kc")
        ld_tab, ld_rope, ld_scal, ld_vc = sem("ld_tab"), sem("ld_rope"), sem("ld_scal"), sem("ld_vc")
        ld_x1, ld_fin = sem("ld_x1"), sem("ld_fin")
        ada_a_in = [sem(f"ada_a_in{s}") for s in range(8)]
        ada_b_in = [sem(f"ada_b_in{s}") for s in range(2)]
        r_ctx_out, vd_stored, k_stored, stored = sem("r_ctx_out"), sem("vd_stored"), sem("k_stored"), sem("stored")
        rows_T = sem("rows_T")
        cols_ready = sem("cols_ready")
        kc_ps, kc_done = sem("kc_ps"), sem("kc_done")
        setup_a, setup_v = sem("setup_a"), sem("setup_v")
        dve_step = sem("dve_step")
        sub_ready = sem("sub_ready")
        ada_row_ps, ada_row, ada_cols = sem("ada_row_ps"), sem("ada_row"), sem("ada_cols")
        ada_pre = sem("ada_pre")
        ada_step = sem("ada_step")
        norm = {n: {q: sem(f"{n}_{q}") for q in ("sums", "mean", "root", "scaled")}
                for n in ("norm1", "normy", "normo", "norm2", "normf")}
        n2t = {n: {q: sem(f"{n}_{q}") for q in ("ps", "f", "f2", "hi", "lo", "scale")} for n in ("h", "yg", "od", "h2")}
        rope_in, rope_mul = sem("rope_in"), sem("rope_mul")
        rope_done = sem("rope_done")
        r_k, r_kT, r_kfb, r_s, r_dec = sem("r_k"), sem("r_kT"), sem("r_kfb"), sem("r_s"), sem("r_dec")
        r_q, r_s0, r_kv, r_ends, r_state = sem("r_q"), sem("r_s0"), sem("r_kv"), sem("r_ends"), sem("r_state")
        r_ctx, r_out, r_y, r_bn, r_mv = sem("r_ctx"), sem("r_out"), sem("r_y"), sem("r_bn"), sem("r_mv")
        y_norm, y_gated = sem("y_norm"), sem("y_gated")
        k_ps = sem("k_ps")
        at_z, at_qz, at_s, at_max, at_e = sem("at_z"), sem("at_qz"), sem("at_s"), sem("at_max"), sem("at_e")
        at_r, at_f, at_a, at_T, at_aT, at_o = (sem(n) for n in ("at_r", "at_f", "at_a", "at_T", "at_aT", "at_o"))
        at_oe = sem("at_oe")
        ones_set, gb_diag, gb_ps, gb_row = sem("ones_set"), sem("gb_diag"), sem("gb_ps"), sem("gb_row")
        mix_sum, mix_h, mix_l = sem("mix_sum"), sem("mix_h"), sem("mix_l")
        x1_done = sem("x1_done")
        hid_h, hid_l = sem("hid_h"), sem("hid_l")
        y_done = sem("y_done")

        def act_split(act, unit, s):
            act.wait_ge(w_landed[s], (unit - s) * 8 + 16)
            act.wait_ge(mm_done, unit * 2 - 2 + AHEAD)
            act.activation(w_hi[s][:, :, :], w_raw[s][:, :, :], ACT.Copy).then_inc(w_hi_done, 1)

        def dve_split(dve, unit, s):
            dve.wait_ge(w_hi_done, unit + 1)
            dve.tensor_tensor(w_lo[s][:, :, :], w_raw[s][:, :, :], w_hi[s][:, :, :].bitcast(F32),
                              ALU.subtract).then_inc(w_lo_done, 1)

        def pe_wait_unit(pe, name, i, par):
            r, val = BEFORE[name][par]
            pe.wait_ge(freed[r], val)
            per_pair = 4 if READER[name][0] == READER[name][1] else 2
            pe.wait_ge(freed[READER[name][par]], freed_after(name, i, par, 1) - per_pair)
            pe.wait_ge(w_lo_done, unit_of(name, i, par) + 1)

        def sums_over_partitions(pe, slot, out):
            for m in range(2):
                for c in range(2):
                    last = pe.matmul(out[:, 2 * m + c:2 * m + c + 1], ada_acc[:, slot, c, m * P:(m + 1) * P],
                                     ones_col[:, :], start=True, stop=True)
            return last

        def pe_ada_sums(pe, name, i, par):
            pe.wait_ge(ada_step, i * 32 + (16 * (ADA_FIRST[name] + par) + 32))
            return sums_over_partitions(pe, par, bank(4 * par + 3, 4, HALF))

        def pe_T_unit(pe, name, i, par, hi, lo, split=None):
            for j in range(2):
                cs = slice(j * P, (j + 1) * P)
                for k in range(KT):
                    if split and par == 0 and j == 0:
                        pe.wait_ge(split[0], split[1] + k + 1)
                    for n, (w, x) in enumerate(((w_lo[par], hi), (w_hi[par], lo), (w_hi[par], hi))):
                        for h in range(2):
                            last = pe.matmul(bank(4 * par + 2 * j + h, HALF), w[:, k, cs],
                                             x[:, k, h * HALF:(h + 1) * HALF],
                                             start=(k == 0 and n == 0), stop=(k == KT - 1 and n == 2))
                if name in ADA_FIRST and j == 1:
                    last = pe_ada_sums(pe, name, i, par)
                last.then_inc(mm_done, 1)

        def pe_N_unit(pe, name, i, par, hi, lo, kt=KT, split=None):
            for t in range(TILES):
                ts = slice(t * P, (t + 1) * P)
                for k in range(kt):
                    if split and par == 0 and t == 0:
                        pe.wait_ge(split[0], split[1] + k + 1)
                    for n, (w, x) in enumerate(((w_lo[par], hi), (w_hi[par], lo), (w_hi[par], hi))):
                        last = pe.matmul(bank(4 * par + t // 2, UC, (t % 2) * UC), x[:, k, ts], w[:, k, :],
                                         start=(k == 0 and n == 0), stop=(k == kt - 1 and n == 2))
                if name in ADA_FIRST and t == LAT_TILES:
                    last = pe_ada_sums(pe, name, i, par)
                if t >= LAT_TILES - 1:
                    last.then_inc(mm_done, 1)

        def pe_dense(pe, name, unit, hi, lo, **kw):
            with pe.Fori(0, COUNT[name] // 2) as i:
                for par in range(2):
                    pe_wait_unit(pe, name, i, par)
                    unit(pe, name, i, par, hi, lo, **kw)

        def pe_to_T(pe, which, src, diagonals=None):
            q = n2t[which]
            readers = (q["f"], q["f2"]) if which in SHIFTED else (q["lo"],)

            def wait_read(k):
                for r in readers:
                    pe.wait_ge(r, k + 1)

            for k in range(KT):
                if k >= 4:
                    wait_read(k - 4)
                b = 2 * (k % 4)
                for t in range(TILES):
                    out, x = bank(b + t // 4, P, (t % 4) * P), src[:, t, k * P:(k + 1) * P]
                    last = pe.matmul(out, x, diagonals[:, t, :], start=True, stop=True) if diagonals is not None else \
                        pe.transpose(out, x, ident[:, :])
                last.then_inc(q["ps"], 1)
            wait_read(5 if which == "yg" else 4)

        def in_pair(k):
            return psum[:, 2 * (k % 4) * BANK:2 * (k % 4) * BANK + TOK]

        def modulated(which, shift, k, c, cs):
            return hf[:, k % 3, cs], in_pair(k)[:, cs], sc[:, k, c:c + 1], mod[:, shift + k, c:c + 1]

        def act_to_T_shifted(act, which, hi, shift):
            q = n2t[which]

            def modulate(k):
                act.wait_ge(q["ps"], k + 1)
                if k >= 3:
                    act.wait_ge(q["lo"], k - 2)
                out, x, scale, bias = modulated(which, shift, k, 1, slice(LAT, TOK))
                act.activation(out, x, ACT.Identity, scale=scale, bias=bias).then_inc(q["f"], 1)

            act.wait_ge(q["scale"], 1)
            modulate(0)
            for k in range(KT):
                if k + 1 < KT:
                    modulate(k + 1)
                act.wait_ge(q["f"], k + 1)
                act.wait_ge(q["f2"], k + 1)
                act.activation(hi[:, k, :], hf[:, k % 3, :], ACT.Copy).then_inc(q["hi"], 1)

        def dve_to_T_shifted(dve, which, hi, lo, shift):
            q = n2t[which]
            dve.wait_ge(q["scale"], 1)
            for k in range(KT + 2):
                if k < KT:
                    dve.wait_ge(q["ps"], k + 1)
                    if k >= 3:
                        dve.wait_ge(q["lo"], k - 2)
                    out, x, scale, bias = modulated(which, shift, k, 0, slice(0, LAT))
                    dve.tensor_scalar(out, x, scale, bias, ALU.mult, ALU.add).then_inc(q["f2"], 1)
                if k >= 2:
                    dve.wait_ge(q["hi"], k - 1)
                    dve.tensor_tensor(lo[:, k - 2, :], hf[:, (k - 2) % 3, :], hi[:, k - 2, :].bitcast(F32),
                                      ALU.subtract).then_inc(q["lo"], 1)

        def act_to_T(act, which, hi, scale):
            q = n2t[which]
            for k in range(KT):
                act.wait_ge(q["ps"], k + 1)
                act.activation(hi[:, k, :], in_pair(k), ACT.Copy, scale=scale(k)).then_inc(q["hi"], 1)

        def dve_to_T(dve, which, hi, lo, scale):
            q = n2t[which]
            for k in range(KT):
                dve.wait_ge(q["hi"], k + 1)
                dve.scalar_tensor_tensor(lo[:, k, :], in_pair(k), scale(k), hi[:, k, :].bitcast(F32),
                                         ALU.mult, ALU.subtract).then_inc(q["lo"], 1)

        def gn_gain(k):
            return cols[:, ROW_GN + k:ROW_GN + k + 1]

        def subln_gain(k):
            return sub_gain[:, :]

        packed = ((ROW_C, a["c"][0]), (ROW_CCTX, a["c_ctx"]), (ROW_BADA, a["b_ada"][0]), (ROW_G1, a["norm1_g"][0]),
                  (ROW_G2, a["norm2_g"][0]), (ROW_BGATE, a["b_gate"][0]), (ROW_GN, a["ret_gn_g"][0]),
                  (ROW_SUBLN, a["diff_subln_g"][0]))

        def load_rows(engine, vectors):
            for row, vec in vectors:
                n = vec.shape[0] // P
                engine.dma_start(rows[row:row + n, :], vec.rearrange("(r c) -> r c", c=P)).then_inc(ld_rows, 16)

        block = ctx.enter_context(nc.Block())

        @block.sync
        def _(sp):
            w_in = a["w_in"][0].rearrange("(k p) c -> p k c", p=P)
            ada = a["w_ada"][0].rearrange("(k p) c -> p k c", p=P)
            load_rows(sp, packed[:4])
            sp.dma_start(x_nat[:, 0:LAT_TILES, :], a["x_sample"][0].rearrange("(t p) c -> p t c", p=P)).then_inc(ld_x, 16)
            sp.dma_start(x_nat[:, LAT_TILES, :], a["x_prompt"][0]).then_inc(ld_x, 16)
            sp.dma_start(dist[:, :, :], a["const_dist"].rearrange("a p t -> p a t")).then_inc(ld_tab, 16)
            sp.dma_start(row_pos[:, :, :], a["const_row_pos"].partition_broadcast(P)).then_inc(ld_tab, 16)
            sp.dma_start(pos_col[:, :], a["const_pos_col"]).then_inc(ld_tab, 16)
            sp.dma_start(k_cache[:, :], a["cache_diff_k"][0, 0].rearrange("p h m d -> p (h m d)")).then_inc(ld_kc, 16)
            for n in (0, 1, 6, 2, 7, 3, 4, 5):
                sp.dma_start(ada_a[n][:, :, :], ada[:, :, n * UC:(n + 1) * UC]).then_inc(ada_a_in[n], 16)
                if n == 4:
                    sp.dma_start(w_raw[0][:, :, :], w_in[:, :, 0:UC]).then_inc(w_landed[0], 16)
            sp.dma_start(w_raw[1][:, :, :], w_in[:, :, UC:2 * UC]).then_inc(w_landed[1], 16)
            for s in range(2):
                sp.wait_ge(w_lo_done, s + 1)
                sp.dma_start(w_raw[s][:, :, :], w_in[:, :, (2 + s) * UC:(3 + s) * UC]).then_inc(w_landed[s], 16)

            def stream(name, sources):
                with sp.Fori(0, COUNT[name] // 2) as i:
                    for s, (view, col, stride, kt) in enumerate(sources):
                        c = sp.snap(i * stride + col)
                        sp.wait_ge(w_lo_done, unit_of(name, i, s) - 1)
                        sp.dma_start(w_raw[s][:, 0:kt, :], view[:, 0:kt, bass.ds(c, UC)]).then_inc(w_landed[s], 16)

            def columns(view, col, kt=KT):
                return [(view, col, 2 * UC, kt), (view, col + UC, 2 * UC, kt)]

            by_tile = {n: a[n][0].rearrange("(k p) c -> p k c", p=P)
                       for n in ("w_ret_out", "w_diff_out", "w_o", "w_ffn_gate", "w_ffn_up", "w_ffn_down")}
            stream("v_r", columns(w_in, 1024))
            stream("g_r", columns(w_in, 2048))
            stream("gate_r", columns(w_in, 6144))
            stream("gate_d", columns(w_in, 7168))
            stream("ret_out", columns(by_tile["w_ret_out"], 0))
            stream("q_d", columns(w_in, 3072))
            stream("k_d", columns(w_in, 4096))
            stream("v_d", columns(w_in, 5120))
            stream("diff_out", columns(by_tile["w_diff_out"], 0))
            stream("w_o", columns(by_tile["w_o"], 0))
            for third in range(3):
                c0, kt = third * D, min(KT, FFN // P - third * KT)
                stream(f"up{third}", [(by_tile["w_ffn_gate"], c0, UC, KT), (by_tile["w_ffn_up"], c0, UC, KT)])
                stream(f"down{third}", columns(by_tile["w_ffn_down"][:, third * KT:third * KT + kt, :], 0, kt))
            for t in range(TILES):
                sp.wait_ge(y_done, t + 1)
                dst = o["y_prompt"][0] if t == LAT_TILES else o["y_sample"][0, t * P:(t + 1) * P, :]
                sp.dma_start(dst, x1[:, t, :]).then_inc(stored, 16)
            sp.wait_ge(stored, TILES * 16)
            sp.wait_ge(vd_stored, 16)
            sp.wait_ge(k_stored, 16)
            sp.wait_ge(r_ctx_out, RH * 32)

        @block.gpsimd
        def _(pool):
            pool.dma_start(ident[:, :], a["const_ident"]).then_inc(ld_ident, 16)
            for n, w in enumerate(("ret_decay_fwd", "ret_decay_bwd")):
                pool.dma_start(lg[:, n, :], a[w][0].partition_broadcast(P)).then_inc(ld_scal, 16)
            for n, w in enumerate(("q1", "q2", "k1", "k2")):
                pool.dma_start(lam_in[:, n, :], a["diff_lambda_" + w][0].partition_broadcast(P)).then_inc(ld_scal, 16)
            pool.dma_start(rope[:, :, :], a["const_rope_ret"].rearrange("a p t -> p a t")).then_inc(ld_rope, 16)

            ada = a["w_ada"][0].rearrange("(k p) c -> p k c", p=P)

            def load_ada(name, i, par):
                u = ADA_FIRST[name] + par
                c = i * (2 * UC) + (2 * D + u * UC)
                if not isinstance(i, int):
                    c = pool.snap(c)
                for r in range(2):
                    pool.wait_ge(ada_step, i * 32 + (16 * u + 8 * r + 8))
                    pool.dma_start(ada_b[r][:, :, :],
                                   ada[:, r * KT // 2:(r + 1) * KT // 2, bass.ds(c, UC)]).then_inc(ada_b_in[r], 16)

            def swap_halves(name, qk, size, first, tile0, i, par):
                pool.wait_ge(freed["act"], freed_after(name, i, par, 1))
                pool.wait_ge(rope_done, i * 2 + (first + par + AHEAD))
                tile = i * 4 + (tile0 + 2 * par)
                for r in range(0, P, size):
                    f = r + size if (r // size) % 2 == 0 else r - size
                    pool.dma_start(swapped[r:r + size, :, :], qk[f:f + size, bass.ds(tile, 2), 0:LAT]).then_inc(rope_in, 16)

            with pool.Fori(0, 2) as i:
                for par in range(2):
                    swap_halves("qk_r", qk_r, P // 2, 0, 0, i, par)

            pool.wait_ge(rope_done, 4 + AHEAD)
            pool.wait_ge(setup_a, SETUP_ACT)

            def load_ends(h):
                for n, src in enumerate(("state_ret_fwd", "state_ret_bwd")):
                    pool.dma_start(s_ends[:, n, :], a[src][0, 0, bass.ds(h, 1)].rearrange("h k v -> k (h v)")).then_inc(r_s0, 16)

            def weigh_queries(h):
                q = qk_r[:, bass.ds(h, 1), 0:LAT].rearrange("p a (c i) -> p (a c) i", i=P)
                for n in range(2):
                    w = w_q[:, n, bass.ds(h, 1), :].to_broadcast([P, LAT_TILES, P])
                    pool.tensor_tensor(q_fb[:, n, :, :], q, w, ALU.mult).then_inc(r_q, 1)

            def place_ends():
                for n, c in enumerate((0, LAT_TILES - 1)):
                    pool.tensor_copy(state[:, n, c, :], s_ends[:, n, :]).then_inc(r_ends, 1)

            load_ends(0)
            weigh_queries(0)
            pool.wait_ge(r_s0, 32)
            place_ends()
            with pool.Fori(0, RH - 1) as h:
                pool.wait_ge(r_ends, h * 2 + 2)
                pool.wait_ge(r_state, h * 3 + 1)
                load_ends(h + 1)
                pool.wait_ge(r_s0, h * 32 + 64)
                pool.wait_ge(r_out, h * TILES + TILES)
                weigh_queries(h + 1)
                place_ends()

            pool.wait_ge(r_out, RH * TILES)
            for name in ("gate_r", "gate_d", "ret_out"):
                with pool.Fori(0, 2) as i:
                    for par in range(2):
                        load_ada(name, i, par)
            pool.wait_ge(y_gated, RH)
            pool.dma_start(rope[:, :, :], a["const_rope_diff"].rearrange("a p t -> p a t")).then_inc(ld_rope, 16)
            load_ada("v_d", 0, 0)
            for name, first, tile0 in (("q_d", 4, 0), ("k_d", 8, DH)):
                with pool.Fori(0, 2) as i:
                    for par in range(2):
                        swap_halves(name, qk_d, P // 4, first, tile0, i, par)
            for i, par in ((0, 1), (1, 0), (1, 1)):
                load_ada("v_d", i, par)
            pool.wait_ge(ada_step, 16 * 17)
            pool.dma_start(v_cache[:, :], a["cache_diff_v"][0, 0].rearrange("p h e -> p (h e)")).then_inc(ld_vc, 16)

            pool.wait_ge(freed["act"], START["diff_out"]["act"])
            pool.dma_start(o["new_diff_v"][0, 0].rearrange("p h e -> p (h e)"), v_d[:, LAT_TILES, :]).then_inc(vd_stored, 16)
            pool.memset(qz[:, :, :, :], 0.0).then_inc(at_z, 1)
            pool.wait_ge(at_z, 1)

            def fill_qz(t, src):
                for m in range(2):
                    r = slice(m * DHD, (m + 1) * DHD)
                    pool.tensor_copy(qz[r, t, m, :], src(r)).then_inc(at_qz, 1)

            for t in range(TILES):
                fill_qz(t, lambda r: qk_d[r, 0, t * P:(t + 1) * P])
            pool.wait_ge(at_oe, 2)
            pool.dma_start(o["new_diff_k"][0, 0].rearrange("p h m d -> p (h m d)"), k_out[:, :]).then_inc(k_stored, 16)
            with pool.Fori(1, DH) as h:
                for t in range(TILES):
                    pool.wait_ge(at_s, h * (2 * TILES) + (2 * t + 2 - 2 * TILES))
                    fill_qz(t, lambda r: qk_d[r, bass.ds(h, 1), t * P:(t + 1) * P])

            pool.wait_ge(at_T, DH * TILES)
            pool.memset(ones[:, :], 1.0).then_inc(ones_set, 1)
            for n in range(8):
                m = (GATE1 if n < 4 else GATE2) + 4 * (n % 2)
                pool.tensor_tensor(diag[:, n, :, :], ident[:, :].unsqueeze(1).to_broadcast([P, 4, P]),
                                  mod[:, m:m + 4, (n // 2) % 2:(n // 2) % 2 + 1].to_broadcast([P, 4, P]), ALU.mult).then_inc(gb_diag, 1)
            pool.wait_ge(mix_sum, KT)
            pool.dma_start(x1[:, 0:LAT_TILES, :], a["x_sample"][0].rearrange("(t p) c -> p t c", p=P)).then_inc(ld_x1, 16)
            pool.dma_start(x1[:, LAT_TILES, :], a["x_prompt"][0]).then_inc(ld_x1, 16)
            pool.dma_start(fin_g[:, :], a["final_norm_g"].partition_broadcast(P)).then_inc(ld_fin, 16)

        @block.tensor
        def _(pe):
            pe.wait_ge(ld_ident, 16)
            pe.wait_ge(ld_rows, 8 * 16)
            pe.transpose(bank(6, ROWS), rows[0:ROWS, :], ident[0:ROWS, 0:ROWS]).then_inc(rows_T, 1)
            pe.wait_ge(ld_kc, 16)
            for h in range(DH):
                last = pe.transpose(bank(4 + h // 4, P, (h % 4) * P), k_cache[:, h * P:(h + 1) * P], ident[:, :])
                if h == 0:
                    last.then_inc(mm_done, AHEAD)
            last.then_inc(kc_ps, 1)

            def mod_columns(group, start, stop):
                pe.wait_ge(ada_row, group)
                for m in range(start, stop):
                    last = pe.transpose(bank(7, 2, 2 * m), mod_rows[0:2, m * P:(m + 1) * P], ident[0:2, 0:2])
                last.then_inc(ada_cols, 1)

            pe.wait_ge(freed["act"], 2)
            for n in range(6):
                if n == 5:
                    mod_columns(1, 0, 8)
                    pe.wait_ge(ada_pre, 32)
                    for m in range(2):
                        sums_over_partitions(pe, m, bank(7, 4, 2 * (12 + 2 * m)))
                pe.wait_ge(ada_a_in[n], 16)
                for k in range(KT):
                    last = pe.matmul(psum[0:2, n * UC:(n + 1) * UC], silu_c[:, k, :], ada_a[n][:, k, :],
                                     start=(k == 0), stop=(k == KT - 1))
                last.then_inc(ada_row_ps, 1)
            mod_columns(2, 8, 12)

            pe.wait_ge(norm["norm1"]["scaled"], TILES)
            pe.wait_ge(kc_done, 1)
            pe.wait_ge(freed["dve"], 2)
            pe_to_T(pe, "h", x_nat)
            pe_dense(pe, "qk_r", pe_T_unit, h_hi, h_lo, split=(n2t["h"]["lo"], 0))
            pe_dense(pe, "v_r", pe_N_unit, h_hi, h_lo)
            pe_dense(pe, "g_r", pe_N_unit, h_hi, h_lo)

            def chunk(c):
                return slice(c * P, (c + 1) * P)

            def keys_and_scores(h):
                pe.wait_ge(r_k, h + 1)
                for c in range(TILES):
                    last = pe.transpose(bank(c // 4, P, (c % 4) * P), k_head[:, chunk(c)], ident[:, :])
                last.then_inc(r_kT, 1)
                for c in range(TILES):
                    q = qk_r[:, bass.ds(h, 1), chunk(c)].rearrange("p a i -> p (a i)")
                    last = pe.matmul(bank(2 + c // 4, P, (c % 4) * P), k_head[:, chunk(c)], q, start=True, stop=True)
                last.then_inc(r_s, 1)

            def states_and_outputs(h, next_too):
                def v_chunk(c):
                    return v_r[:, c, bass.ds(h * RDV, RDV)]

                pe.wait_ge(r_kfb, h * 2 + 2)
                for s in range(4):
                    f, b = (s, 3 - s) if s < 3 else (4, 4)
                    if s >= 2:
                        pe.wait_ge(r_state, h * 3 + (s - 1))
                    pe.matmul(bank(4 + s % 2, RDV), k_fb[:, 0, f, :], v_chunk(f), start=True, stop=True)
                    pe.matmul(bank(4 + s % 2, RDV, RDV), k_fb[:, 1, b, :], v_chunk(b), start=True, stop=True).then_inc(r_kv, 1)
                pe.wait_ge(r_dec, h + 1)
                if next_too:
                    keys_and_scores(h + 1)
                pe.wait_ge(r_q, h * 2 + 2)
                for p_, c in enumerate(OUT_ORDER):
                    pe.wait_ge(r_y, h * TILES + (AHEAD + max(0, p_ - 1)))
                    out = bank(6 + p_ % 2, RDV)
                    if c < LAT_TILES:
                        pe.wait_ge(r_state, h * 3 + (2 if c in (1, 2) else 3))
                        if c in (0, LAT_TILES - 1):
                            pe.wait_ge(r_ends, h * 2 + 2)
                        pe.matmul(out, q_fb[:, 0, c, :], state[:, 0, c, :], start=True, stop=False)
                        pe.matmul(out, q_fb[:, 1, c, :], state[:, 1, c, :], start=False, stop=False)
                    pe.matmul(out, s_dec[:, c, :], v_chunk(c), start=(c == LAT_TILES), stop=True).then_inc(r_out, 1)

            pe.wait_ge(freed["act"], START["gate_r"]["act"])
            pe.wait_ge(rope_done, 4 + AHEAD)
            keys_and_scores(0)
            with pe.Fori(0, RH - 1) as h:
                states_and_outputs(h, True)
            states_and_outputs(RH - 1, False)
            pe.wait_ge(r_y, AHEAD + RH * TILES)
            pe.wait_ge(r_state, RH * 3)
            pe.wait_ge(r_ctx, RH)

            pe_dense(pe, "gate_r", pe_T_unit, h_hi, h_lo)
            pe.wait_ge(freed["act"], START["gate_d"]["act"])
            pe.wait_ge(y_gated, RH)
            pe_to_T(pe, "yg", y_nat)
            pe_dense(pe, "gate_d", pe_T_unit, h_hi, h_lo)
            pe_dense(pe, "ret_out", pe_T_unit, yg_hi, yg_lo, split=(n2t["yg"]["lo"], 0))
            pe_dense(pe, "q_d", pe_T_unit, h_hi, h_lo)
            pe_dense(pe, "k_d", pe_T_unit, h_hi, h_lo)
            pe_dense(pe, "v_d", pe_N_unit, h_hi, h_lo)

            pe.wait_ge(freed["act"], START["diff_out"]["act"])
            pe.wait_ge(rope_done, 12 + AHEAD)
            for h in range(DH):
                last = pe.transpose(bank(6 + h // 4, P, (h % 4) * P), qk_d[:, DH + h, LAT:TOK], ident[:, :])
            last.then_inc(k_ps, 1)
            pe.wait_ge(ld_vc, 16)
            pe.wait_ge(kc_done, 1)

            def scores(h0, t0, m, first=False):
                h, t, n = tile_of(h0, t0)
                pe.wait_ge(at_qz, n * 2 + (m + 1))
                if not first:
                    pe.wait_ge(at_e, n * 2 + (m - 1))
                if t < LAT_TILES:
                    k = qk_d[:, bass.ds(h + DH, 1), 0:LAT].rearrange("p a i -> p (a i)")
                    pe.matmul(bank(2 * m), qz[:, t, m, :], k, start=True, stop=True)
                    k = kc_T[:, bass.ds(h, 1), :].rearrange("p a i -> p (a i)")
                    last = pe.matmul(bank(2 * m + 1, P), qz[:, t, m, :], k, start=True, stop=True)
                else:
                    k = qk_d[:, bass.ds(h + DH, 1), LAT:TOK].rearrange("p a i -> p (a i)")
                    last = pe.matmul(bank(2 * m, P), qz[:, t, m, :], k, start=True, stop=True)
                last.then_inc(at_s, 1)

            def weights_T(h0, t0, first=False):
                h, t, n = tile_of(h0, t0)
                pe.wait_ge(at_a, n + 1)
                if not first:
                    pe.wait_ge(at_aT, n)
                for c in range(TILES if t < LAT_TILES else 1):
                    last = pe.transpose(bank(4 + c // 4, P, (c % 4) * P), probs[:, PBUF[t], 0, c * P:(c + 1) * P], ident[:, :])
                last.then_inc(at_T, 1)

            def outputs(h0, t0):
                h, t, n = tile_of(h0, t0)
                pe.wait_ge(at_aT, n + 1)
                pe.wait_ge(at_oe, n + (2 if t == 0 else 1))
                out = bank(6 + t % 2, P)
                for c in range(TILES if t < LAT_TILES else 1):
                    if t == LAT_TILES:
                        val = v_d[:, LAT_TILES, bass.ds(h * P, P)]
                    else:
                        val = v_d[:, c, bass.ds(h * P, P)] if c < LAT_TILES else v_cache[:, bass.ds(h * P, P)]
                    last = pe.matmul(out, aT[:, TBUF[t], c, :], val, start=(c == 0),
                                     stop=(c == LAT_TILES or t == LAT_TILES))
                last.then_inc(at_o, 1)

            scores(0, 0, 0, first=True)
            scores(0, 0, 1, first=True)
            scores(0, 1, 0)
            scores(0, 1, 1)
            scores(0, 2, 0)
            weights_T(0, 0, first=True)
            scores(0, 2, 1)
            with pe.Fori(0, DH - 1) as h:
                for t in range(2, TILES + 2):
                    scores(h, t + 1, 0)
                    weights_T(h, t - 1)
                    scores(h, t + 1, 1)
                    outputs(h, t - 2)
            for t in range(2, TILES + 2):
                if t + 1 < TILES:
                    scores(DH - 1, t + 1, 0)
                if t - 1 < TILES:
                    weights_T(DH - 1, t - 1)
                if t + 1 < TILES:
                    scores(DH - 1, t + 1, 1)
                outputs(DH - 1, t - 2)

            pe.wait_ge(at_oe, 2 + DH * TILES)
            pe.wait_ge(ones_set, 1)
            for n in range(8):
                pe.wait_ge(gb_diag, n + 1)
                pe.matmul(bank(n), ones[:, :], diag[:, n, :, :].rearrange("p a b -> p (a b)"),
                          start=True, stop=True).then_inc(gb_ps, 1)
            pe.wait_ge(norm["normo"]["scaled"], TILES)
            pe.wait_ge(gb_row, 8)
            pe_to_T(pe, "od", o_nat)
            pe_dense(pe, "diff_out", pe_T_unit, od_hi, od_lo, split=(n2t["od"]["lo"], 0))
            pe_dense(pe, "w_o", pe_N_unit, mix_hi, mix_lo, split=(mix_l, 0))
            pe.wait_ge(freed["dve"], START["up0"]["dve"])
            pe.wait_ge(norm["norm2"]["scaled"], TILES)
            pe_to_T(pe, "h2", x1, diag_r)
            tiles = 0
            for third in range(3):
                pe_dense(pe, f"up{third}", pe_T_unit, h2_hi, h2_lo, split=(n2t["h2"]["lo"], 0))
                kt = COUNT[f"up{third}"]
                pe_dense(pe, f"down{third}", pe_N_unit, hid_hi, hid_lo, kt=kt, split=(hid_l, tiles + AHEAD))
                tiles += kt

        @block.scalar
        def _(act):
            load_rows(act, packed[4:])
            primes = iter(range(16))

            def set_table(func, **kw):
                n = next(primes)
                return act.activation(prime[:, n:n + 1], ident[:, 0:1], func, **kw)

            act.wait_ge(rows_T, 1)
            act.activation(cols[:, :], bank(6, ROWS), ACT.Copy).then_inc(cols_ready, 1)
            for n, row in enumerate((ROW_C, ROW_CCTX)):
                act.activation(silu_c[:, :, n], bank(6, KT, row), ACT.Silu).then_inc(freed["act"], 1)

            def sums(which, src, waste):
                for t in range(TILES):
                    if t:
                        act.wait_ge(norm[which]["sums"], t)
                    act.activation(waste[:, :], src[:, t, :], ACT.Square, accum_out=stats[:, t:t + 1]).then_inc(norm[which]["sums"], 1)

            def block_sums(which, done0):
                def evacuate(i, par):
                    for t in range(TILES):
                        if t in (0, LAT_TILES):
                            act.wait_ge(x1_done, i * 4 + (done0 + 2 * par + (1 if t == 0 else 2) + AHEAD))
                        act.wait_ge(norm[which]["sums"], i * (2 * TILES) + (par * TILES + t + AHEAD))
                        act.activation(junk2[:, 0:UC], x1[:, t, bass.ds(i * (2 * UC) + par * UC, UC)], ACT.Square,
                                       accum_out=stats[:, bass.ds(i * 2 + (t * 4 + par), 1)]).then_inc(norm[which]["sums"], 1)
                return evacuate

            def root(which, n):
                act.wait_ge(norm[which]["mean"], 1)
                act.activation(rstd[:, 0:n], rstd[:, 0:n], ACT.Sqrt).then_inc(norm[which]["root"], 1)

            act.wait_ge(ld_x, 32)
            sums("norm1", x_nat, junk)
            root("norm1", TILES)

            act.wait_ge(kc_ps, 1)
            act.activation(kc_T[:, :, :].rearrange("p a b -> p (a b)"), psum[:, 4 * BANK:6 * BANK], ACT.Copy).then_inc(kc_done, 1)

            act.wait_ge(setup_v, 1)
            act.activation(w_k[:, :, :], gam_c[:, :, :], ACT.Exp, scale=-1.0).then_inc(setup_a, 1)
            act.wait_ge(setup_v, 2)
            act.activation(stats[:, 8:16], gam_c[:, :, :].rearrange("p a b -> p (a b)"), ACT.Ln).then_inc(setup_a, 1)
            act.wait_ge(setup_v, 4)
            act.activation(lamv[:, 0:2], lamv[:, 0:2], ACT.Exp).then_inc(setup_a, 1)
            act.activation(gam_c[:, :, :], lg[:, :, :], ACT.Exp, scale=float(P)).then_inc(setup_a, 1)
            act.wait_ge(setup_v, 6)
            act.activation(w_k[:, :, :], w_k[:, :, :], ACT.Exp).then_inc(setup_a, 1)
            act.activation(decay[:, :, :], decay[:, :, :], ACT.Exp).then_inc(setup_a, 1)
            for n in range(2):
                for h in range(RH):
                    act.activation(w_q[:, n, h, :], row_pos[:, n, :], ACT.Exp, scale=lg[:, n, h:h + 1]).then_inc(setup_a, 1)

            def evacuate_rows(u, v):
                act.wait_ge(ada_row_ps, v)
                act.activation(mod_rows[:, u * UC:v * UC], psum[0:2, u * UC:v * UC], ACT.Copy).then_inc(ada_row, 1)

            evacuate_rows(0, 4)
            act.wait_ge(w_landed[0], 16)
            act.activation(w_hi[0][:, :, :], w_raw[0][:, :, :], ACT.Copy).then_inc(w_hi_done, 1)
            evacuate_rows(4, 6)
            act_to_T_shifted(act, "h", h_hi, SHIFT1)

            def dense(name, evacuate, peel=0):
                def pair(i, last):
                    for par in range(2):
                        if not (last and par == 1):
                            act_split(act, unit_of(name, i, par) + 1, 1 - par)
                        evacuate(i, par)

                with act.Fori(0, COUNT[name] // 2 - peel) as i:
                    pair(i, False)
                if peel:
                    set_table(ACT.Sqrt)
                    pair(COUNT[name] // 2 - 1, True)

            def copy_ada(name, i, par):
                act.activation(mod[:, bass.ds(i * 4 + (GATE1 + 2 * (ADA_FIRST[name] + par)), 2), :],
                               bank(4 * par + 3, 4, HALF).rearrange("p (m s) -> p m s", s=2), ACT.Copy)

            def copy_T(name, dst, tile0, scale):
                def evacuate(i, par):
                    for j in range(2):
                        act.wait_ge(mm_done, ready(name, i, par, j))
                        act.activation(one_tile(dst, i * 4 + (tile0 + 2 * par + j)), T_tile(4 * par + 2 * j), ACT.Copy,
                                       scale=scale).then_inc(freed["act"], 1)
                return evacuate

            def copy_N(name, dst, func, after=0):
                def evacuate(i, par):
                    cs = i * (2 * UC) + par * UC
                    if after:
                        act.wait_ge(rope_done, after + AHEAD)
                    act.wait_ge(mm_done, ready(name, i, par, 0))
                    act.activation(dst[:, 0:LAT_TILES, bass.ds(cs, UC)],
                                   psum[:, 4 * par * BANK:(4 * par + 2) * BANK].rearrange("p (t c) -> p t c", c=UC),
                                   func).then_inc(freed["act"], 1)
                    act.wait_ge(mm_done, ready(name, i, par, 1))
                    if name in ADA_FIRST:
                        copy_ada(name, i, par)
                    act.activation(dst[:, LAT_TILES, bass.ds(cs, UC)], bank(4 * par + 2, UC), func).then_inc(freed["act"], 1)
                return evacuate

            dense("qk_r", copy_T("qk_r", qk_r, 0, 1.0))
            dense("v_r", copy_N("v_r", v_r, ACT.Copy))
            set_table(ACT.Silu)
            dense("g_r", copy_N("g_r", g_r, ACT.Silu, after=4))

            def copy_keys(h):
                act.activation(k_head[:, :], qk_r[:, bass.ds(h + RH, 1), :].rearrange("p a i -> p (a i)"), ACT.Copy).then_inc(r_k, 1)

            def weigh_keys(h):
                act.wait_ge(r_kT, h + 1)
                for n in range(2):
                    act.activation(k_fb[:, n, :, :].rearrange("p a b -> p (a b)"), psum[:, 0:TOK], ACT.Copy,
                                   scale=w_k[:, n, bass.ds(h, 1)]).then_inc(r_kfb, 1)

            def store_and_evacuate(h, next_too):
                if next_too:
                    act.wait_ge(r_s, h + 1)
                    copy_keys(h + 1)
                act.wait_ge(r_kv, h * 4 + 4)
                act.activation(kv_ctx[:, :], bank(5), ACT.Copy).then_inc(r_ctx, 1)
                if next_too:
                    weigh_keys(h + 1)
                act.wait_ge(r_ctx, h + 1)
                for n, dst in enumerate(("new_ret_fwd", "new_ret_bwd")):
                    act.dma_start(o[dst][0, 0, bass.ds(h, 1)].rearrange("h k v -> k (h v)"),
                                  kv_ctx[:, n * RDV:(n + 1) * RDV]).then_inc(r_ctx_out, 16)
                for p_, c in enumerate(OUT_ORDER):
                    act.wait_ge(r_out, h * TILES + (p_ + 1))
                    act.activation(y_nat[:, c, bass.ds(h * RDV, RDV)], bank(6 + p_ % 2, RDV), ACT.Copy).then_inc(r_y, 1)
                act.wait_ge(r_ctx_out, h * 32 + 32)

            set_table(ACT.Copy).then_inc(r_y, AHEAD)
            act.wait_ge(setup_v, SETUP_DVE)
            copy_keys(0)
            weigh_keys(0)
            with act.Fori(0, RH - 1) as h:
                store_and_evacuate(h, True)
            store_and_evacuate(RH - 1, False)
            root("normy", RH * TILES)
            act.wait_ge(norm["normy"]["scaled"], 1)

            def normalize_head(h):
                for t in range(TILES):
                    n, y = h * TILES + t, y_nat[:, t, bass.ds(h * RDV, RDV)]
                    act.activation(y, y, ACT.Identity, scale=rstd[:, bass.ds(n, 1)],
                                   bias=rstd[:, bass.ds(n + RH * TILES, 1)]).then_inc(y_norm, 1)

            def gate(name, dst, col0):
                def evacuate(i, par):
                    if name == "gate_r":
                        normalize_head(i * 2 + par)
                    for j in range(2):
                        act.wait_ge(mm_done, ready(name, i, par, j))
                        if j == 1:
                            copy_ada(name, i, par)
                        tile = i * 4 + (2 * par + j)
                        act.activation(one_tile(dst, tile), T_tile(4 * par + 2 * j), ACT.Sigmoid,
                                       bias=cols[:, bass.ds(tile + (ROW_BGATE + col0), 1)]).then_inc(freed["act"], 1)
                return evacuate

            set_table(ACT.Sigmoid)
            dense("gate_r", gate("gate_r", mixT, 0))
            act_to_T(act, "yg", yg_hi, gn_gain)
            dense("gate_d", gate("gate_d", gate_d, KT))
            dense("ret_out", lambda i, par: None)
            dense("q_d", copy_T("q_d", qk_d, 0, DHD ** -0.5))
            dense("k_d", copy_T("k_d", qk_d, DH, 1.0))
            dense("v_d", copy_N("v_d", v_d, ACT.Copy, after=12))
            act.wait_ge(r_ctx_out, RH * 32)
            act.wait_ge(k_ps, 1)
            act.activation(k_out[:, :], psum[:, 6 * BANK:8 * BANK], ACT.Copy).then_inc(at_oe, 2)

            def exp(h0, t0, m):
                h, t, n = tile_of(h0, t0)
                size = TOK if t < LAT_TILES else P
                if m == 0 and not (isinstance(h0, int) and h0 == 0 and t0 < 3):
                    pe_read = n - (1 if t < 2 else 2)
                    act.wait_ge(at_T, pe_read)
                act.wait_ge(at_max, n * 2 + (m + 1))
                act.activation(probs[:, PBUF[t], m, 0:size], psum[:, 2 * m * BANK:2 * m * BANK + size], ACT.Exp,
                               bias=sm[:, t, m:m + 1], accum_out=sm[:, t, 2 + m:3 + m]).then_inc(at_e, 1)

            def evacuate_T(h0, t0):
                h, t, n = tile_of(h0, t0)
                size = TOK if t < LAT_TILES else P
                act.wait_ge(at_T, n + 1)
                act.activation(aT[:, TBUF[t], :, :].rearrange("p a b -> p (a b)")[:, 0:size],
                               psum[:, 4 * BANK:4 * BANK + size], ACT.Copy).then_inc(at_aT, 1)

            def evacuate_o(h0, t0):
                h, t, n = tile_of(h0, t0)
                act.wait_ge(at_o, n + 1)
                if t == LAT_TILES:
                    act.wait_ge(k_stored, 16)
                act.wait_ge(at_oe, n + 2)
                act.activation(junk_o[:, :], bank(6 + t % 2, P), ACT.Square, scale=sm[:, t, 4:5],
                               accum_out=stats[:, bass.ds(n, 1)])
                act.activation(o_nat[:, t, bass.ds(h * P, P)], bank(6 + t % 2, P), ACT.Copy, scale=sm[:, t, 4:5]).then_inc(at_oe, 1)

            set_table(ACT.Exp)
            exp(0, 0, 0)
            exp(0, 0, 1)
            exp(0, 1, 0)
            exp(0, 1, 1)
            exp(0, 2, 0)
            evacuate_T(0, 0)
            exp(0, 2, 1)
            with act.Fori(0, DH - 1) as h:
                for t in range(2, TILES + 2):
                    exp(h, t + 1, 0)
                    evacuate_T(h, t - 1)
                    exp(h, t + 1, 1)
                    evacuate_o(h, t - 2)
            for t in range(2, TILES + 2):
                if t == TILES - 1:
                    set_table(ACT.Sqrt)
                if t + 1 < TILES:
                    exp(DH - 1, t + 1, 0)
                if t - 1 < TILES:
                    evacuate_T(DH - 1, t - 1)
                if t + 1 < TILES:
                    exp(DH - 1, t + 1, 1)
                evacuate_o(DH - 1, t - 2)
            root("normo", DH * TILES)
            act.wait_ge(vd_stored, 16)
            for n in range(8):
                act.wait_ge(gb_ps, n + 1)
                act.activation(gate_row[:, n // 2, (n % 2) * BANK:(n % 2 + 1) * BANK], bank(n), ACT.Copy).then_inc(gb_row, 1)
            act.wait_ge(sub_ready, 1)
            act_to_T(act, "od", od_hi, subln_gain)

            def mix_hi_part(i, par):
                for j in range(2):
                    act.wait_ge(mix_sum, i * 4 + (2 * par + j + 1))
                    tile = i * 4 + (2 * par + j)
                    act.activation(one_tile(mix_hi, tile), one_tile(mixT, tile), ACT.Copy).then_inc(mix_h, 1)

            dense("diff_out", mix_hi_part)
            set_table(ACT.Copy).then_inc(norm["norm2"]["sums"], AHEAD)
            set_table(ACT.Sqrt)
            dense("w_o", block_sums("norm2", 0))
            root("norm2", TILES)
            act_to_T_shifted(act, "h2", h2_hi, SHIFT2)

            def up(third):
                name = f"up{third}"

                def evacuate(i, par):
                    for j in range(2):
                        if par == 0:
                            act.wait_ge(freed["dve"], i * 2 + START[name]["dve"])
                            act.wait_ge(mm_done, ready(name, i, 0, j))
                            act.activation(in_halves(silu_g[:, j, :]), T_tile(2 * j), ACT.Silu).then_inc(freed["act"], 1)
                        else:
                            act.wait_ge(freed["dve"], freed_after(name, i, 1, j))
                            tile = i * 2 + j
                            act.activation(hid_hi[:, bass.ds(tile, 1), :].rearrange("p a b -> p (a b)"),
                                           hid_f[:, j, :], ACT.Copy).then_inc(hid_h, 1)
                return evacuate

            set_table(ACT.Silu)
            for third in range(3):
                dense(f"up{third}", up(third))
                if third == 2:
                    set_table(ACT.Copy).then_inc(norm["normf"]["sums"], AHEAD)
                dense(f"down{third}", block_sums("normf", 24) if third == 2 else lambda i, par: None, peel=int(third == 2))
            root("normf", TILES)

        @block.vector
        def _(dve):
            steps = [0]

            def link(ins):
                steps[0] += 1
                ins.then_inc(dve_step, 1)
                dve.wait_ge(dve_step, steps[0])

            def ada_terms(k, slot, w, done, before):
                for c in range(2):
                    acc, x = ada_acc[:, slot, c, :], silu_c[:, k, c:c + 1]
                    if k == 0:
                        last = dve.tensor_scalar(acc, w, x, None, ALU.mult)
                    else:
                        dve.wait_ge(done, before + (2 * k + c - 1))
                        last = dve.scalar_tensor_tensor(acc, w, x, acc, ALU.mult, ALU.add)
                    last.then_inc(done, 1)

            flat = lambda x: x[:, :, :].rearrange("p a b -> p (a b)")

            def total_of_blocks(which):
                dve.wait_ge(norm[which]["sums"], 4 * TILES + AHEAD)
                link(dve.reduce_sum(stats[:, 20:20 + TILES], stats[:, 0:4 * TILES].rearrange("p (t u) -> p t u", u=4), axis=AX.X))

            def mean(which, n, scale, eps, first=0):
                dve.tensor_scalar(rstd[:, 0:n], stats[:, first:first + n], scale, eps, ALU.mult, ALU.add).then_inc(norm[which]["mean"], 1)

            def inverse(which, n):
                dve.wait_ge(norm[which]["root"], 1)
                link(dve.reciprocal(rstd[:, 0:n], rstd[:, 0:n]))

            dve.memset(ones_col[:, :], 1.0).then_inc(ada_step, 16)
            for n, ahead in enumerate((rope_done, hid_l, x1_done)):
                dve.memset(spare[:, n:n + 1], 0.0).then_inc(ahead, AHEAD)
            dve.wait_ge(ld_scal, 6 * 16)
            link(dve.tensor_scalar(gam_c[:, :, :], lg[:, :, :], -1.0, None, ALU.mult))
            dve.tensor_tensor(gam_c[:, :, :], lg[:, :, :], gam_c[:, :, :], ALU.max).then_inc(setup_v, 1)
            link(dve.tensor_tensor(lam_mul[:, :, :], lam_in[:, 0:2, :], lam_in[:, 2:4, :], ALU.mult))
            link(dve.reduce_sum(lamv[:, 0:2], lam_mul[:, :, :], axis=AX.X))
            dve.wait_ge(norm["norm1"]["sums"], TILES)
            mean("norm1", TILES, 1.0 / D, RMS_EPS)
            inverse("norm1", TILES)
            for t in range(TILES):
                dve.tensor_scalar(x_nat[:, t, :], x_nat[:, t, :], rstd[:, t:t + 1], None, ALU.mult).then_inc(norm["norm1"]["scaled"], 1)
            y, u, t0, t1, log1p = flat(w_k), flat(gam_c), stats[:, 16:24], stats[:, 24:32], stats[:, 8:16]
            dve.wait_ge(setup_a, 1)
            dve.tensor_scalar(u, y, 1.0, None, ALU.add).then_inc(setup_v, 1)
            dve.wait_ge(setup_v, 2)
            link(dve.tensor_scalar(t0, u, -1.0, None, ALU.add))
            link(dve.tensor_tensor(t0, y, t0, ALU.subtract))
            link(dve.reciprocal(t1, u))
            link(dve.tensor_tensor(t0, t0, t1, ALU.mult))
            dve.wait_ge(setup_a, 2)
            link(dve.tensor_tensor(log1p, log1p, t0, ALU.add))
            link(dve.tensor_scalar(flat(lg), flat(lg), 0.0, None, ALU.min))
            dve.tensor_tensor(flat(lg), flat(lg), log1p, ALU.subtract).then_inc(setup_v, 2)
            dve.wait_ge(setup_v, 4)
            dve.wait_ge(ld_tab, 3 * 16)
            for n in range(2):
                last = dve.tensor_scalar(w_k[:, n, :], lg[:, n, :], pos_col[:, n:n + 1], None, ALU.mult)
            last.then_inc(setup_v, 1)
            for h in range(RH):
                last = dve.tensor_scalar(decay[:, h, :], dist[:, 0, :], lg[:, 0, h:h + 1], None, ALU.mult)
            link(last)
            for h in range(RH):
                last = dve.scalar_tensor_tensor(decay[:, h, :], dist[:, 1, :], lg[:, 1, h:h + 1], decay[:, h, :], ALU.mult, ALU.add)
            last.then_inc(setup_v, 1)
            dve.wait_ge(setup_a, 3)
            link(dve.tensor_tensor(lamv[:, 2:3], lamv[:, 1:2], lamv[:, 0:1], ALU.subtract))
            link(dve.tensor_scalar(lamv[:, 2:3], lamv[:, 2:3], -LAM_INIT, None, ALU.add))
            dve.wait_ge(setup_a, 6)
            dve.tensor_scalar(w_k[:, :, :], w_k[:, :, :], P ** -0.5, None, ALU.mult).then_inc(setup_v, 1)
            dve.tensor_scalar(decay[:, :, :], decay[:, :, :], P ** -0.5, None, ALU.mult).then_inc(setup_v, 1)

            dve.wait_ge(freed["act"], 2)
            for n in range(2):
                dve.wait_ge(ada_a_in[6 + n], 16)
                for k in range(KT):
                    ada_terms(k, n, ada_a[6 + n][:, k, :], ada_pre, 16 * n)
            dve_split(dve, 0, 0)
            dve.wait_ge(cols_ready, 1)
            dve.wait_ge(ada_cols, 2)
            for n, m in enumerate((SHIFT1, SCALE1)):
                last = dve.tensor_tensor(mod[:, m:m + KT, :], bank(7, 2 * KT, 2 * m).rearrange("p (m s) -> p m s", s=2),
                                         cols[:, ROW_BADA + m:ROW_BADA + m + KT].unsqueeze(2).to_broadcast([P, KT, 2]), ALU.add)
                last.then_inc(freed["dve"], 1)
            dve.wait_ge(freed["dve"], 2)

            dve.tensor_scalar(sub_gain[:, :], cols[:, ROW_SUBLN:ROW_SUBLN + 1], 1.0 - LAM_INIT, None, ALU.mult).then_inc(sub_ready, 1)

            def scales(which, m, gain):
                dve.wait_ge(dve_step, steps[0])
                (dve.scalar_tensor_tensor(sc[:, :, :], mod[:, m:m + KT, :], 1.0,
                                              cols[:, gain:gain + KT].unsqueeze(2).to_broadcast([P, KT, 2]), ALU.add, ALU.mult)
                 .then_inc(n2t[which]["scale"], 1))

            scales("h", SCALE1, ROW_G1)
            dve_to_T_shifted(dve, "h", h_hi, h_lo, SHIFT1)

            def ada_partial(name, i, par):
                u = ADA_FIRST[name] + par
                for k in range(KT):
                    half = 2 * k // KT
                    if k % (KT // 2) == 0:
                        dve.wait_ge(ada_b_in[half], i * 32 + 16 * (u + 1))
                    ada_terms(k, par, ada_b[half][:, k % (KT // 2), :], ada_step, i * 32 + (16 + 16 * u))

            def dense(name, evacuate, peel=0):
                def pair(i, last):
                    for par in range(2):
                        if not (name == "down2" and last and par == 1):
                            dve_split(dve, unit_of(name, i, par) + 1, 1 - par)
                        if name == "v_d":
                            if not (last and par == 1):
                                ada_partial(name, i + par, 1 - par)
                        elif name in ADA_FIRST:
                            ada_partial(name, i, par)
                        evacuate(i, par)

                with dve.Fori(0, COUNT[name] // 2 - peel) as i:
                    pair(i, False)
                if peel:
                    pair(COUNT[name] // 2 - 1, True)

            def rotate(name, qk, first, tile0, swaps, before):
                def evacuate(i, par):
                    x = qk[:, bass.ds(i * 4 + (tile0 + 2 * par), 2), 0:LAT]
                    dve.wait_ge(freed["act"], freed_after(name, i, par, 1))
                    dve.wait_ge(rope_done, i * 2 + (first + par + AHEAD))
                    dve.tensor_tensor(rope_tmp[:, :, :], x, rope[:, 0:1, :].to_broadcast([P, 2, LAT]), ALU.mult).then_inc(rope_mul, 1)
                    dve.wait_ge(rope_in, i * (32 * swaps) + (before + 16 * swaps * (par + 1)))
                    dve.tensor_tensor(swapped[:, :, :], swapped[:, :, :], rope[:, 1:2, :].to_broadcast([P, 2, LAT]), ALU.mult).then_inc(rope_mul, 1)
                    dve.wait_ge(rope_mul, i * 4 + (2 * (first + par) + 2))
                    dve.tensor_tensor(x, rope_tmp[:, :, :], swapped[:, :, :], ALU.add).then_inc(rope_done, 1)
                return evacuate

            nothing = lambda i, par: None
            dve.wait_ge(ld_rope, 16)
            dense("qk_r", rotate("qk_r", qk_r, 0, 0, 2, 0))
            dense("v_r", nothing)
            dense("g_r", nothing)

            with dve.Fori(0, RH) as h:
                dve.wait_ge(r_s0, h * 32 + 32)
                for s in range(3):
                    dve.wait_ge(r_kv, h * 4 + (s + 1))
                    if s:
                        dve.wait_ge(r_state, h * 3 + s)
                    for n, (c_to, c_from) in enumerate(((s + 1, s), (2 - s, 3 - s))):
                        last = dve.scalar_tensor_tensor(state[:, n, c_to, :], state[:, n, c_from, :] if s else s_ends[:, n, :],
                                                        gam_c[:, n, bass.ds(h, 1)], bank(4 + s % 2, RDV, n * RDV), ALU.mult, ALU.add)
                    last.then_inc(r_state, 1)
                    if s == 1:
                        dve.wait_ge(r_s, h + 1)
                        dve.tensor_tensor(s_dec[:, :, :], psum[:, 2 * BANK:2 * BANK + TOK].rearrange("p (c i) -> p c i", i=P),
                                          decay[:, bass.ds(h, 1), :].to_broadcast([P, TILES, P]), ALU.mult).then_inc(r_dec, 1)
                for p_, c in enumerate(OUT_ORDER):
                    dve.wait_ge(r_y, h * TILES + (p_ + 1 + AHEAD))
                    dve.bn_stats(bn6[:, bass.ds(h * TILES + c, 1), :].rearrange("p a b -> p (a b)"),
                                 y_nat[:, c, bass.ds(h * RDV, RDV)]).then_inc(r_bn, 1)
            dve.wait_ge(r_bn, RH * TILES)
            for n in range(RH * TILES):
                last = dve.bn_aggr(mean_var[:, n, :], bn6[:, n, :])
            last.then_inc(r_mv, 1)
            n = RH * TILES
            dve.wait_ge(r_mv, 1)
            dve.tensor_scalar(rstd[:, 0:n], mean_var[:, :, 1], GN_EPS, None, ALU.add).then_inc(norm["normy"]["mean"], 1)
            inverse("normy", n)
            dve.scalar_tensor_tensor(rstd[:, n:2 * n], mean_var[:, :, 0], -1.0, rstd[:, 0:n], ALU.mult, ALU.mult).then_inc(norm["normy"]["scaled"], 1)

            def gate_head(i, par):
                hs = bass.ds((i * 2 + par) * RDV, RDV)
                dve.wait_ge(y_norm, (i * 2 + par) * TILES + TILES)
                dve.tensor_tensor(y_nat[:, :, hs], y_nat[:, :, hs], g_r[:, :, hs], ALU.mult).then_inc(y_gated, 1)

            dve.wait_ge(r_ctx_out, RH * 32)
            dense("gate_r", gate_head)
            dve_to_T(dve, "yg", yg_hi, yg_lo, gn_gain)
            dense("gate_d", nothing)

            def gated_ret(i, par):
                for j in range(2):
                    dve.wait_ge(mm_done, ready("ret_out", i, par, j))
                    if j == 1:
                        dve.tensor_copy(mod[:, bass.ds(i * 4 + (GATE1 + 2 * (ADA_FIRST["ret_out"] + par)), 2), :],
                                        bank(4 * par + 3, 4, HALF).rearrange("p (m s) -> p m s", s=2))
                    x = one_tile(mixT, i * 4 + (2 * par + j))
                    dve.tensor_tensor(x, T_tile(4 * par + 2 * j), x, ALU.mult).then_inc(freed["dve"], 1)

            dense("ret_out", gated_ret)
            ada_partial("v_d", 0, 0)
            dve.wait_ge(ld_rope, 32)
            dense("q_d", rotate("q_d", qk_d, 4, 0, 4, 128))
            dense("k_d", rotate("k_d", qk_d, 8, DH, 4, 128 + 256))
            dense("v_d", nothing, peel=1)
            dve.wait_ge(freed["act"], START["diff_out"]["act"])
            dve.wait_ge(freed["dve"], START["diff_out"]["dve"])
            link(dve.tensor_tensor(mod[:, GATE1:, :], mod[:, GATE1:, :],
                                   cols[:, ROW_BADA + GATE1:ROW_BADA + 48].unsqueeze(2).to_broadcast([P, 32, 2]), ALU.add))
            scales("h2", SCALE2, ROW_G2)

            def maximum(h0, t0, m):
                h, t, n = tile_of(h0, t0)
                size = TOK if t < LAT_TILES else P
                dve.wait_ge(at_s, n * 2 + (m + 1))
                dve.reduce_max(sm[:, t, m:m + 1], psum[:, 2 * m * BANK:2 * m * BANK + size], axis=AX.X,
                               negate=True).then_inc(at_max, 1)

            def weights(h0, t0, part):
                h, t, n = tile_of(h0, t0)
                size = TOK if t < LAT_TILES else P
                p0, p1 = probs[:, PBUF[t], 0, 0:size], probs[:, PBUF[t], 1, 0:size]
                if part == 0:
                    dve.wait_ge(at_e, n * 2 + 2)
                    dve.reciprocal(sm[:, t, 4:6], sm[:, t, 2:4]).then_inc(at_r, 1)
                    dve.wait_ge(at_r, n + 1)
                    dve.tensor_scalar(sm[:, t, 6:7], sm[:, t, 5:6], sm[:, t, 2:3], lamv[:, 2:3], ALU.mult, ALU.mult).then_inc(at_f, 1)
                else:
                    dve.wait_ge(at_f, n + 1)
                    dve.scalar_tensor_tensor(p0, p1, sm[:, t, 6:7], p0, ALU.mult, ALU.add).then_inc(at_a, 1)

            maximum(0, 0, 0)
            maximum(0, 0, 1)
            maximum(0, 1, 0)
            weights(0, 0, 0)
            maximum(0, 1, 1)
            weights(0, 0, 1)
            maximum(0, 2, 0)
            weights(0, 1, 0)
            maximum(0, 2, 1)
            weights(0, 1, 1)
            with dve.Fori(0, DH - 1) as h:
                for t in range(2, TILES + 2):
                    maximum(h, t + 1, 0)
                    weights(h, t, 0)
                    maximum(h, t + 1, 1)
                    weights(h, t, 1)
            for t in range(2, TILES):
                if t + 1 < TILES:
                    maximum(DH - 1, t + 1, 0)
                weights(DH - 1, t, 0)
                if t + 1 < TILES:
                    maximum(DH - 1, t + 1, 1)
                weights(DH - 1, t, 1)

            dve.wait_ge(at_oe, 2 + DH * TILES)
            mean("normo", DH * TILES, 1.0 / P, RMS_EPS)
            inverse("normo", DH * TILES)
            r = rstd[:, :].rearrange("p (h t) -> p h t", t=TILES)
            for t in range(TILES):
                x = o_nat[:, t, :].rearrange("p (h e) -> p h e", e=P)
                dve.tensor_tensor(x, x, r[:, :, t:t + 1].to_broadcast([P, DH, P]), ALU.mult).then_inc(norm["normo"]["scaled"], 1)
            dve_to_T(dve, "od", od_hi, od_lo, subln_gain)

            def mixed(i, par):
                for j in range(2):
                    tile = i * 4 + (2 * par + j)
                    g, x = one_tile(gate_d, tile), one_tile(mixT, tile)
                    dve.wait_ge(mm_done, ready("diff_out", i, par, j))
                    dve.tensor_tensor(g, T_tile(4 * par + 2 * j), g, ALU.mult).then_inc(freed["dve"], 1)
                    dve.wait_ge(freed["dve"], freed_after("diff_out", i, par, j))
                    dve.tensor_tensor(x, x, g, ALU.add).then_inc(mix_sum, 1)
                for j in range(2):
                    tile = i * 4 + (2 * par + j)
                    dve.wait_ge(mix_h, i * 4 + (2 * par + j + 1))
                    dve.tensor_tensor(one_tile(mix_lo, tile), one_tile(mixT, tile), one_tile(mix_hi, tile).bitcast(F32),
                                      ALU.subtract).then_inc(mix_l, 1)

            dense("diff_out", mixed)

            def residual(name, g, done0):
                def evacuate(i, par):
                    cs = bass.ds(i * (2 * UC) + par * UC, UC)
                    for j in range(2):
                        dve.wait_ge(mm_done, ready(name, i, par, j))
                        nt = LAT_TILES if j == 0 else 1
                        src = bank(4 * par + 2 * j, nt * UC).rearrange("p (t c) -> p t c", c=UC) if j else \
                            psum[:, 4 * par * BANK:(4 * par + 2) * BANK].rearrange("p (t c) -> p t c", c=UC)
                        row = gate_row[:, 2 * g + j:2 * g + j + 1, cs].to_broadcast([P, nt, UC])
                        x = x1[:, 0:LAT_TILES, cs] if j == 0 else x1[:, LAT_TILES:TILES, cs]
                        dve.wait_ge(x1_done, i * 4 + (done0 + 2 * par + j + AHEAD))
                        dve.tensor_tensor(gated[:, 0:nt, :], src, row, ALU.mult).then_inc(freed["dve"], 1)
                        dve.wait_ge(freed["dve"], freed_after(name, i, par, j))
                        dve.tensor_tensor(x, x, gated[:, 0:nt, :], ALU.add).then_inc(x1_done, 1)
                return evacuate

            dve.wait_ge(ld_x1, 32)
            dense("w_o", residual("w_o", 0, 0))
            total_of_blocks("norm2")
            mean("norm2", TILES, 1.0 / D, RMS_EPS, first=20)
            inverse("norm2", TILES)
            for t in range(TILES):
                dve.tensor_scalar(diag_r[:, t, :], ident[:, :], rstd[:, t:t + 1], None, ALU.mult).then_inc(norm["norm2"]["scaled"], 1)
            dve_to_T_shifted(dve, "h2", h2_hi, h2_lo, SHIFT2)

            def hidden(third):
                name = f"up{third}"
                base = sum(COUNT[f"up{n}"] for n in range(third))

                def evacuate(i, par):
                    if par == 0:
                        return
                    for j in range(2):
                        dve.wait_ge(mm_done, ready(name, i, 1, j))
                        dve.wait_ge(freed["act"], freed_after(name, i, 0, j))
                        dve.wait_ge(hid_l, i * 2 + (base + AHEAD))
                        dve.tensor_tensor(in_halves(hid_f[:, j, :]), T_tile(4 + 2 * j), in_halves(silu_g[:, j, :]),
                                          ALU.mult).then_inc(freed["dve"], 1)
                    for j in range(2):
                        tile = i * 2 + j
                        dve.wait_ge(hid_h, i * 2 + (base + j + 1))
                        dve.tensor_tensor(hid_lo[:, bass.ds(tile, 1), :].rearrange("p a b -> p (a b)"), hid_f[:, j, :],
                                          hid_hi[:, bass.ds(tile, 1), :].rearrange("p a b -> p (a b)").bitcast(F32),
                                          ALU.subtract).then_inc(hid_l, 1)
                return evacuate

            for third in range(3):
                dense(f"up{third}", hidden(third))
                dense(f"down{third}", residual(f"down{third}", 1, 8 * (third + 1)), peel=int(third == 2))
            total_of_blocks("normf")
            mean("normf", TILES, 1.0 / D, RMS_EPS, first=20)
            inverse("normf", TILES)
            dve.wait_ge(ld_fin, 16)
            for t in range(TILES):
                dve.scalar_tensor_tensor(x1[:, t, :], x1[:, t, :], rstd[:, t:t + 1], fin_g[:, :], ALU.mult, ALU.mult).then_inc(y_done, 1)


def shape_constants():
    f = np.float32
    pos_r, pos_c = np.repeat(np.arange(LAT // GRID_W), GRID_W), np.tile(np.arange(GRID_W), LAT // GRID_W)

    def rotary(d):
        n = d // 4
        inv = (10000.0 ** (-np.arange(n) / n)).astype(f)
        ang = np.concatenate([pos_r[:, None].astype(f) * inv, pos_c[:, None].astype(f) * inv], axis=-1)
        cos, sin = np.cos(ang.astype(np.float64)).T, np.sin(ang.astype(np.float64)).T
        cos, sin = np.concatenate([cos, cos]), np.concatenate([-sin, sin])
        return np.stack([np.tile(cos, (P // d, 1)), np.tile(sin, (P // d, 1))]).astype(f)

    i = np.arange(P)
    gap = (i[None, :] - i[:, None]).astype(f)
    return {"const_ident": np.eye(P, dtype=f), "const_rope_ret": rotary(P), "const_rope_diff": rotary(DHD),
            "const_dist": np.stack([np.maximum(gap, 0), np.maximum(-gap, 0)]).astype(f),
            "const_row_pos": np.stack([i + 1, P - i]).astype(f),
            "const_pos_col": np.stack([P - 1 - i, i], axis=1).astype(f)}


OUTPUTS = (("y_prompt", (1, P, D)), ("y_sample", (1, LAT, D)), ("new_ret_fwd", (1, 1, RH, P, RDV)),
           ("new_ret_bwd", (1, 1, RH, P, RDV)), ("new_diff_k", (1, 1, P, DH, 2, DHD)),
           ("new_diff_v", (1, 1, P, DH, 2 * DHD)))


def kernel(**inputs):
    import concourse.bacc as bacc
    from concourse.bass_utils import run_bass_kernel_spmd

    nc = bacc.Bacc("TRN2", target_bir_lowering=False, num_devices=1)
    arrays, a, o = {}, {}, {}
    for name, x in {**inputs, **shape_constants()}.items():
        x = np.ascontiguousarray(x)
        arrays["in_" + name] = x
        a[name] = nc.dram_tensor("in_" + name, x.shape, F32, kind="ExternalInput").ap()
    for name, shape in OUTPUTS:
        o[name] = nc.dram_tensor("out_" + name, shape, F32, kind="ExternalOutput").ap()
    build(nc, a, o)
    r = run_bass_kernel_spmd(nc, [arrays], core_ids=[0])
    return tuple(r.results[0]["out_" + name] for name, _ in OUTPUTS)
```
